# Optimizing a Trainium2 kernel written in Bass

```python
import jax, jax.numpy as jnp
from jax import lax
import numpy as np

D_MODEL = 1024
BATCH = 1
SEQ = 1024
DEPTH = 2

CHUNK = 64
N_EVEN = (DEPTH + 1) // 2
N_ODD = DEPTH // 2
RMS_EPS = 1e-6

RWKV_WIDTH = D_MODEL // 2
RWKV_HEAD_DIM = 64
RWKV_HEADS = RWKV_WIDTH // RWKV_HEAD_DIM
RWKV_DECAY_RANK = 64
RWKV_A_RANK = 64
RWKV_GATE_RANK = 128
RWKV_COLS = 3 * RWKV_WIDTH + RWKV_DECAY_RANK + RWKV_A_RANK + RWKV_GATE_RANK
RWKV_GN_EPS = 64e-5

LRU_WIDTH = D_MODEL // 2
LRU_BLOCKS = 8
LRU_BLOCK_DIM = LRU_WIDTH // LRU_BLOCKS
CONV_WIDTH = 4
LRU_C = 8.0
LRU_COLS = 2 * LRU_WIDTH
AB_COLS = RWKV_COLS + LRU_COLS
AB_MIX_WIDTH = RWKV_WIDTH + LRU_WIDTH

HGRN_WIDTH = D_MODEL
HGRN_EXPAND = 128
HGRN_HEADS = HGRN_WIDTH // HGRN_EXPAND
HGRN_COLS = 4 * HGRN_WIDTH

N_GROUPS = 4
EXPERTS_PER_GROUP = 8
N_EXPERTS = N_GROUPS * EXPERTS_PER_GROUP
TOP_K = 2
EXPERT_FF = 512
ROUTE_BLOCK = 128

kernel_name = "hybrid_rwkv7_rglru_hgrn2_hmoe"

def rmsnorm(x, g):
    xf = x.astype(jnp.float32)
    y = xf * lax.rsqrt(jnp.mean(xf * xf, -1, keepdims=True) + RMS_EPS)
    return (y * g.astype(jnp.float32)).astype(x.dtype)

def token_shift(p, mu):
    prev = jnp.pad(p, ((0, 0), (1, 0), (0, 0)))[:, :-1]
    return p + (prev - p) * mu

def split_heads(t, heads):
    b, s, w = t.shape
    return t.reshape(b, s, heads, w // heads).astype(jnp.float32)

def rwkv7_recurrence(r, w, k, v, kk, a):
    b, _, h, n = r.shape

    def step(S, inp):
        r_t, w_t, k_t, v_t, kk_t, a_t = inp
        sa = jnp.einsum('bhvk,bhk->bhv', S, -kk_t)
        S = (S * w_t[:, :, None, :] + sa[..., None] * (kk_t * a_t)[:, :, None, :]
             + v_t[..., None] * k_t[:, :, None, :])
        return S, jnp.einsum('bhvk,bhk->bhv', S, r_t)

    xs = tuple(jnp.moveaxis(t, 1, 0) for t in (r, w, k, v, kk, a))
    _, y = lax.scan(step, jnp.zeros((b, h, n, n), jnp.float32), xs)
    return jnp.moveaxis(y, 0, 1)

def rwkv7_mixer(p, mu, w0, w2, a0, a2, g2, k_k, k_a, r_k, ln_w, ln_b):
    b, s, _ = p.shape
    p = token_shift(p, mu)
    idx = [RWKV_WIDTH, 2 * RWKV_WIDTH, 3 * RWKV_WIDTH,
           3 * RWKV_WIDTH + RWKV_DECAY_RANK, 3 * RWKV_WIDTH + RWKV_DECAY_RANK + RWKV_A_RANK]
    r, k, v, wl, al, gl = jnp.split(p, idx, axis=-1)
    w = -jax.nn.softplus(-(w0 + jnp.tanh(wl) @ w2)) - 0.5
    decay = jnp.exp(-jnp.exp(w.astype(jnp.float32)))
    a = jax.nn.sigmoid(a0 + al @ a2)
    g = jax.nn.sigmoid(gl) @ g2
    kk = split_heads(k * k_k, RWKV_HEADS)
    kk = kk / jnp.maximum(jnp.linalg.norm(kk, axis=-1, keepdims=True), 1e-12)
    k = k * (1.0 + (a - 1.0) * k_a)
    rh, kh, vh = (split_heads(t, RWKV_HEADS) for t in (r, k, v))
    y = rwkv7_recurrence(rh, split_heads(decay, RWKV_HEADS), kh, vh, kk,
                         split_heads(a, RWKV_HEADS))
    mean = jnp.mean(y, -1, keepdims=True)
    var = jnp.mean(jnp.square(y - mean), -1, keepdims=True)
    y = ((y - mean) * lax.rsqrt(var + RWKV_GN_EPS)).reshape(b, s, RWKV_WIDTH)
    y = y * ln_w + ln_b
    bonus = jnp.sum(rh * kh * r_k.astype(jnp.float32), -1, keepdims=True) * vh
    return ((y + bonus.reshape(b, s, RWKV_WIDTH)) * g).astype(p.dtype)

def rglru_mixer(p, conv_w, conv_b, w_a, b_a, w_x, b_x, lam):
    b, s, _ = p.shape
    gate, xb = jnp.split(p, [LRU_WIDTH], axis=-1)
    xc = lax.conv_general_dilated(xb, conv_w[:, None, :], window_strides=(1,),
                                  padding=[(CONV_WIDTH - 1, 0)],
                                  dimension_numbers=('NWC', 'WIO', 'NWC'),
                                  feature_group_count=LRU_WIDTH) + conv_b
    xg = xc.reshape(b, s, LRU_BLOCKS, LRU_BLOCK_DIM)
    r = jax.nn.sigmoid(jnp.einsum('btnd,nde->btne', xg, w_a).reshape(b, s, LRU_WIDTH) + b_a)
    i = jax.nn.sigmoid(jnp.einsum('btnd,nde->btne', xg, w_x).reshape(b, s, LRU_WIDTH) + b_x)
    log_a = -LRU_C * r.astype(jnp.float32) * jax.nn.softplus(-lam.astype(jnp.float32))
    a = jnp.exp(log_a)
    u = jnp.sqrt(-jnp.expm1(2.0 * log_a)) * i.astype(jnp.float32) * xc.astype(jnp.float32)

    def combine(c1, c2):
        return c1[0] * c2[0], c2[0] * c1[1] + c2[1]

    _, h = lax.associative_scan(combine, (a, u), axis=1)
    return (h * jax.nn.gelu(gate.astype(jnp.float32))).astype(p.dtype)

def gla_chunkwise(q, k, v, log_f):
    b, s, h, dk = q.shape
    dv = v.shape[-1]
    n_chunks = s // CHUNK

    def to_chunks(t):
        return t.reshape(b, n_chunks, CHUNK, h, t.shape[-1]).transpose(1, 0, 3, 2, 4)

    mask = jnp.tril(jnp.ones((CHUNK, CHUNK), dtype=bool))[:, :, None]

    def step(S, inp):
        q_c, k_c, v_c, lf_c = inp
        bc = jnp.cumsum(lf_c, axis=2)
        diff = bc[:, :, :, None, :] - bc[:, :, None, :, :]
        dec = jnp.exp(jnp.where(mask, diff, -jnp.inf))
        scores = jnp.einsum('bhtd,bhsd,bhtsd->bhts', q_c, k_c, dec)
        o = (jnp.einsum('bhts,bhsv->bhtv', scores, v_c)
             + jnp.einsum('bhtd,bhdv->bhtv', q_c * jnp.exp(bc), S))
        bl = bc[:, :, -1:, :]
        S = (jnp.exp(bl[:, :, 0, :])[..., None] * S
             + jnp.einsum('bhsd,bhsv->bhdv', k_c * jnp.exp(bl - bc), v_c))
        return S, o

    xs = tuple(to_chunks(t) for t in (q, k, v, log_f))
    _, o = lax.scan(step, jnp.zeros((b, h, dk, dv), jnp.float32), xs)
    return o.transpose(1, 0, 3, 2, 4).reshape(b, s, h, dv)

def hgrn2_mixer(hn, w_in, lower_bound, norm_w, w_out):
    b, s, _ = hn.shape
    q, f, i, g = jnp.split(hn @ w_in, 4, axis=-1)
    q = jax.nn.silu(q.astype(jnp.float32))
    fg = lower_bound + (1.0 - lower_bound) * jax.nn.sigmoid(f.astype(jnp.float32))
    k = 1.0 - fg
    log_f = jnp.log(fg)
    o = gla_chunkwise(split_heads(q, HGRN_HEADS), split_heads(k, HGRN_HEADS),
                      split_heads(i, HGRN_HEADS), split_heads(log_f, HGRN_HEADS))
    o = o * lax.rsqrt(jnp.mean(o * o, -1, keepdims=True) + RMS_EPS)
    o = o.reshape(b, s, HGRN_WIDTH) * norm_w * jax.nn.silu(g.astype(jnp.float32))
    return o.astype(hn.dtype) @ w_out

def hier_moe(hn, w_group, b_group, w_expert, b_expert, w_gate, w_up, w_down):
    b, s, d = hn.shape
    n_tok = b * s
    xf = hn.reshape(n_tok, d)
    g_logits = (xf @ w_group + b_group).astype(jnp.float32)
    g_sel = jnp.argmax(g_logits, -1)
    g_gate = jnp.take_along_axis(jax.nn.softmax(g_logits, -1), g_sel[:, None], 1)
    e_logits = (xf @ w_expert + b_expert).astype(jnp.float32).reshape(n_tok, N_GROUPS, EXPERTS_PER_GROUP)
    e_logits = jnp.take_along_axis(e_logits, g_sel[:, None, None], 1)[:, 0]
    top_v, top_i = lax.top_k(jax.nn.softmax(e_logits, -1), TOP_K)
    gates = (g_gate * top_v / jnp.sum(top_v, -1, keepdims=True)).reshape(-1)
    e_flat = (g_sel[:, None] * EXPERTS_PER_GROUP + top_i).reshape(-1).astype(jnp.int32)
    n_assign = n_tok * TOP_K
    tok = jnp.arange(n_assign, dtype=jnp.int32) // TOP_K
    order = jnp.argsort(e_flat)
    e_sorted = e_flat[order]
    counts = jnp.zeros((N_EXPERTS,), jnp.int32).at[e_flat].add(1)
    padded = (counts + ROUTE_BLOCK - 1) // ROUTE_BLOCK * ROUTE_BLOCK
    start = jnp.cumsum(counts) - counts
    pend = jnp.cumsum(padded)
    pstart = pend - padded
    dest = pstart[e_sorted] + jnp.arange(n_assign, dtype=jnp.int32) - start[e_sorted]
    n_blocks = (n_assign + ROUTE_BLOCK - 1) // ROUTE_BLOCK + N_EXPERTS
    n_rows = n_blocks * ROUTE_BLOCK
    row_tok = jnp.full((n_rows,), n_tok, jnp.int32).at[dest].set(tok[order])
    row_gate = jnp.zeros((n_rows,), hn.dtype).at[dest].set(gates[order].astype(hn.dtype))
    block_e = jnp.clip(jnp.searchsorted(pend, jnp.arange(n_blocks, dtype=jnp.int32) * ROUTE_BLOCK,
                                        side='right'), 0, N_EXPERTS - 1)
    x_pad = jnp.concatenate([xf, jnp.zeros((1, d), xf.dtype)], 0)
    xs = x_pad[row_tok].reshape(n_blocks, ROUTE_BLOCK, d)

    def expert_block(args):
        xb, e = args
        hid = jax.nn.silu(xb @ w_gate[e]) * (xb @ w_up[e])
        return hid @ w_down[e]

    ys = lax.map(expert_block, (xs, block_e)).reshape(n_rows, d)
    out = jax.ops.segment_sum(ys * row_gate[:, None], row_tok, num_segments=n_tok + 1)[:n_tok]
    return out.reshape(b, s, d)

def setup_inputs(seed: int = 0) -> dict:
    key = jax.random.key(seed)
    keys = iter(jax.random.split(key, 48))

    def nrm(shape, scale):
        return jax.random.normal(next(keys), shape, jnp.float32) * scale

    def gain(shape, base=1.0):
        return base + nrm(shape, 0.01)

    lam_u = jax.random.uniform(next(keys), (N_EVEN, LRU_WIDTH), jnp.float32, 0.9, 0.999)
    lam_a = lam_u ** (1.0 / LRU_C)
    return {
        "x": nrm((BATCH, SEQ, D_MODEL), 1.0),
        "norm_mix": gain((DEPTH, D_MODEL)),
        "norm_ffn": gain((DEPTH, D_MODEL)),
        "norm_final": gain((D_MODEL,)),
        "ab_w_in": nrm((N_EVEN, D_MODEL, AB_COLS), D_MODEL ** -0.5),
        "rw_mu": jax.random.uniform(next(keys), (N_EVEN, RWKV_COLS), jnp.float32),
        "rw_w0": jax.random.uniform(next(keys), (N_EVEN, RWKV_WIDTH), jnp.float32, -6.0, -0.5),
        "rw_w2": nrm((N_EVEN, RWKV_DECAY_RANK, RWKV_WIDTH), 0.5 * RWKV_DECAY_RANK ** -0.5),
        "rw_a0": nrm((N_EVEN, RWKV_WIDTH), 0.1),
        "rw_a2": nrm((N_EVEN, RWKV_A_RANK, RWKV_WIDTH), RWKV_A_RANK ** -0.5),
        "rw_g2": nrm((N_EVEN, RWKV_GATE_RANK, RWKV_WIDTH), RWKV_GATE_RANK ** -0.5),
        "rw_k_k": gain((N_EVEN, RWKV_WIDTH), 0.85),
        "rw_k_a": gain((N_EVEN, RWKV_WIDTH)),
        "rw_r_k": nrm((N_EVEN, RWKV_HEADS, RWKV_HEAD_DIM), 0.1),
        "rw_ln_w": gain((N_EVEN, RWKV_WIDTH)),
        "rw_ln_b": nrm((N_EVEN, RWKV_WIDTH), 0.01),
        "lru_conv_w": nrm((N_EVEN, CONV_WIDTH, LRU_WIDTH), CONV_WIDTH ** -0.5),
        "lru_conv_b": nrm((N_EVEN, LRU_WIDTH), 0.01),
        "lru_w_a": nrm((N_EVEN, LRU_BLOCKS, LRU_BLOCK_DIM, LRU_BLOCK_DIM), LRU_BLOCK_DIM ** -0.5),
        "lru_b_a": nrm((N_EVEN, LRU_WIDTH), 0.01),
        "lru_w_x": nrm((N_EVEN, LRU_BLOCKS, LRU_BLOCK_DIM, LRU_BLOCK_DIM), LRU_BLOCK_DIM ** -0.5),
        "lru_b_x": nrm((N_EVEN, LRU_WIDTH), 0.01),
        "lru_lambda": jnp.log(lam_a) - jnp.log1p(-lam_a),
        "ab_w_out": nrm((N_EVEN, AB_MIX_WIDTH, D_MODEL), AB_MIX_WIDTH ** -0.5),
        "c_w_in": nrm((N_ODD, D_MODEL, HGRN_COLS), D_MODEL ** -0.5),
        "c_lower_bound": nrm((DEPTH, HGRN_WIDTH), 0.1),
        "c_norm_w": gain((N_ODD, HGRN_WIDTH)),
        "c_w_out": nrm((N_ODD, HGRN_WIDTH, D_MODEL), HGRN_WIDTH ** -0.5),
        "moe_w_group": nrm((DEPTH, D_MODEL, N_GROUPS), D_MODEL ** -0.5),
        "moe_b_group": nrm((DEPTH, N_GROUPS), 0.01),
        "moe_w_expert": nrm((DEPTH, D_MODEL, N_EXPERTS), D_MODEL ** -0.5),
        "moe_b_expert": nrm((DEPTH, N_EXPERTS), 0.01),
        "moe_w_gate": nrm((DEPTH, N_EXPERTS, D_MODEL, EXPERT_FF), D_MODEL ** -0.5),
        "moe_w_up": nrm((DEPTH, N_EXPERTS, D_MODEL, EXPERT_FF), D_MODEL ** -0.5),
        "moe_w_down": nrm((DEPTH, N_EXPERTS, EXPERT_FF, D_MODEL), EXPERT_FF ** -0.5),
    }

def reference(x, norm_mix, norm_ffn, norm_final,
              ab_w_in, rw_mu, rw_w0, rw_w2, rw_a0, rw_a2, rw_g2, rw_k_k, rw_k_a, rw_r_k,
              rw_ln_w, rw_ln_b,
              lru_conv_w, lru_conv_b, lru_w_a, lru_b_a, lru_w_x, lru_b_x, lru_lambda, ab_w_out,
              c_w_in, c_lower_bound, c_norm_w, c_w_out,
              moe_w_group, moe_b_group, moe_w_expert, moe_b_expert, moe_w_gate, moe_w_up,
              moe_w_down):
    lbs = jnp.cumsum(jax.nn.softmax(c_lower_bound.astype(jnp.float32), axis=0), axis=0)
    lbs = lbs - lbs[0]
    for layer in range(DEPTH):
        j = layer // 2
        hn = rmsnorm(x, norm_mix[layer])
        if layer % 2 == 0:
            p = hn @ ab_w_in[j]
            ya = rwkv7_mixer(p[..., :RWKV_COLS], rw_mu[j], rw_w0[j], rw_w2[j], rw_a0[j],
                             rw_a2[j], rw_g2[j], rw_k_k[j], rw_k_a[j], rw_r_k[j],
                             rw_ln_w[j], rw_ln_b[j])
            yb = rglru_mixer(p[..., RWKV_COLS:], lru_conv_w[j], lru_conv_b[j], lru_w_a[j],
                             lru_b_a[j], lru_w_x[j], lru_b_x[j], lru_lambda[j])
            x = x + jnp.concatenate([ya, yb], axis=-1) @ ab_w_out[j]
        else:
            x = x + hgrn2_mixer(hn, c_w_in[j], lbs[layer], c_norm_w[j], c_w_out[j])
        hn = rmsnorm(x, norm_ffn[layer])
        x = x + hier_moe(hn, moe_w_group[layer], moe_b_group[layer], moe_w_expert[layer],
                         moe_b_expert[layer], moe_w_gate[layer], moe_w_up[layer],
                         moe_w_down[layer])
    return rmsnorm(x, norm_final)


_drawn_inputs = setup_inputs


def setup_inputs(seed=0):
    import zlib

    import numpy as np

    out = dict(_drawn_inputs(seed))
    spreads = {}
    factors = {'norm_final': 189.185,
     'rw_k_k': 29.867,
     'rw_ln_b': 8.538,
     'lru_b_a': 21.893,
     'lru_b_x': 14.764,
     'c_lower_bound': 3.902,
     'c_norm_w': 131.851,
     'rw_k_a': 3.501,
     'rw_ln_w': 9.886,
     'moe_b_group': 7.854,
     'moe_b_expert': 9.293,
     'norm_ffn': 3.007}
    for name, (base, spread) in spreads.items():
        noise = np.random.default_rng([zlib.crc32(name.encode()), seed]).standard_normal(out[name].shape)
        drawn = base * np.exp(spread * noise) if base else spread * noise
        out[name] = __import__('jax').numpy.asarray(drawn.astype(out[name].dtype))
    for name, factor in factors.items():
        out[name] = (out[name] * factor).astype(out[name].dtype)
    return out
```

```python
from contextlib import ExitStack, contextmanager

import concourse.bass as bass
from concourse import mybir

F32 = mybir.dt.float32
I32 = mybir.dt.int32
U32 = mybir.dt.uint32
ALU = mybir.AluOpType
ACT = mybir.ActivationFunctionType
AX = mybir.AxisListType

P = 128
D = 1024
S = 1024
KT = D // P
TT = S // P
HALF = 512
NH = S // HALF
EPS = 1e-6

W_RW = D // 2
NPAIR = W_RW // P
HD = 64
GN_EPS = 64e-5
AB_COLS = 3 * W_RW + 64 + 64 + 128 + D
AB_TILES = AB_COLS // P
T_R, T_K, T_V, T_WA, T_G, T_GATE, T_XB = 0, 4, 8, 12, 13, 14, 18
NCH = S // HD
LEVELS = (1, 2, 4, 8, 16, 32)

HEADS = 8
HLEVELS = (64, 32, 16, 8, 4, 2, 1)

NG, EPG, NE, FF = 4, 8, 32, 512
NBLK = 2 * S // P + NE
BIG = 1.0e30


def take(eng, sem, n=1):
    eng.wait_ge(sem, n)
    eng.sem_inc(sem, -n)


class Chain:

    def __init__(self, eng, sem):
        self.eng, self.sem, self.n = eng, sem, 0

    def __call__(self, ins):
        self.n += 1
        ins.then_inc(self.sem, 1)
        self.eng.wait_ge(self.sem, self.n)


@contextmanager
def phase(nc, c):
    with ExitStack() as ctx:
        sems, tag = [], nc.next_id()

        def sem(name, by_pool_dma=False):
            if by_pool_dma:
                return c.ctx.enter_context(nc.semaphore(f"{name}_{tag}"))
            s = ctx.enter_context(nc.semaphore(name))
            sems.append(s)
            return s

        def sb(name, shape, dt=F32):
            return ctx.enter_context(nc.sbuf_tensor(f"{name}_{tag}", shape, dt))

        yield sem, sb
        with nc.Block() as block:

            @block.gpsimd
            def _(pool):
                for s in sems:
                    pool.sem_clear(s)


def bcast(ap, axis, n):
    ap = ap.unsqueeze(axis)
    shape = list(ap.shape)
    shape[axis] = n
    return ap.to_broadcast(shape)


def column(vec, lo=0, n=None):
    n = vec.shape[0] if n is None else n
    return vec[lo:lo + n].rearrange("(j p) -> p j", p=P)


def load_x(nc, c, x):
    with phase(nc, c) as (sem, sb):
        x_in, made = sem("x_in"), sem("made")
        with nc.Block() as block:

            @block.sync
            def _(sp):
                for t in range(TT):
                    sp.dma_start(c.res[:, t, :], x[t * P:(t + 1) * P, :]).then_inc(x_in, 16)
                sp.wait_ge(x_in, 16 * TT)

            @block.gpsimd
            def _(pool):
                ch = Chain(pool, made)
                ch(pool.memset(c.ident[:], 1.0))
                ch(pool.affine_select(out=c.ident[:], in_=c.ident[:], pattern=[[-1, P]], compare_op=ALU.is_equal,
                                      fill=0.0, base=0, channel_multiplier=1))
                ch(pool.memset(c.ones[:], 1.0))
                ch(pool.memset(c.head_ones[:], 0.0))
                for p in (0, HD):
                    ch(pool.memset(c.head_ones[p:p + HD, p:p + HD], 1.0))


def norm(nc, c, gain, h_T=None, rows=None):
    with phase(nc, c) as (sem, sb):
        gain_in, squared, var_ready, std_ready, hn_ready = (
            sem(n) for n in ("gain_in", "squared", "var_ready", "std_ready", "hn_ready"))
        turned, copied, stored, order = sem("turned"), sem("copied"), sem("stored"), sem("order")
        hn = sb("hn", [P, TT, D])
        gb = sb("gain_rows", [P, D])
        ss = sb("square_sums", [P, TT])
        var = sb("var", [P, TT])
        std = sb("std", [P, TT])
        rstd = sb("rstd", [P, TT])
        ps = c.ps
        with nc.Block() as block:

            @block.sync
            def _(sp):
                sp.dma_start(gb[:], gain.partition_broadcast(P)).then_inc(gain_in, 16)
                if rows is not None:
                    for t in range(TT):
                        sp.wait_ge(hn_ready, t + 1)
                        sp.dma_start(rows[t * P:(t + 1) * P, :], hn[:, t, :]).then_inc(stored, 16)
                    sp.wait_ge(stored, 16 * TT)

            @block.scalar
            def _(act):
                for t in range(TT):
                    act.activation(hn[:, t, :], c.res[:, t, :], ACT.Square, accum_out=ss[:, t:t + 1]).then_inc(squared, 1)
                act.wait_ge(var_ready, 1)
                act.activation(std[:], var[:], ACT.Sqrt).then_inc(std_ready, 1)
                if h_T is not None:
                    for t in range(TT):
                        for h in range(2):
                            act.wait_ge(turned, 2 * t + h + 1)
                            act.copy(h_T[:, 4 * h:4 * h + 4, t * P:(t + 1) * P],
                                     ps[:, 2 * (t % 2) + h, :].rearrange("p (k n) -> p k n", k=4)).then_inc(copied, 1)

            @block.vector
            def _(dve):
                ch = Chain(dve, order)
                dve.wait_ge(squared, TT)
                dve.tensor_scalar(var[:], ss[:], 1.0 / D, EPS, ALU.mult, ALU.add).then_inc(var_ready, 1)
                dve.wait_ge(std_ready, 1)
                ch(dve.reciprocal(rstd[:], std[:]))
                dve.wait_ge(gain_in, 16)
                for t in range(TT):
                    dve.scalar_tensor_tensor(out=hn[:, t, :], in0=c.res[:, t, :], scalar=rstd[:, t:t + 1], in1=gb[:],
                                             op0=ALU.mult, op1=ALU.mult).then_inc(hn_ready, 1)

            @block.tensor
            def _(pe):
                if h_T is None:
                    return
                for t in range(TT):
                    pe.wait_ge(hn_ready, t + 1)
                    for h in range(2):
                        if t >= 2:
                            pe.wait_ge(copied, 2 * (t - 2) + h + 1)
                        for k in range(4):
                            last = pe.transpose(ps[:, 2 * (t % 2) + h, k * P:(k + 1) * P],
                                                hn[:, t, (4 * h + k) * P:(4 * h + k + 1) * P], c.ident[:])
                        last.then_inc(turned, 1)


def project_ab(nc, c, w, mu, h_T, proj):
    w_t = w.rearrange("(k p) m -> p k m", p=P)
    with phase(nc, c) as (sem, sb):
        w_in = [sem("w_in0"), sem("w_in1")]
        w_free, summed = sem("w_free"), [sem("summed_a"), sem("summed_v")]
        bank_free = [sem("bank_free_a"), sem("bank_free_v")]
        order, order_a, first_copied, mu_in = sem("order"), sem("order_a"), sem("first_copied"), sem("mu_in")
        wt = sb("w_tiles", [P, 2, KT, P])
        mu_t = sb("mu", [P, AB_TILES])
        shift = sb("shift", [P, 1, S])
        ps = c.ps
        cleared, zero_made = sem("cleared", True), sem("zero_made")
        zero = sb("zero_rows", [P, D])
        with nc.Block() as block:

            @block.gpsimd
            def _(pool):
                pool.memset(zero[:], 0.0).then_inc(zero_made, 1)
                pool.wait_ge(zero_made, 1)
                for n in range(NBLK + 1):
                    pool.dma_start(c.ys[n * P:(n + 1) * P, :], zero[:]).then_inc(cleared, 16)
                pool.wait_ge(cleared, 16 * (NBLK + 1))

            @block.sync
            def _(sp):
                sp.dma_start(mu_t[:, 0:T_GATE], column(mu)).then_inc(mu_in, 16)
                with sp.Fori(0, AB_TILES // 2) as i:
                    for q in range(2):
                        take(sp, w_free)
                        sp.dma_start(wt[:, q], w_t[:, :, bass.ds(i * (2 * P) + q * P, P)]).then_inc(w_in[q], 16)

            @block.tensor
            def _(pe):
                pe.sem_inc(w_free, 2)
                with pe.Fori(0, AB_TILES // 2):
                    for q in range(2):
                        take(pe, w_in[q], 16)
                        for h in range(NH):
                            take(pe, bank_free[h])
                            for k in range(KT):
                                last = pe.matmul(ps[:, 2 * q + h, :], wt[:, q, k, :], h_T[:, k, h * HALF:(h + 1) * HALF],
                                                 start=k == 0, stop=k == KT - 1)
                            last.then_inc(summed[h], 1)
                        pe.drain().then_inc(w_free, 1)

            @block.scalar
            def _(act):
                act.sem_inc(bank_free[0], 2)
                with act.Fori(0, AB_TILES // 2) as i:
                    for q in range(2):
                        take(act, summed[0])
                        act.copy(proj[:, bass.ds(2 * i + q, 1), 0:HALF], ps[:, 2 * q:2 * q + 1, :]).then_inc(order_a, 1)
                        take(act, order_a)
                        act.sem_inc(bank_free[0], 1)
                        act.sem_inc(first_copied, 1)

            @block.vector
            def _(dve):
                def link(ins):
                    ins.then_inc(order, 1)
                    take(dve, order)

                link(dve.memset(mu_t[:, T_GATE:AB_TILES], 0.0))
                dve.wait_ge(mu_in, 16)
                dve.sem_inc(bank_free[1], 2)
                with dve.Fori(0, AB_TILES // 2) as i:
                    for q in range(2):
                        take(dve, summed[1])
                        m = bass.ds(2 * i + q, 1)
                        dve.tensor_copy(proj[:, m, HALF:S], ps[:, 2 * q + 1:2 * q + 2, :]).then_inc(order, 1)
                        take(dve, order)
                        dve.sem_inc(bank_free[1], 1)
                        take(dve, first_copied)
                        link(dve.tensor_tensor(shift[:, :, 1:S], proj[:, m, 0:S - 1], proj[:, m, 1:S], ALU.subtract))
                        link(dve.tensor_scalar(shift[:, :, 0:1], proj[:, m, 0:1], -1.0, None, ALU.mult))
                        link(dve.scalar_tensor_tensor(out=proj[:, m, :], in0=shift[:], scalar=mu_t[:, m], in1=proj[:, m, :],
                                                      op0=ALU.mult, op1=ALU.add))


def lru(nc, c, a, proj):
    gate, xb = proj[:, T_GATE:T_GATE + 4, :], proj[:, T_XB:T_XB + 4, :]
    w_a = a["lru_w_a"][0].rearrange("(j p) d e -> (p d) j e", p=2)
    w_x = a["lru_w_x"][0].rearrange("(j p) d e -> (p d) j e", p=2)
    with phase(nc, c) as (sem, sb):
        names = ("par_in", "order", "exp_lam", "lam_ready", "conv_done", "gates_summed", "gates_done", "i_done",
                 "decay_done", "tanh_done", "power_ready", "root_done", "gelu_done", "bank_free")
        s = {n: sem(n) for n in names}
        wa, wx = sb("lru_wa", [P, 4, HD]), sb("lru_wx", [P, 4, HD])
        cw, cb = sb("conv_w", [P, 4, 4]), sb("conv_b", [P, 4])
        ba, bx, lam = sb("b_a", [P, 4]), sb("b_x", [P, 4]), sb("lam", [P, 4])
        neg, y, z, z2, ser, rate, nrate = (sb(n, [P, 4]) for n in ("lam_neg", "lam_y", "lam_z", "lam_z2", "lam_ser", "rate", "nrate"))
        xc, rr, ii, dec = (sb(n, [P, 4, S]) for n in ("conv", "r_gate", "i_gate", "decay"))
        ps = c.ps
        with nc.Block() as block:

            @block.sync
            def _(sp):
                sp.dma_start(wa[:], w_a).then_inc(s["par_in"], 16)
                sp.dma_start(wx[:], w_x).then_inc(s["par_in"], 16)
                for i in range(4):
                    sp.dma_start(cw[:, i, :], column(a["lru_conv_w"][0, i])).then_inc(s["par_in"], 16)
                for t, v in ((cb, "lru_conv_b"), (ba, "lru_b_a"), (bx, "lru_b_x"), (lam, "lru_lambda")):
                    sp.dma_start(t[:], column(a[v][0])).then_inc(s["par_in"], 16)
                sp.wait_ge(s["par_in"], 160)

            @block.vector
            def _(dve):
                ch = Chain(dve, s["order"])
                dve.wait_ge(s["par_in"], 160)
                ch(dve.tensor_scalar(neg[:], lam[:], -1.0, None, ALU.mult))
                dve.tensor_tensor(z[:], lam[:], neg[:], ALU.max).then_inc(s["lam_ready"], 1)
                dve.wait_ge(s["exp_lam"], 1)
                ch(dve.tensor_scalar(z[:], y[:], 2.0, None, ALU.add))
                ch(dve.reciprocal(z2[:], z[:]))
                ch(dve.tensor_tensor(z[:], y[:], z2[:], ALU.mult))
                ch(dve.tensor_tensor(z2[:], z[:], z[:], ALU.mult))
                ch(dve.tensor_scalar(ser[:], z2[:], 1.0 / 17, None, ALU.mult))
                for k in range(7, 0, -1):
                    ch(dve.scalar_tensor_tensor(out=ser[:], in0=ser[:], scalar=1.0 / (2 * k + 1), in1=z2[:],
                                                op0=ALU.add, op1=ALU.mult))
                ch(dve.scalar_tensor_tensor(out=ser[:], in0=ser[:], scalar=1.0, in1=z[:], op0=ALU.add, op1=ALU.mult))
                ch(dve.tensor_scalar(neg[:], neg[:], 0.0, None, ALU.max))
                ch(dve.scalar_tensor_tensor(out=ser[:], in0=ser[:], scalar=2.0, in1=neg[:], op0=ALU.mult, op1=ALU.add))
                ch(dve.tensor_scalar(rate[:], ser[:], -8.0, None, ALU.mult))
                dve.tensor_scalar(nrate[:], ser[:], 8.0, None, ALU.mult).then_inc(s["lam_ready"], 1)
                for j in range(4):
                    ch(dve.tensor_scalar(xc[:, j, :], xb[:, j, :], cw[:, 3, j:j + 1], cb[:, j:j + 1], ALU.mult, ALU.add))
                for d in range(1, 4):
                    for j in range(4):
                        ins = dve.scalar_tensor_tensor(out=xc[:, j, d:S], in0=xb[:, j, 0:S - d], scalar=cw[:, 3 - d, j:j + 1],
                                                       in1=xc[:, j, d:S], op0=ALU.mult, op1=ALU.add)
                        if d < 3:
                            ch(ins)
                        else:
                            ins.then_inc(s["conv_done"], 1)
                for j in range(4):
                    dve.wait_ge(s["tanh_done"], j + 1)
                    ch(dve.tensor_scalar(xb[:, j, :], rr[:, j, :], 1.0, None, ALU.add))
                    ch(dve.reciprocal(xb[:, j, :], xb[:, j, :]))
                    dve.scalar_tensor_tensor(out=rr[:, j, :], in0=rr[:, j, :], scalar=2.0, in1=xb[:, j, :],
                                             op0=ALU.mult, op1=ALU.mult).then_inc(s["power_ready"], 1)
                for j in range(4):
                    dve.wait_ge(s["i_done"], j + 1)
                    ch(dve.tensor_tensor(ii[:, j, :], ii[:, j, :], xc[:, j, :], ALU.mult))
                for j in range(4):
                    dve.wait_ge(s["root_done"], j + 1)
                    ch(dve.tensor_tensor(ii[:, j, :], ii[:, j, :], rr[:, j, :], ALU.mult))
                    ch(dve.tensor_tensor_scan(xc[:, j, :], dec[:, j, :], ii[:, j, :], 0.0, ALU.mult, ALU.add))
                    dve.wait_ge(s["gelu_done"], j + 1)
                    ch(dve.tensor_tensor(gate[:, j, :], gate[:, j, :], xc[:, j, :], ALU.mult))

            @block.tensor
            def _(pe):
                pe.wait_ge(s["par_in"], 160)
                for j in range(4):
                    pe.wait_ge(s["conv_done"], j + 1)
                    if j >= 2:
                        pe.wait_ge(s["gates_done"], j - 1)
                        pe.wait_ge(s["i_done"], j - 1)
                    for g, w in ((0, wa), (1, wx)):
                        for h in range(NH):
                            for p in (0, HD):
                                last = pe.matmul(ps[p:p + HD, 4 * (j % 2) + 2 * g + h, :], w[p:p + HD, j, :],
                                                 xc[p:p + HD, j, h * HALF:(h + 1) * HALF], start=True, stop=True)
                    last.then_inc(s["gates_summed"], 1)

            @block.scalar
            def _(act):
                act.wait_ge(s["lam_ready"], 1)
                act.activation(y[:], z[:], ACT.Exp, scale=-1.0).then_inc(s["exp_lam"], 1)
                for j in range(4):
                    act.wait_ge(s["gates_summed"], j + 1)
                    b = 4 * (j % 2)
                    act.activation(rr[:, j, :], ps[:, b:b + 2, :].rearrange("p h n -> p (h n)"), ACT.Sigmoid,
                                   bias=ba[:, j:j + 1]).then_inc(s["gates_done"], 1)
                    act.activation(ii[:, j, :], ps[:, b + 2:b + 4, :].rearrange("p h n -> p (h n)"), ACT.Sigmoid,
                                   bias=bx[:, j:j + 1]).then_inc(s["i_done"], 1)
                act.wait_ge(s["lam_ready"], 2)
                for j in range(4):
                    act.wait_ge(s["gates_done"], j + 1)
                    act.activation(dec[:, j, :], rr[:, j, :], ACT.Exp, scale=rate[:, j:j + 1]).then_inc(s["decay_done"], 1)
                for j in range(4):
                    act.wait_ge(s["decay_done"], j + 1)
                    act.activation(rr[:, j, :], rr[:, j, :], ACT.Tanh, scale=nrate[:, j:j + 1]).then_inc(s["tanh_done"], 1)
                for j in range(4):
                    act.activation(gate[:, j, :], gate[:, j, :], ACT.Gelu_apprx_tanh).then_inc(s["gelu_done"], 1)
                for j in range(4):
                    act.wait_ge(s["power_ready"], j + 1)
                    act.activation(rr[:, j, :], rr[:, j, :], ACT.Sqrt).then_inc(s["root_done"], 1)


def rwkv_prepare(nc, c, a, proj, b):
    r, k, v = (proj[:, t:t + 4, :] for t in (T_R, T_K, T_V))
    kk = proj[:, T_XB:T_XB + 4, :]
    B0, B1, B2, B3, B4 = b.bufs
    flat = lambda t: t.rearrange("p j s -> p (j s)")
    chunked = lambda t: t.rearrange("p j (n q) -> p (j n) q", q=HD)
    with phase(nc, c) as (sem, sb):
        names = ("par_in", "order", "order_a", "tanh_done", "z_summed", "z_done", "a_summed", "a_done", "cum_ready",
                 "kk_ready", "kk_squared", "kk_summed", "kk_max", "kk_root", "bonus_in", "bonus_summed",
                 "exp_done", "mask_made", "step_ready", "step_done")
        s = {n: sem(n) for n in names}
        w2, a2, g2 = b.w2a2, b.w2a2, b.g2
        th = proj[:, T_WA, :]
        reset = B4[:, 0, :]
        w0, a0, k_k, k_a, r_k, k_a1 = (sb(n, [P, 4]) for n in ("w0", "a0", "k_k", "k_a", "r_k", "one_minus_k_a"))
        mid, end, tmp = (sb(n, [P, 4, NCH]) for n in ("cum_mid", "cum_end", "step_log"))
        ps = c.ps

        with nc.Block() as block:

            @block.sync
            def _(sp):
                sp.dma_start(w2[0:HD, :], a["rw_w2"][0]).then_inc(s["par_in"], 16)
                sp.dma_start(a2[HD:P, :], a["rw_a2"][0]).then_inc(s["par_in"], 16)
                sp.dma_start(g2[:], a["rw_g2"][0]).then_inc(s["par_in"], 16)
                for t, n in ((w0, "rw_w0"), (a0, "rw_a0"), (k_k, "rw_k_k"), (k_a, "rw_k_a"), (b.ln_w, "rw_ln_w"), (b.ln_b, "rw_ln_b")):
                    sp.dma_start(t[:], column(a[n][0])).then_inc(s["par_in"], 16)
                sp.dma_start(r_k[:], a["rw_r_k"][0].rearrange("(j h) n -> (h n) j", h=2)).then_inc(s["par_in"], 16)
                sp.wait_ge(s["par_in"], 160)

            @block.gpsimd
            def _(pool):
                ch = Chain(pool, s["mask_made"])
                ch(pool.memset(reset, 1.0))
                ch(pool.memset(reset.rearrange("p (n q) -> p n q", q=HD)[:, :, 0:1], 0.0))

            @block.scalar
            def _(act):
                ch = Chain(act, s["order_a"])
                act.wait_ge(s["par_in"], 160)
                act.activation(th[0:HD, :], proj[0:HD, T_WA, :], ACT.Tanh).then_inc(s["tanh_done"], 1)
                ch(act.activation(proj[:, T_G, :], proj[:, T_G, :], ACT.Sigmoid))
                for j in range(4):
                    q = j % 2
                    act.wait_ge(s["z_summed"], j + 1)
                    act.activation(B0[:, j, :], ps[:, 2 * q:2 * q + 2, :].rearrange("p h n -> p (h n)"), ACT.Sigmoid,
                                   bias=w0[:, j:j + 1]).then_inc(s["z_done"], 1)
                    act.wait_ge(s["a_summed"], j + 1)
                    act.activation(B1[:, j, :], ps[:, 4 + 2 * q:6 + 2 * q, :].rearrange("p h n -> p (h n)"), ACT.Sigmoid,
                                   bias=a0[:, j:j + 1]).then_inc(s["a_done"], 1)
                act.wait_ge(s["kk_ready"], 1)
                act.activation(flat(B3[:]), flat(kk), ACT.Square).then_inc(s["kk_squared"], 1)
                act.wait_ge(s["kk_max"], 1)
                act.activation(flat(B3[:]), flat(B3[:]), ACT.Sqrt).then_inc(s["kk_root"], 1)
                act.wait_ge(s["step_ready"], 1)
                act.activation(b.step[:].rearrange("p j n -> p (j n)"), tmp[:].rearrange("p j n -> p (j n)"), ACT.Exp).then_inc(s["step_done"], 1)
                act.wait_ge(s["cum_ready"], 2)
                act.activation(flat(B4[:]), flat(B2[:]), ACT.Exp, scale=-1.0).then_inc(s["exp_done"], 1)
                act.activation(flat(B3[:]), flat(B3[:]), ACT.Exp).then_inc(s["exp_done"], 1)
                act.wait_ge(s["exp_done"], 1)
                act.activation(flat(B2[:]), flat(B2[:]), ACT.Exp).then_inc(s["exp_done"], 1)
                act.wait_ge(s["step_done"], 1)

            @block.tensor
            def _(pe):
                pe.wait_ge(s["par_in"], 160)
                pe.wait_ge(s["tanh_done"], 1)
                for j in range(4):
                    q = j % 2
                    if j >= 2:
                        pe.wait_ge(s["z_done"], j - 1)
                        pe.wait_ge(s["a_done"], j - 1)
                    for h in range(NH):
                        last = pe.matmul(ps[:, 2 * q + h, :], w2[0:HD, j * P:(j + 1) * P], th[0:HD, h * HALF:(h + 1) * HALF],
                                         start=True, stop=True)
                    last.then_inc(s["z_summed"], 1)
                    for h in range(NH):
                        last = pe.matmul(ps[:, 4 + 2 * q + h, :], a2[HD:P, j * P:(j + 1) * P],
                                         proj[HD:P, T_WA, h * HALF:(h + 1) * HALF], start=True, stop=True)
                    last.then_inc(s["a_summed"], 1)
                pe.wait_ge(s["kk_squared"], 1)
                pe.wait_ge(s["z_done"], 4)
                pe.wait_ge(s["a_done"], 4)
                for j in range(4):
                    for h in range(NH):
                        last = pe.matmul(ps[:, 2 * j + h, :], c.head_ones[:], B3[:, j, h * HALF:(h + 1) * HALF], start=True, stop=True)
                last.then_inc(s["kk_summed"], 1)
                pe.wait_ge(s["bonus_in"], 1)
                for j in range(4):
                    for h in range(NH):
                        last = pe.matmul(ps[:, 2 * j + h, :], c.head_ones[:], B0[:, j, h * HALF:(h + 1) * HALF], start=True, stop=True)
                last.then_inc(s["bonus_summed"], 1)

            @block.vector
            def _(dve):
                ch = Chain(dve, s["order"])
                dve.wait_ge(s["par_in"], 160)
                ch(dve.tensor_scalar(k_a1[:], k_a[:], -1.0, 1.0, ALU.mult, ALU.add))
                for j in range(4):
                    ch(dve.tensor_scalar(kk[:, j, :], k[:, j, :], k_k[:, j:j + 1], None, ALU.mult))
                dve.sem_inc(s["kk_ready"], 1)
                dve.wait_ge(s["z_done"], 4)
                ch(dve.tensor_scalar(flat(B0[:]), flat(B0[:]), -0.6065306597126334, None, ALU.mult))
                dve.wait_ge(s["mask_made"], 2)
                for j in range(4):
                    ch(dve.tensor_tensor_scan(B2[:, j, :], reset, B0[:, j, :], 0.0, ALU.mult, ALU.add))
                cum = B2[:].rearrange("p j (n q) -> p j n q", q=HD)
                ch(dve.tensor_copy(mid[:], cum[:, :, :, HD // 2 - 1]))
                ch(dve.tensor_copy(end[:], cum[:, :, :, HD - 1]))
                ch(dve.tensor_tensor(tmp[:], end[:], mid[:], ALU.subtract))
                dve.tensor_tensor(tmp[:, :, 0:NCH - 1], tmp[:, :, 0:NCH - 1], mid[:, :, 1:NCH], ALU.add).then_inc(s["step_ready"], 1)
                ch(dve.tensor_tensor(chunked(B2[:]), chunked(B2[:]),
                                     bcast(mid[:].rearrange("p j n -> p (j n)"), 2, HD), ALU.subtract))
                dve.wait_ge(s["kk_summed"], 1)
                dve.tensor_scalar(flat(B3[:]), ps[:].rearrange("p b n -> p (b n)"), 1e-24, None, ALU.max).then_inc(s["kk_max"], 1)
                dve.wait_ge(s["kk_root"], 1)
                ch(dve.reciprocal(flat(B3[:]), flat(B3[:])))
                ch(dve.tensor_tensor(flat(kk), flat(kk), flat(B3[:]), ALU.mult))
                dve.tensor_tensor(flat(B3[:]), flat(B2[:]), flat(B0[:]), ALU.subtract).then_inc(s["cum_ready"], 2)
                dve.wait_ge(s["a_done"], 4)
                dve.wait_ge(s["cum_ready"], 2)
                for j in range(4):
                    ch(dve.tensor_scalar(B0[:, j, :], B1[:, j, :], k_a[:, j:j + 1], k_a1[:, j:j + 1], ALU.mult, ALU.add))
                ch(dve.tensor_tensor(flat(k), flat(k), flat(B0[:]), ALU.mult))
                for j in range(4):
                    ch(dve.scalar_tensor_tensor(out=B0[:, j, :], in0=r[:, j, :], scalar=r_k[:, j:j + 1], in1=k[:, j, :],
                                                op0=ALU.mult, op1=ALU.mult))
                dve.sem_inc(s["bonus_in"], 1)
                ch(dve.tensor_tensor(flat(B1[:]), flat(B1[:]), flat(kk), ALU.mult))
                dve.wait_ge(s["exp_done"], 3)
                ch(dve.tensor_tensor(flat(B1[:]), flat(B1[:]), flat(B4[:]), ALU.mult))
                ch(dve.scalar_tensor_tensor(out=flat(B3[:]), in0=flat(kk), scalar=-1.0, in1=flat(B3[:]), op0=ALU.mult, op1=ALU.mult))
                ch(dve.tensor_tensor(flat(r), flat(r), flat(B2[:]), ALU.mult))
                ch(dve.tensor_tensor(flat(k), flat(k), flat(B4[:]), ALU.mult))
                dve.wait_ge(s["bonus_summed"], 1)
                ch(dve.tensor_tensor(flat(B0[:]), ps[:].rearrange("p b n -> p (b n)"), flat(v), ALU.mult))


def make_chunk_masks(nc, c, b):
    with phase(nc, c) as (sem, sb):
        made = sem("masks_made")
        with nc.Block() as block:

            @block.gpsimd
            def _(pool):
                ch = Chain(pool, made)
                for p in (0, HD):
                    ch(pool.tensor_copy(b.ident64[p:p + HD, :], c.ident[p:p + HD, p:p + HD]))
                ch(pool.memset(c.lower_1[:], 1.0))
                ch(pool.memset(c.upper[:], 1.0))
                ch(pool.memset(c.strict_incl[:], 1.0))
                for p in (0, HD):
                    def keep(view, pattern, base, mult=0):
                        ch(pool.affine_select(out=view, in_=view, pattern=pattern, compare_op=ALU.is_ge, fill=0.0,
                                              base=base, channel_multiplier=mult))
                    low = c.lower_1[p:p + HD, :].rearrange("p (n h) -> p n h", h=2)
                    keep(low, [[-2, 32], [-1000, 2]], -1, 1)
                    keep(low, [[2, 32], [0, 2]], 1, -1)
                    for i, w in enumerate(LEVELS):
                        up = c.upper[p:p + HD, i, :].rearrange("p (n h q) -> p n h q", h=2, q=w)
                        keep(up, [[-2 * w, HD // (2 * w)], [1000, 2], [0, w]], -1000, 1)
                        keep(up, [[2 * w, HD // (2 * w)], [0, 2], [0, w]], w - 1, -1)
                    keep(c.strict_incl[p:p + HD, 0, :], [[1, HD]], -1, -1)
                    keep(c.strict_incl[p:p + HD, 1, :], [[1, HD]], 0, -1)


def rwkv_chunks(nc, c, proj, b):
    r, k, v = (proj[:, t:t + 4, :] for t in (T_R, T_K, T_V))
    ab, bb = b.bufs[3], b.bufs[1]
    y = r
    NI = 2 * NPAIR
    with phase(nc, c) as (sem, sb):
        names = ("staged", "stage_free", "gram_done", "turned_done", "order", "order_a", "masked", "tok_ready", "x_first",
                 "t1_done", "t1_copied", "dx_done", "x_next", "u_done", "u_copied", "sa_done", "sa_copied", "ds_done",
                 "s_ready", "y_done", "y_copied", "turn_end_a", "turn_end_v")
        s = {n: sem(n) for n in names}
        AR = sb("stage_ar", [P, 2, NPAIR, 2, HD])
        BS, KS, VS = (sb(n, [P, 2, NPAIR, HD]) for n in ("stage_b", "stage_k", "stage_v"))
        tok = sb("row_major", [P, 3, NI, HD])
        MK = proj[:, T_XB + 3, :].rearrange("p (m i n) -> p m i n", m=2, i=NI)
        RB = sb("masked_rb", [P, NI, HD])
        LO = proj[:, T_XB:T_XB + 3, :].rearrange("p t s -> p (t s)")[:, 0:5 * NI * HD].rearrange("p (v i n) -> p v i n", v=5, i=NI)
        X, XT, T1 = (sb(n, [P, NI, HD]) for n in ("x_inv", "x_inv_t", "t1"))
        U, SA = (sb(n, [P, 2, NPAIR, HD]) for n in ("u_rows", "sa_rows"))
        SS = sb("state", [P, 2, NPAIR, HD])
        sn = sb("state_sum", [P, NPAIR, HD])
        ps = c.ps
        eye = [c.ident[p:p + HD, p:p + HD] for p in (0, HD)]
        items = [(ci, j) for ci in range(2) for j in range(NPAIR)]
        lt_rb = ps[:, 0:2, :].rearrange("p k (i m n) -> p (k i) m n", m=2, n=HD)
        mt_rk = ps[:, 2:4, :].rearrange("p k (i m n) -> p (k i) m n", m=2, n=HD)
        low = ps[:, 4, :].rearrange("p (i n) -> p i n", n=HD)
        eye_b = [None]

        def halves():
            return ((0, slice(0, HD)), (1, slice(HD, P)))

        with nc.Block() as block:

            @block.scalar
            def _(act):
                def link(ins):
                    ins.then_inc(s["order_a"], 1)
                    take(act, s["order_a"])

                with act.Fori(0, NCH // 2) as i:
                    for src, dst in ((ab, AR[:, :, :, 0, :]), (r, AR[:, :, :, 1, :])):
                        for ci in range(2):
                            link(act.copy(dst[:, ci], src[:, :, bass.ds(i * P + ci * HD, HD)]))
                    for src, dst in ((bb, BS), (k, KS), (v, VS)):
                        for ci in range(2):
                            link(act.copy(dst[:, ci], src[:, :, bass.ds(i * P + ci * HD, HD)]))
                    act.sem_inc(s["staged"], 1)
                    take(act, s["turned_done"])
                    for m in range(3):
                        link(act.copy(tok[:, m].rearrange("p i n -> p (i n)"), ps[:, 5 + m, :]))
                    act.sem_inc(s["tok_ready"], 1)
                    for lv in range(5):
                        take(act, s["t1_done"])
                        act.copy(T1[:].rearrange("p i n -> p (i n)"), ps[:, 0, :]).then_inc(s["t1_copied"], 1)
                    for ci in range(2):
                        take(act, s["u_done"])
                        act.copy(U[:, ci].rearrange("p j n -> p (j n)"), ps[:, 3, 0:NPAIR * HD]).then_inc(s["u_copied"], 1)
                        take(act, s["sa_done"])
                        act.copy(SA[:, ci].rearrange("p j n -> p (j n)"), ps[:, 4, 0:NPAIR * HD]).then_inc(s["sa_copied"], 1)
                        take(act, s["y_done"])
                        link(act.copy(y[:, :, bass.ds(i * P + ci * HD, HD)], ps[:, 6 + ci, 0:NPAIR * HD].rearrange("p (j n) -> p j n", j=NPAIR)))
                    act.sem_inc(s["turn_end_a"], 1)

            @block.tensor
            def _(pe):
                pe.sem_inc(s["turn_end_v"], 1)
                pe.sem_inc(s["turn_end_a"], 1)
                with pe.Fori(0, NCH // 2):
                    take(pe, s["staged"])
                    take(pe, s["turn_end_a"])
                    take(pe, s["turn_end_v"])
                    for m, src in enumerate((VS, BS, KS)):
                        for n, (ci, j) in enumerate(items):
                            for h, q in halves():
                                last = pe.matmul(ps[q, 5 + m, n * HD:(n + 1) * HD], src[q, ci, j, :], eye[h], start=True, stop=True)
                    last.then_inc(s["turned_done"], 1)
                    for n, (ci, j) in enumerate(items):
                        for h, q in halves():
                            pe.matmul(lt_rb[q, n].rearrange("p m n -> p (m n)"), BS[q, ci, j, :],
                                      AR[q, ci, j].rearrange("p m n -> p (m n)"), start=True, stop=True)
                            pe.matmul(mt_rk[q, n].rearrange("p m n -> p (m n)"), KS[q, ci, j, :],
                                      AR[q, ci, j].rearrange("p m n -> p (m n)"), start=True, stop=True)
                            last = pe.matmul(low[q, n], AR[q, ci, j, 0, :], BS[q, ci, j, :], start=True, stop=True)
                    last.then_inc(s["gram_done"], 1)
                    take(pe, s["x_first"])
                    for lv in range(5):
                        if lv:
                            take(pe, s["x_next"])
                        for n in range(NI):
                            for h, q in halves():
                                last = pe.matmul(ps[q, 0, n * HD:(n + 1) * HD], LO[q, lv, n, :], X[q, n, :], start=True, stop=True)
                        last.then_inc(s["t1_done"], 1)
                        take(pe, s["t1_copied"])
                        for n in range(NI):
                            for h, q in halves():
                                if lv < 4:
                                    pe.matmul(ps[q, 1, n * HD:(n + 1) * HD], XT[q, n, :], T1[q, n, :], start=True, stop=True)
                                last = pe.matmul(ps[q, 2, n * HD:(n + 1) * HD], T1[q, n, :], XT[q, n, :], start=True, stop=True)
                        last.then_inc(s["dx_done"], 1)
                    take(pe, s["x_next"])
                    take(pe, s["tok_ready"])
                    for ci in range(2):
                        take(pe, s["s_ready"])
                        for j in range(NPAIR):
                            n = ci * NPAIR + j
                            for h, q in halves():
                                pe.matmul(ps[q, 3, j * HD:(j + 1) * HD], MK[q, 0, n, :], tok[q, 0, n, :], start=True, stop=False)
                                last = pe.matmul(ps[q, 3, j * HD:(j + 1) * HD], AR[q, ci, j, 0, :], SS[q, ci, j, :], start=False, stop=True)
                        last.then_inc(s["u_done"], 1)
                        take(pe, s["u_copied"])
                        for j in range(NPAIR):
                            n = ci * NPAIR + j
                            for h, q in halves():
                                last = pe.matmul(ps[q, 4, j * HD:(j + 1) * HD], XT[q, n, :], U[q, ci, j, :], start=True, stop=True)
                        last.then_inc(s["sa_done"], 1)
                        take(pe, s["sa_copied"])
                        for j in range(NPAIR):
                            n = ci * NPAIR + j
                            for h, q in halves():
                                pe.matmul(ps[q, 5, j * HD:(j + 1) * HD], tok[q, 1, n, :], SA[q, ci, j, :], start=True, stop=False)
                                last = pe.matmul(ps[q, 5, j * HD:(j + 1) * HD], tok[q, 2, n, :], tok[q, 0, n, :], start=False, stop=True)
                        last.then_inc(s["ds_done"], 1)
                        for j in range(NPAIR):
                            n = ci * NPAIR + j
                            for h, q in halves():
                                o = ps[q, 6 + ci, j * HD:(j + 1) * HD]
                                pe.matmul(o, SS[q, ci, j, :], AR[q, ci, j, 1, :], start=True, stop=False)
                                pe.matmul(o, SA[q, ci, j, :], RB[q, n, :], start=False, stop=False)
                                last = pe.matmul(o, tok[q, 0, n, :], MK[q, 1, n, :], start=False, stop=True)
                        last.then_inc(s["y_done"], 1)

            @block.vector
            def _(dve):
                def link(ins):
                    ins.then_inc(s["order"], 1)
                    take(dve, s["order"])

                link(dve.memset(SS[:, 0], 0.0))
                dve.sem_inc(s["s_ready"], 1)
                ident64 = b.ident64
                up = lambda lv: bcast(c.upper[:, lv, :], 1, NI)
                with dve.Fori(0, NCH // 2) as i:
                    take(dve, s["gram_done"])
                    link(dve.tensor_tensor(X[:], low, bcast(c.lower_1[:], 1, NI), ALU.mult))
                    link(dve.tensor_tensor(X[:], X[:], bcast(ident64[:], 1, NI), ALU.add))
                    link(dve.tensor_tensor(XT[:], lt_rb[:, :, 0, :], up(0), ALU.mult))
                    link(dve.tensor_tensor(XT[:], XT[:], bcast(ident64[:], 1, NI), ALU.add))
                    for lv in range(5):
                        link(dve.tensor_tensor(LO[:, lv], lt_rb[:, :, 0, :], up(lv + 1), ALU.mult))
                    link(dve.tensor_tensor(RB[:], lt_rb[:, :, 1, :], bcast(c.strict_incl[:, 1, :], 1, NI), ALU.mult))
                    for m in range(2):
                        link(dve.tensor_tensor(MK[:, m], mt_rk[:, :, m, :], bcast(c.strict_incl[:, m, :], 1, NI), ALU.mult))
                    dve.sem_inc(s["x_first"], 1)
                    for lv in range(5):
                        take(dve, s["dx_done"])
                        fl = lambda t: t[:].rearrange("p i n -> p (i n)")
                        if lv < 4:
                            link(dve.tensor_tensor(fl(X), fl(X), ps[:, 1, :], ALU.add))
                        dve.tensor_tensor(fl(XT), fl(XT), ps[:, 2, :], ALU.add).then_inc(s["x_next"], 1)
                    for ci in range(2):
                        take(dve, s["ds_done"])
                        link(dve.tensor_tensor(sn[:], SS[:, ci], ps[:, 5, 0:NPAIR * HD].rearrange("p (j n) -> p j n", j=NPAIR), ALU.add))
                        stepc = b.step[:, :, bass.ds(2 * i + ci, 1)].to_broadcast([P, NPAIR, HD])
                        dve.tensor_tensor(SS[:, 1 - ci], sn[:], stepc, ALU.mult).then_inc(s["s_ready"], 1)
                    dve.sem_inc(s["turn_end_v"], 1)


def rwkv_finish(nc, c, proj, b):
    B0, y = b.bufs[0], proj[:, T_R:T_R + 4, :]
    yc = y
    flat = lambda t: t.rearrange("p j s -> p (j s)")
    with phase(nc, c) as (sem, sb):
        names = ("order", "mean_summed", "centred", "squared", "var_summed", "var_ready", "root_done", "g_summed", "banks_read")
        s = {n: sem(n) for n in names}
        B4 = sb("squares", [P, NPAIR, S])
        ps = c.ps
        psf = ps[:].rearrange("p b n -> p (b n)")
        with nc.Block() as block:

            @block.tensor
            def _(pe):
                for j in range(4):
                    for h in range(NH):
                        last = pe.matmul(ps[:, 2 * j + h, :], c.head_ones[:], y[:, j, h * HALF:(h + 1) * HALF], start=True, stop=True)
                last.then_inc(s["mean_summed"], 1)
                pe.wait_ge(s["squared"], 1)
                for j in range(4):
                    for h in range(NH):
                        last = pe.matmul(ps[:, 2 * j + h, :], c.head_ones[:], B4[:, j, h * HALF:(h + 1) * HALF], start=True, stop=True)
                last.then_inc(s["var_summed"], 1)
                pe.wait_ge(s["var_ready"], 1)
                for j in range(4):
                    for h in range(NH):
                        last = pe.matmul(ps[:, 2 * j + h, :], b.g2[:, j * P:(j + 1) * P], proj[:, T_G, h * HALF:(h + 1) * HALF],
                                         start=True, stop=True)
                last.then_inc(s["g_summed"], 1)

            @block.scalar
            def _(act):
                act.wait_ge(s["centred"], 1)
                act.activation(flat(B4[:]), flat(yc), ACT.Square).then_inc(s["squared"], 1)
                act.wait_ge(s["var_ready"], 1)
                act.activation(flat(B4[:]), flat(B4[:]), ACT.Sqrt).then_inc(s["root_done"], 1)

            @block.vector
            def _(dve):
                ch = Chain(dve, s["order"])
                dve.wait_ge(s["mean_summed"], 1)
                dve.scalar_tensor_tensor(out=flat(yc), in0=psf, scalar=-1.0 / HD, in1=flat(y), op0=ALU.mult,
                                         op1=ALU.add).then_inc(s["centred"], 1)
                dve.wait_ge(s["var_summed"], 1)
                dve.tensor_scalar(flat(B4[:]), psf, 1.0 / HD, GN_EPS, ALU.mult, ALU.add).then_inc(s["var_ready"], 1)
                dve.wait_ge(s["root_done"], 1)
                ch(dve.reciprocal(flat(B4[:]), flat(B4[:])))
                ch(dve.tensor_tensor(flat(yc), flat(yc), flat(B4[:]), ALU.mult))
                for j in range(4):
                    ch(dve.tensor_scalar(yc[:, j, :], yc[:, j, :], b.ln_w[:, j:j + 1], b.ln_b[:, j:j + 1], ALU.mult, ALU.add))
                ch(dve.tensor_tensor(flat(yc), flat(yc), flat(B0[:]), ALU.add))
                dve.wait_ge(s["g_summed"], 1)
                ch(dve.tensor_tensor(flat(yc), flat(yc), psf, ALU.mult))


def project_out(nc, c, w, parts):
    w_t = w.rearrange("(k p) n -> p k n", p=P)
    with phase(nc, c) as (sem, sb):
        w_in, staged, stage_free = sem("w_in"), sem("staged"), sem("stage_free")
        summed, bank_free, order = sem("summed"), sem("bank_free"), sem("order")
        wt = sb("w_out", [P, KT, D])
        st = sb("y_stage", [P, 2, KT, P])
        ps = c.ps
        with nc.Block() as block:

            @block.sync
            def _(sp):
                for k in range(KT):
                    sp.dma_start(wt[:, k, :], w_t[:, k, :]).then_inc(w_in, 16)
                sp.wait_ge(w_in, 16 * KT)

            @block.scalar
            def _(act):
                act.sem_inc(stage_free, 2)
                with act.Fori(0, TT // 2) as i:
                    for q in range(2):
                        take(act, stage_free)
                        k0 = 0
                        for part in parts:
                            n = part.shape[1]
                            act.copy(st[:, q, k0:k0 + n, :], part[:, :, bass.ds(i * (2 * P) + q * P, P)]).then_inc(order, 1)
                            take(act, order)
                            k0 += n
                        act.sem_inc(staged, 1)

            @block.tensor
            def _(pe):
                pe.wait_ge(w_in, 16 * KT)
                with pe.Fori(0, TT // 2):
                    for q in range(2):
                        take(pe, staged)
                        for h in range(2):
                            take(pe, bank_free)
                            for k in range(KT):
                                last = pe.matmul(ps[:, 2 * q + h, :], st[:, q, k, :], wt[:, k, h * HALF:(h + 1) * HALF],
                                                 start=k == 0, stop=k == KT - 1)
                            last.then_inc(summed, 1)
                        pe.drain().then_inc(stage_free, 1)

            @block.vector
            def _(dve):
                dve.sem_inc(bank_free, 4)
                with dve.Fori(0, TT // 2) as i:
                    for q in range(2):
                        for h in range(2):
                            take(dve, summed)
                            rs = c.res[:, bass.ds(2 * i + q, 1), h * HALF:(h + 1) * HALF]
                            dve.tensor_tensor(rs, rs, ps[:, 2 * q + h:2 * q + h + 1, :], ALU.add).then_inc(bank_free, 1)


def route(nc, c, m, h_T, w_group, b_group, w_expert, b_expert):
    NL = NG + NE
    with phase(nc, c) as (sem, sb):
        names = ("par_in", "made", "summed", "order", "group_shift", "group_exp", "pair_shift", "pair_exp", "picked",
                 "ranked")
        s = {n: sem(n) for n in names}
        wr = sb("w_router", [P, KT, NL])
        bias = sb("b_router", [P, NL])
        upper = sb("tokens_before", [P, P])
        it = sb("iota", [P, 64])
        i128 = sb("iota_128", [P, EPG])
        lg = sb("logits", [P, TT, NL])
        col = {n: sb(n, [P, TT]) for n in ("gmax", "gsum", "ggate", "m1", "m2", "rden", "first")}
        gsh, gsel, gtmp = (sb(n, [P, TT, NG]) for n in ("g_shift", "g_sel", "g_tmp"))
        ex, ex2, etmp, oh1, oh2 = (sb(n, [P, TT, EPG]) for n in ("e_logits", "e_rest", "e_tmp", "e_hot1", "e_hot2"))
        prod = sb("e_prod", [P, TT, EPG, NG])
        sel = [sb(f"sel{k}", [P, TT, NE]) for k in range(2)]
        both = sb("sel_both", [P, TT, NE])
        rows = sb("rows_of_expert", [P, TT, NE])
        rtmp = sb("rows_tmp", [P, TT, NE])
        rowf = sb("row_f", [P, 2, TT])
        nblk, pend, pstart = (sb(n, [P, NE]) for n in ("n_blocks", "blocks_end", "blocks_start"))
        cmp8 = sb("cmp_blocks", [P, NE, EPG])
        cmpb = sb("cmp_expert", [P, NBLK, NE])
        blkf = sb("block_expert_f", [P, NBLK])
        turnf, tcmp = sb("turns_f", [P, 1]), sb("turns_cmp", [P, NBLK // 2])
        ps = c.ps
        with nc.Block() as block:

            @block.sync
            def _(sp):
                sp.dma_start(wr[:, :, 0:NG], w_group.rearrange("(k p) g -> p k g", p=P)).then_inc(s["par_in"], 16)
                sp.dma_start(wr[:, :, NG:NL], w_expert.rearrange("(k p) g -> p k g", p=P)).then_inc(s["par_in"], 16)
                sp.dma_start(bias[:, 0:NG], b_group.partition_broadcast(P)).then_inc(s["par_in"], 16)
                sp.dma_start(bias[:, NG:NL], b_expert.partition_broadcast(P)).then_inc(s["par_in"], 16)
                sp.wait_ge(s["par_in"], 64)

            @block.gpsimd
            def _(pool):
                ch = Chain(pool, s["made"])
                ch(pool.iota(it[:], [[1, 64]], base=0, channel_multiplier=0, allow_small_or_imprecise_dtypes=True))
                ch(pool.iota(i128[:], [[P, EPG]], base=0, channel_multiplier=0, allow_small_or_imprecise_dtypes=True))
                ch(pool.memset(upper[:], 1.0))
                ch(pool.affine_select(out=upper[:], in_=upper[:], pattern=[[1, P]], compare_op=ALU.is_gt, fill=0.0,
                                      base=0, channel_multiplier=-1))

            @block.tensor
            def _(pe):
                pe.wait_ge(s["par_in"], 64)
                for t in range(TT):
                    for k in range(KT):
                        last = pe.matmul(ps[:, 0, t * NL:(t + 1) * NL], h_T[:, k, t * P:(t + 1) * P], wr[:, k, :],
                                         start=k == 0, stop=k == KT - 1)
                last.then_inc(s["summed"], 1)
                pe.wait_ge(s["picked"], 1)
                pe.wait_ge(s["made"], 4)
                for t in range(TT):
                    for u in range(t + 1):
                        pe.matmul(ps[:, 1, t * NE:(t + 1) * NE], upper[:] if u == t else c.ones[:], both[:, u, :],
                                  start=u == 0, stop=u == t)
                for u in range(TT):
                    last = pe.matmul(ps[:, 2, 0:NE], c.ones[:], both[:, u, :], start=u == 0, stop=u == TT - 1)
                last.then_inc(s["ranked"], 1)

            @block.scalar
            def _(act):
                act.wait_ge(s["group_shift"], 1)
                act.activation(gtmp[:], gsh[:], ACT.Exp).then_inc(s["group_exp"], 1)
                act.wait_ge(s["pair_shift"], 1)
                act.activation(col["m2"][:], col["m2"][:], ACT.Exp).then_inc(s["pair_exp"], 1)

            @block.vector
            def _(dve):
                ch = Chain(dve, s["order"])

                def first_hot(hot, src, top, n):
                    ch(dve.tensor_reduce(top[:], src, AX.X, ALU.max))
                    ch(dve.tensor_tensor(hot, src, bcast(top[:], 2, n), ALU.is_equal))
                    ch(dve.scalar_tensor_tensor(out=hot, in0=hot, scalar=-64.0, in1=bcast(it[:, 0:n], 1, TT),
                                                op0=ALU.mult, op1=ALU.add))
                    ch(dve.tensor_reduce(col["first"][:], hot, AX.X, ALU.min))
                    ch(dve.tensor_tensor(hot, hot, bcast(col["first"][:], 2, n), ALU.is_equal))

                dve.wait_ge(s["made"], 2)
                dve.wait_ge(s["summed"], 1)
                ch(dve.tensor_tensor(lg[:], ps[:, 0, 0:TT * NL].rearrange("p (t n) -> p t n", t=TT), bcast(bias[:], 1, TT), ALU.add))
                g = lg[:, :, 0:NG]
                first_hot(gsel[:], g, col["gmax"], NG)
                dve.tensor_tensor(gsh[:], g, bcast(col["gmax"][:], 2, NG), ALU.subtract).then_inc(s["group_shift"], 1)
                dve.wait_ge(s["group_exp"], 1)
                ch(dve.tensor_reduce(col["gsum"][:], gtmp[:], AX.X, ALU.add))
                ch(dve.reciprocal(col["ggate"][:], col["gsum"][:]))
                ch(dve.tensor_tensor(prod[:], lg[:, :, NG:NL].rearrange("p t (g e) -> p t e g", g=NG),
                                     bcast(gsel[:], 2, EPG), ALU.mult))
                ch(dve.tensor_reduce(ex[:], prod[:], AX.X, ALU.add))
                first_hot(oh1[:], ex[:], col["m1"], EPG)
                ch(dve.scalar_tensor_tensor(out=ex2[:], in0=oh1[:], scalar=-BIG, in1=ex[:], op0=ALU.mult, op1=ALU.add))
                first_hot(oh2[:], ex2[:], col["m2"], EPG)
                dve.tensor_tensor(col["m2"][:], col["m2"][:], col["m1"][:], ALU.subtract).then_inc(s["pair_shift"], 1)
                for k, oh in enumerate((oh1, oh2)):
                    ch(dve.tensor_tensor(sel[k][:].rearrange("p t (g e) -> p t g e", g=NG), bcast(gsel[:], 3, EPG),
                                         bcast(oh[:], 2, NG), ALU.mult))
                dve.tensor_tensor(both[:], sel[0][:], sel[1][:], ALU.add).then_inc(s["picked"], 1)
                dve.wait_ge(s["pair_exp"], 1)
                ch(dve.tensor_scalar(col["rden"][:], col["m2"][:], 1.0, None, ALU.add))
                ch(dve.reciprocal(col["rden"][:], col["rden"][:]))
                ch(dve.tensor_tensor(m.gate[:, 0, :], col["rden"][:], col["ggate"][:], ALU.mult))
                ch(dve.tensor_tensor(m.gate[:, 1, :], m.gate[:, 0, :], col["m2"][:], ALU.mult))
                dve.wait_ge(s["ranked"], 1)
                ch(dve.tensor_copy(nblk[:], ps[:, 2, 0:NE]))
                ch(dve.tensor_tensor(cmp8[:], bcast(nblk[:], 2, EPG), bcast(i128[:], 1, NE), ALU.is_gt))
                ch(dve.tensor_reduce(nblk[:], cmp8[:], AX.X, ALU.add))
                ch(dve.tensor_tensor_scan(pend[:], c.ones[:, 0:NE], nblk[:], 0.0, ALU.mult, ALU.add))
                ch(dve.tensor_tensor(pstart[:], pend[:], nblk[:], ALU.subtract))
                ch(dve.tensor_scalar(pstart[:], pstart[:], float(P), float(P), ALU.mult, ALU.add))
                ch(dve.tensor_tensor(rows[:], ps[:, 1, 0:TT * NE].rearrange("p (t n) -> p t n", t=TT), bcast(pstart[:], 1, TT), ALU.add))
                for k in range(2):
                    ch(dve.tensor_tensor(rtmp[:], rows[:], sel[k][:], ALU.mult))
                    ch(dve.tensor_reduce(rowf[:, k, :], rtmp[:], AX.X, ALU.add))
                ch(dve.tensor_copy(m.row[:], rowf[:]))
                ch(dve.tensor_tensor(cmpb[:], bcast(pend[:], 1, NBLK), bcast(it[:, 0:NBLK], 2, NE), ALU.is_le))
                ch(dve.tensor_reduce(blkf[:], cmpb[:], AX.X, ALU.add))
                ch(dve.tensor_scalar(blkf[:], blkf[:], float(NE - 1), None, ALU.min))
                ch(dve.tensor_copy(m.block_expert[:], blkf[:]))
                ch(dve.tensor_scalar(tcmp[:], it[:, 0:NBLK // 2], 2.0, None, ALU.mult))
                ch(dve.tensor_tensor(tcmp[:], tcmp[:], pend[:, NE - 1:NE].to_broadcast([P, NBLK // 2]), ALU.is_lt))
                ch(dve.tensor_reduce(turnf[:], tcmp[:], AX.X, ALU.add))
                ch(dve.tensor_copy(m.turns[:], turnf[:]))


def dispatch(nc, c, m, row_tok):
    with phase(nc, c) as (sem, sb):
        made, cleared, placed, back = sem("made"), sem("cleared", True), sem("placed", True), sem("back", True)
        widened, turned = sem("widened"), sem("turned")
        by_block, by_block_f = sb("token_by_block", [NBLK, P], I32), sb("token_by_block_f", [NBLK, P])
        ps = c.ps
        zero = sb("zero_rows", [P, NBLK + 1], I32)
        tok = sb("token_id", [P, TT], I32)
        with nc.Block() as block:

            @block.gpsimd
            def _(pool):
                ch = Chain(pool, made)
                ch(pool.memset(zero[:], 0))
                ch(pool.iota(tok[:], [[P, TT]], base=0, channel_multiplier=1))
                pool.dma_start(row_tok.rearrange("(p n) o -> p (n o)", p=P), zero[:]).then_inc(cleared, 16)
                pool.wait_ge(cleared, 16)
                for k in range(2):
                    for t in range(TT):
                        pool.indirect_dma_start(row_tok, bass.IndirectOffsetOnAxis(ap=m.row[:, k, t:t + 1], axis=0),
                                                tok[:, t:t + 1], None).then_inc(placed, 16)
                pool.wait_ge(placed, 32 * TT)
                pool.dma_start(by_block[:], row_tok[P:, 0].rearrange("(b p) -> b p", p=P)).then_inc(back, 16)

            @block.vector
            def _(dve):
                dve.wait_ge(back, 16)
                dve.tensor_copy(by_block_f[:], by_block[:]).then_inc(widened, 1)
                dve.wait_ge(turned, 1)
                dve.tensor_copy(m.row_token[:], ps[:, 0, 0:NBLK])

            @block.tensor
            def _(pe):
                pe.wait_ge(widened, 1)
                pe.transpose(ps[:, 0, 0:NBLK], by_block_f[:], c.ident[0:NBLK, 0:NBLK]).then_inc(turned, 1)


def experts(nc, c, m, rows, ys, w_gate, w_up, w_down):
    with phase(nc, c) as (sem, sb):
        two = lambda n: [sem(n + "0"), sem(n + "1")]
        x_in, x_ready, x_free = [sem("x_in0", True), sem("x_in1", True)], two("x_ready"), two("x_free")
        gu_in, gu_free, d_in, d_free = two("gu_in"), two("gu_free"), two("d_in"), two("d_free")
        x_turned, xT_ready = sem("x_turned"), sem("xT_ready")
        g_done, u_done, silu_ready, hid_ready = sem("g_done"), sem("u_done"), sem("silu_ready"), sem("hid_ready")
        hid_turned, hidT_ready = sem("hid_turned"), sem("hidT_ready")
        d_done, d_bank_free, y_ready, y_stored = two("d_done"), two("d_bank_free"), two("y_ready"), two("y_stored")
        order, order_p = sem("order"), sem("order_p")
        wg, wu = sb("w_gate", [P, 2, KT, FF]), sb("w_up", [P, 2, KT, FF])
        wd = sb("w_down", [P, 2, FF // P, D])
        idx = sb("row_index", [P, 2, 1], I32)
        xg, xT = sb("x_rows", [P, 2, D]), sb("x_T", [P, 2, KT, P])
        sg, hid, hT = sb("silu", [P, 2, FF]), sb("hidden", [P, 2, FF]), sb("hidden_T", [P, 2, FF // P, P])
        yb = sb("y_rows", [P, 2, D])
        ps = c.ps

        def turns(eng):
            return eng.value_load(m.turns[0:1, 0:1], min_val=1, max_val=NBLK // 2)

        with nc.Block() as block:

            @block.sync
            def _(sp):
                n = turns(sp)
                with sp.Fori(0, n) as i:
                    e = [sp.value_load(m.block_expert[0:1, bass.ds(2 * i + q, 1)], min_val=0, max_val=NE - 1) for q in range(2)]
                    for q in range(2):
                        take(sp, gu_free[q])
                        sp.dma_start(wg[:, q], w_gate[bass.ds(e[q], 1)].rearrange("e (k p) f -> p (e k) f", p=P)).then_inc(gu_in[q], 16)
                        sp.dma_start(wu[:, q], w_up[bass.ds(e[q], 1)].rearrange("e (k p) f -> p (e k) f", p=P)).then_inc(gu_in[q], 16)
                    for q in range(2):
                        take(sp, d_free[q])
                        sp.dma_start(wd[:, q], w_down[bass.ds(e[q], 1)].rearrange("e (k p) f -> p (e k) f", p=P)).then_inc(d_in[q], 16)

            @block.gpsimd
            def _(pool):
                pool.memset(yb[:], 0.0).then_inc(order_p, 1)
                take(pool, order_p)
                pool.sem_inc(y_ready[1], 1)
                n = turns(pool)
                with pool.Fori(0, n) as i:
                    for q in range(2):
                        take(pool, x_free[q])
                        pool.tensor_copy(idx[:, q, :], m.row_token[:, bass.ds(2 * i + q, 1)]).then_inc(order_p, 1)
                        take(pool, order_p)
                        pool.indirect_dma_start(xg[:, q, :], None, rows, bass.IndirectOffsetOnAxis(ap=idx[:, q, :], axis=0)).then_inc(x_in[q], 16)
                    for q in range(2):
                        pool.wait_ge(x_in[q], 16 * i + 16)
                        pool.sem_inc(x_ready[q], 1)

            @block.scalar
            def _(act):
                for q in range(2):
                    act.sem_inc(x_free[q], 1)
                act.sem_inc(y_stored[0], 16)

                def x_copies(q):
                    for h in range(2):
                        take(act, x_turned)
                        act.copy(xT[:, q, 4 * h:4 * h + 4, :], ps[:, h, :].rearrange("p (k n) -> p k n", k=4)).then_inc(xT_ready, 1)
                    act.sem_inc(x_free[q], 1)

                def silu(q):
                    take(act, g_done)
                    act.activation(sg[:, q, :], ps[:, 2 + q, :], ACT.Silu).then_inc(silu_ready, 1)

                def hidden_copy(q):
                    take(act, hid_turned)
                    act.copy(hT[:, q].rearrange("p k n -> p (k n)"), ps[:, 5, :]).then_inc(hidT_ready, 1)

                n = turns(act)
                with act.Fori(0, n) as i:
                    x_copies(0)
                    silu(0)
                    take(act, y_ready[1])
                    act.dma_start(ys[bass.ds(2 * i * P, P), :], yb[:, 1, :]).then_inc(y_stored[1], 16)
                    x_copies(1)
                    silu(1)
                    hidden_copy(0)
                    hidden_copy(1)
                    take(act, y_ready[0])
                    act.dma_start(ys[bass.ds((2 * i + 1) * P, P), :], yb[:, 0, :]).then_inc(y_stored[0], 16)
                take(act, y_ready[1])
                act.dma_start(ys[bass.ds(2 * n * P, P), :], yb[:, 1, :]).then_inc(y_stored[1], 16)
                act.wait_ge(y_stored[0], 16)
                act.wait_ge(y_stored[1], 16)

            @block.tensor
            def _(pe):
                def turn_x(q):
                    take(pe, x_ready[q])
                    for h in range(2):
                        for k in range(4):
                            last = pe.transpose(ps[:, h, k * P:(k + 1) * P], xg[:, q, (4 * h + k) * P:(4 * h + k + 1) * P], c.ident[:])
                        last.then_inc(x_turned, 1)
                    take(pe, xT_ready, 2)

                def into(bank, w, q, done):
                    for k in range(KT):
                        last = pe.matmul(ps[:, bank, :], xT[:, q, k, :], w[:, q, k, :], start=k == 0, stop=k == KT - 1)
                    last.then_inc(done, 1)

                def turn_hidden(q):
                    take(pe, hid_ready)
                    for k in range(FF // P):
                        last = pe.transpose(ps[:, 5, k * P:(k + 1) * P], hid[:, q, k * P:(k + 1) * P], c.ident[:])
                    last.then_inc(hid_turned, 1)

                def down(q, h):
                    take(pe, d_bank_free[h])
                    for k in range(FF // P):
                        last = pe.matmul(ps[:, 6 + h, :], hT[:, q, k, :], wd[:, q, k, h * HALF:(h + 1) * HALF],
                                         start=k == 0, stop=k == FF // P - 1)
                    last.then_inc(d_done[h], 1)

                n = turns(pe)
                with pe.Fori(0, n):
                    turn_x(0)
                    take(pe, gu_in[0], 32)
                    into(2, wg, 0, g_done)
                    into(4, wu, 0, u_done)
                    turn_x(1)
                    take(pe, gu_in[1], 32)
                    into(3, wg, 1, g_done)
                    turn_hidden(0)
                    into(4, wu, 1, u_done)
                    take(pe, hidT_ready)
                    take(pe, d_in[0], 16)
                    down(0, 0)
                    turn_hidden(1)
                    down(0, 1)
                    take(pe, hidT_ready)
                    take(pe, d_in[1], 16)
                    down(1, 0)
                    down(1, 1)

            @block.vector
            def _(dve):
                for q in range(2):
                    dve.sem_inc(gu_free[q], 1)
                    dve.sem_inc(d_free[q], 1)
                    dve.sem_inc(d_bank_free[q], 1)
                n = turns(dve)
                with dve.Fori(0, n):
                    for q in range(2):
                        take(dve, silu_ready)
                        take(dve, u_done)
                        dve.sem_inc(gu_free[q], 1)
                        dve.tensor_tensor(hid[:, q, :], sg[:, q, :], ps[:, 4, :], ALU.mult).then_inc(hid_ready, 1)
                    for q in range(2):
                        take(dve, y_stored[q], 16)
                        for h in range(2):
                            take(dve, d_done[h])
                            dve.tensor_copy(yb[:, q, h * HALF:(h + 1) * HALF], ps[:, 6 + h, :]).then_inc(order, 1)
                            take(dve, order)
                            dve.sem_inc(d_bank_free[h], 1)
                        dve.sem_inc(d_free[q], 1)
                        dve.sem_inc(y_ready[q], 1)


def combine(nc, c, m, ys):
    NB = 4
    with phase(nc, c) as (sem, sb):
        got = [sem(f"got{i}", True) for i in range(NB)]
        used = sem("used")
        yg = sb("y_gathered", [P, NB, D])
        with nc.Block() as block:

            @block.gpsimd
            def _(pool):
                for n in range(2 * TT):
                    t, k = n // 2, n % 2
                    if n >= NB:
                        pool.wait_ge(used, n - NB + 1)
                    pool.indirect_dma_start(yg[:, n % NB, :], None, ys, bass.IndirectOffsetOnAxis(ap=m.row[:, k, t:t + 1], axis=0)).then_inc(got[n % NB], 16)

            @block.vector
            def _(dve):
                for n in range(2 * TT):
                    t, k = n // 2, n % 2
                    dve.wait_ge(got[n % NB], 16 * (n // NB + 1))
                    if n:
                        dve.wait_ge(used, n)
                    dve.scalar_tensor_tensor(out=c.res[:, t, :], in0=yg[:, n % NB, :], scalar=m.gate[:, k, t:t + 1],
                                             in1=c.res[:, t, :], op0=ALU.mult, op1=ALU.add).then_inc(used, 1)


def moe(nc, c, a, layer):
    with ExitStack() as ctx:
        def sb(name, shape, dt=F32):
            return ctx.enter_context(nc.sbuf_tensor(f"{name}_{layer}", shape, dt))

        m = Chip()
        m.row, m.gate = sb("row_of", [P, 2, TT], I32), sb("gate_of", [P, 2, TT])
        m.row_token = sb("token_of_row", [P, NBLK], I32)
        m.block_expert, m.turns = sb("block_expert", [P, NBLK], I32), sb("turns", [P, 1], I32)
        with nc.sbuf_tensor(f"h_T_ffn_{layer}", [P, KT, S], F32) as h_T:
            norm(nc, c, a["norm_ffn"][layer], h_T=h_T, rows=c.rows)
            route(nc, c, m, h_T, a["moe_w_group"][layer], a["moe_b_group"][layer], a["moe_w_expert"][layer], a["moe_b_expert"][layer])
        dispatch(nc, c, m, c.row_tok)
        experts(nc, c, m, c.rows, c.ys, a["moe_w_gate"][layer], a["moe_w_up"][layer], a["moe_w_down"][layer])
        combine(nc, c, m, c.ys)


def hgrn(nc, c, w, lower_bound, norm_w, h_T, y_T):
    w_t = w.rearrange("(k p) m -> p k m", p=P)
    NL = len(HLEVELS)
    with phase(nc, c) as (sem, sb):
        names = ("par_in", "lb_order", "lb_exp", "masks_made", "order", "order_a",
                 "proj_done", "head_ready", "v_ready", "head_done", "fg_ready", "lf_ready", "k_ready",
                 "diff_ready", "exp_ready", "level_ready", "step_ready", "kd_ready", "qe_ready", "bc_ready",
                 "v_turned", "v_rows_ready", "kd_turned", "kd_rows_ready", "ds_done", "s_ready", "score_ready",
                 "o_done", "sq_ready", "sq_summed", "var_ready", "rstd_ready", "tail_free", "o_read")
        s = {n: sem(n) for n in names}
        w_in, w_free = [sem(f"w_in{n}") for n in range(4)], [sem(f"w_free{n}") for n in range(4)]
        bank_free = [sem("bank_free0"), sem("bank_free1")]
        gram_done, gram_free = [sem("gram_done0"), sem("gram_done1")], [sem("gram_free0"), sem("gram_free1")]
        wt = sb("w_tiles", [P, 4, KT, P])
        Q, G, V, F = (sb(n, [P, 2, S]) for n in ("q", "g", "v", "log_f"))
        K, BC = sb("k", [P, S]), sb("cum_log_f", [P, S])
        E = sb("level_ops", [P, 4, S])
        KD, QE = sb("k_to_end", [P, S]), sb("q_from_start", [P, S])
        VR, KR = sb("v_rows", [P, TT, P]), sb("k_rows", [P, TT, P])
        SC = sb("scores_T", [P, TT, P])
        ST = sb("states", [P, TT, P])
        reset = sb("chunk_reset", [P, S])
        mask = sb("level_masks", [P, NL, P])
        step = sb("step", [P, TT])
        lb, lb1, nw = sb("lower_bound", [P, HEADS]), sb("one_minus_lb", [P, HEADS]), sb("norm_w", [P, HEADS])
        l0, l1, lm = (sb(n, [P, HEADS]) for n in ("lb0", "lb1_in", "lb_max"))
        ps = c.ps
        pair = lambda ap: ap.rearrange("p b n -> p (b n)")
        col = lambda t, h: t[:, bass.ds(h, 1)]

        def make_masks(pool):
            ch = Chain(pool, s["masks_made"])
            ch(pool.memset(mask[:], 1.0))
            for i, hw in enumerate(HLEVELS):
                up = mask[:, i, :].rearrange("p (n h q) -> p n h q", h=2, q=hw)
                for pat, base, mult in (([[-2 * hw, P // (2 * hw)], [1000, 2], [0, hw]], -1000, 1),
                                        ([[2 * hw, P // (2 * hw)], [0, 2], [0, hw]], hw - 1, -1)):
                    ch(pool.affine_select(out=up, in_=up, pattern=pat, compare_op=ALU.is_ge, fill=0.0, base=base,
                                          channel_multiplier=mult))
            ch(pool.memset(reset[:], 1.0))
            ch(pool.memset(reset[:].rearrange("p (n q) -> p n q", q=P)[:, :, 0:1], 0.0))
            return ch.n

        n_masks = 1 + 2 * NL + 2

        def level_view(t, lv):
            return t.rearrange("p (n w) -> p n w", w=2 * HLEVELS[lv])

        with nc.Block() as block:

            @block.gpsimd
            def _(pool):
                assert make_masks(pool) == n_masks

            @block.sync
            def _(sp):
                for t, v in ((l0, lower_bound[0]), (l1, lower_bound[1]), (nw, norm_w)):
                    sp.dma_start(t[:], column(v)).then_inc(s["par_in"], 16)

                def load(h):
                    for m in range(4):
                        take(sp, w_free[m])
                        c0 = ORDER[m] * D
                        sp.dma_start(wt[:, m], w_t[:, :, bass.ds(h * P + c0, P)]).then_inc(w_in[m], 16)

                ORDER = (1, 0, 3, 2)
                with sp.Fori(0, HEADS) as h:
                    load(h)
                sp.wait_ge(s["par_in"], 48)

            @block.tensor
            def _(pe):
                def project(m):
                    take(pe, w_in[m], 16)
                    take(pe, bank_free[m % 2])
                    for h in range(NH):
                        for k in range(KT):
                            last = pe.matmul(ps[:, 2 * (m % 2) + h, :], wt[:, m, k, :], h_T[:, k, h * HALF:(h + 1) * HALF],
                                             start=k == 0, stop=k == KT - 1)
                    last.then_inc(s["proj_done"], 1)

                def gram(left, right):
                    for b in range(2):
                        take(pe, gram_free[b])
                        for n in range(4):
                            t = slice((4 * b + n) * P, (4 * b + n + 1) * P)
                            last = pe.matmul(ps[:, 4 + b, n * P:(n + 1) * P], left[:, t], right[:, t], start=True, stop=True)
                        last.then_inc(gram_done[b], 1)

                def turn(src, done):
                    for n in range(TT):
                        last = pe.transpose(ps[:, 6 + n // 4, (n % 4) * P:(n % 4 + 1) * P], src[:, n * P:(n + 1) * P], c.ident[:])
                    last.then_inc(done, 1)

                def half(par, more):
                    take(pe, s["v_ready"])
                    take(pe, s["tail_free"])
                    turn(V[:, par, :], s["v_turned"])
                    take(pe, s["k_ready"])
                    gram(K[:], Q[:, par, :])
                    for m in range(4):
                        if more:
                            project(m)
                        for lv in (2 * m, 2 * m + 1):
                            if lv < NL:
                                take(pe, s["level_ready"])
                                gram(E[:, lv % 4, :], E[:, lv % 4, :])
                    take(pe, s["v_rows_ready"])
                    take(pe, s["kd_ready"])
                    turn(KD[:], s["kd_turned"])
                    take(pe, s["kd_rows_ready"])
                    for n in range(TT):
                        last = pe.matmul(ps[:, 6 + n // 4, (n % 4) * P:(n % 4 + 1) * P], KR[:, n, :], VR[:, n, :], start=True, stop=True)
                    last.then_inc(s["ds_done"], 1)
                    take(pe, s["s_ready"])
                    take(pe, s["qe_ready"])
                    for b in range(2):
                        take(pe, gram_free[b])
                    for n in range(TT):
                        o = ps[:, 4 + n // 4, (n % 4) * P:(n % 4 + 1) * P]
                        pe.matmul(o, VR[:, n, :], SC[:, n, :], start=True, stop=False)
                        last = pe.matmul(o, ST[:, n, :], QE[:, n * P:(n + 1) * P], start=False, stop=True)
                    last.then_inc(s["o_done"], 1)
                    take(pe, s["sq_ready"])
                    for h in range(NH):
                        last = pe.matmul(ps[:, 6 + h, :], c.ones[:], BC[:, h * HALF:(h + 1) * HALF], start=True, stop=True)
                    last.then_inc(s["sq_summed"], 1)

                for m in range(4):
                    project(m)
                with pe.Fori(0, HEADS // 2 - 1):
                    half(0, True)
                    half(1, True)
                half(0, True)
                half(1, False)

            @block.scalar
            def _(act):
                act.wait_ge(s["lb_order"], 2)
                act.activation(l0[:], l0[:], ACT.Exp).then_inc(s["lb_exp"], 1)
                act.activation(l1[:], l1[:], ACT.Exp).then_inc(s["lb_exp"], 1)
                for m in range(4):
                    act.sem_inc(w_free[m], 1)
                for q in range(2):
                    act.sem_inc(bank_free[q], 1)

                def link(ins):
                    ins.then_inc(s["order_a"], 1)
                    take(act, s["order_a"])

                def copy_out(m, par):
                    take(act, s["proj_done"])
                    act.sem_inc(w_free[m], 1)
                    src = pair(ps[:, 2 * (m % 2):2 * (m % 2) + 2, :])
                    if m == 0:
                        link(act.activation(F[:, par, :], src, ACT.Sigmoid))
                    elif m == 3:
                        link(act.copy(V[:, par, :], src))
                    else:
                        link(act.activation((Q, G)[m - 1][:, par, :], src, ACT.Silu))
                    act.sem_inc(bank_free[m % 2], 1)
                    if m == 3:
                        act.sem_inc(s["head_ready"], 1)
                        act.sem_inc(s["v_ready"], 1)

                def level_exp(lv):
                    take(act, s["diff_ready"])
                    v, hw = level_view(E[:, lv % 4, :], lv), HLEVELS[lv]
                    link(act.activation(v[:, :, 0:hw], v[:, :, 0:hw], ACT.Exp, scale=-1.0))
                    act.activation(v[:, :, hw:2 * hw], v[:, :, hw:2 * hw], ACT.Exp).then_inc(s["exp_ready"], 1)

                def half(par, more):
                    take(act, s["fg_ready"])
                    act.activation(F[:, par, :], F[:, par, :], ACT.Ln).then_inc(s["lf_ready"], 1)
                    take(act, s["v_turned"])
                    act.copy(VR[:].rearrange("p t n -> p (t n)"), pair(ps[:, 6:8, :])).then_inc(s["v_rows_ready"], 1)
                    take(act, s["bc_ready"])
                    act.activation(step[:], BC[:].rearrange("p (n q) -> p n q", q=P)[:, :, P - 1], ACT.Exp).then_inc(s["step_ready"], 1)
                    if more:
                        take(act, s["head_done"])
                    for m in range(4):
                        if more:
                            copy_out(m, 1 - par)
                        for lv in (2 * m, 2 * m + 1):
                            if lv < NL:
                                level_exp(lv)
                    take(act, s["diff_ready"])
                    act.activation(KD[:], KD[:], ACT.Exp).then_inc(s["exp_ready"], 1)
                    act.activation(QE[:], BC[:], ACT.Exp).then_inc(s["exp_ready"], 1)
                    take(act, s["kd_turned"])
                    act.copy(KR[:].rearrange("p t n -> p (t n)"), pair(ps[:, 6:8, :])).then_inc(s["kd_rows_ready"], 1)
                    take(act, s["o_done"])
                    act.activation(BC[:], pair(ps[:, 4:6, :]), ACT.Square).then_inc(s["sq_ready"], 1)
                    take(act, s["var_ready"])
                    link(act.activation(F[:, par, :], F[:, par, :], ACT.Ln))
                    act.activation(F[:, par, :], F[:, par, :], ACT.Exp, scale=-0.5).then_inc(s["rstd_ready"], 1)

                for m in range(4):
                    copy_out(m, 0)
                with act.Fori(0, HEADS // 2 - 1):
                    half(0, True)
                    half(1, True)
                half(0, True)
                half(1, False)

            @block.vector
            def _(dve):
                ch = Chain(dve, s["lb_order"])
                dve.wait_ge(s["par_in"], 48)
                ch(dve.tensor_tensor(lm[:], l0[:], l1[:], ALU.max))
                dve.tensor_tensor(l0[:], l0[:], lm[:], ALU.subtract)
                ch(dve.tensor_tensor(l1[:], l1[:], lm[:], ALU.subtract))
                dve.wait_ge(s["lb_exp"], 2)
                ch(dve.tensor_tensor(l0[:], l0[:], l1[:], ALU.add))
                ch(dve.reciprocal(l0[:], l0[:]))
                ch(dve.tensor_tensor(lb[:], l1[:], l0[:], ALU.mult))
                ch(dve.tensor_scalar(lb1[:], lb[:], -1.0, 1.0, ALU.mult, ALU.add))
                dve.wait_ge(s["masks_made"], n_masks)

                def link(ins):
                    ins.then_inc(s["order"], 1)
                    take(dve, s["order"])

                for b in range(2):
                    dve.sem_inc(gram_free[b], 1)
                dve.sem_inc(s["tail_free"], 1)
                dve.sem_inc(s["head_done"], 1)
                link(dve.memset(ST[:, 0, :], 0.0))

                def pick(lv):
                    m = c.ident[:] if lv is None else mask[:, lv, :]
                    for b in range(2):
                        take(dve, gram_done[b])
                        link(dve.copy_predicated(SC[:, 4 * b:4 * b + 4, :], bcast(m.bitcast(U32), 1, 4),
                                                 ps[:, 4 + b, :].rearrange("p (n t) -> p n t", n=4)))
                        dve.sem_inc(gram_free[b], 1)

                def diff(lv):
                    v, hw = level_view(BC[:], lv), HLEVELS[lv]
                    ref = v[:, :, hw - 1:hw].to_broadcast([P, S // (2 * hw), 2 * hw])
                    dve.tensor_tensor(level_view(E[:, lv % 4, :], lv), v, ref, ALU.subtract).then_inc(s["diff_ready"], 1)

                def scale(lv, par):
                    take(dve, s["exp_ready"])
                    v, hw = level_view(E[:, lv % 4, :], lv), HLEVELS[lv]
                    kv, qv = level_view(K[:], lv), level_view(Q[:, par, :], lv)
                    link(dve.tensor_tensor(v[:, :, 0:hw], v[:, :, 0:hw], kv[:, :, 0:hw], ALU.mult))
                    dve.tensor_tensor(v[:, :, hw:2 * hw], v[:, :, hw:2 * hw], qv[:, :, hw:2 * hw], ALU.mult).then_inc(s["level_ready"], 1)

                def half(h, par):
                    take(dve, s["head_ready"])
                    link(dve.tensor_scalar(F[:, par, :], F[:, par, :], col(lb1, h), col(lb, h), ALU.mult, ALU.add))
                    link(dve.tensor_scalar(K[:], F[:, par, :], -1.0, 1.0, ALU.mult, ALU.add))
                    dve.sem_inc(s["fg_ready"], 1)
                    dve.sem_inc(s["k_ready"], 1)
                    link(dve.memset(SC[:], 0.0))
                    take(dve, s["lf_ready"])
                    link(dve.tensor_tensor_scan(BC[:], reset[:], F[:, par, :], 0.0, ALU.mult, ALU.add))
                    dve.sem_inc(s["bc_ready"], 1)
                    diff(0)
                    pick(None)
                    diff(1)
                    scale(0, par)
                    for lv in range(2, NL):
                        diff(lv)
                        scale(lv - 1, par)
                        pick(lv - 2)
                    bc = BC[:].rearrange("p (n q) -> p n q", q=P)
                    dve.tensor_tensor(KD[:].rearrange("p (n q) -> p n q", q=P), bc[:, :, P - 1:P].to_broadcast([P, TT, P]), bc,
                                      ALU.subtract).then_inc(s["diff_ready"], 1)
                    scale(NL - 1, par)
                    pick(NL - 2)
                    pick(NL - 1)
                    take(dve, s["exp_ready"])
                    dve.tensor_tensor(KD[:], KD[:], K[:], ALU.mult).then_inc(s["kd_ready"], 1)
                    take(dve, s["exp_ready"])
                    dve.tensor_tensor(QE[:], QE[:], Q[:, par, :], ALU.mult).then_inc(s["qe_ready"], 1)
                    take(dve, s["ds_done"])
                    take(dve, s["step_ready"])
                    for n in range(TT - 1):
                        link(dve.scalar_tensor_tensor(out=ST[:, n + 1, :], in0=ST[:, n, :], scalar=step[:, n:n + 1],
                                                      in1=ps[:, 6 + n // 4, (n % 4) * P:(n % 4 + 1) * P], op0=ALU.mult, op1=ALU.add))
                    dve.sem_inc(s["s_ready"], 1)
                    take(dve, s["sq_summed"])
                    link(dve.tensor_scalar(F[:, par, :], pair(ps[:, 6:8, :]), 1.0 / P, EPS, ALU.mult, ALU.add))
                    dve.sem_inc(s["var_ready"], 1)
                    dve.sem_inc(s["tail_free"], 1)
                    take(dve, s["rstd_ready"])
                    link(dve.scalar_tensor_tensor(out=F[:, par, :], in0=pair(ps[:, 4:6, :]), scalar=col(nw, h), in1=F[:, par, :],
                                                  op0=ALU.mult, op1=ALU.mult))
                    for b in range(2):
                        dve.sem_inc(gram_free[b], 1)
                    link(dve.tensor_tensor(y_T[:, bass.ds(h, 1), :], F[:, par:par + 1, :], G[:, par:par + 1, :], ALU.mult))
                    dve.sem_inc(s["head_done"], 1)

                with dve.Fori(0, HEADS // 2) as i:
                    half(2 * i, 0)
                    half(2 * i + 1, 1)


def finish(nc, c, gain, out):
    norm(nc, c, gain, rows=out)


class Chip:
    pass


def trunk(nc, a, out):
    c = Chip()
    with ExitStack() as ctx:
        def sb(name, shape, dt=F32):
            return ctx.enter_context(nc.sbuf_tensor(name, shape, dt))

        c.ctx = ctx
        c.res = sb("residual", [P, TT, D])
        c.ident = sb("ident", [P, P])
        c.ones = sb("ones", [P, P])
        c.head_ones = sb("head_ones", [P, P])
        c.ps = ctx.enter_context(nc.psum_tensor("ps", [P, 8, HALF], F32))
        c.rows = nc.dram_tensor("h_rows", [S, D], F32).ap()
        c.row_tok = nc.dram_tensor("row_token", [(NBLK + 1) * P, 1], I32).ap()
        c.ys = nc.dram_tensor("expert_rows", [(NBLK + 1) * P, D], F32).ap()
        load_x(nc, c, a["x"])
        with nc.sbuf_tensor("proj", [P, AB_TILES, S], F32) as proj:
            with nc.sbuf_tensor("h_T", [P, KT, S], F32) as h_T:
                norm(nc, c, a["norm_mix"][0], h_T=h_T)
                project_ab(nc, c, a["ab_w_in"][0], a["rw_mu"][0], h_T, proj)
            lru(nc, c, a, proj)
            with ExitStack() as mix:
                def mb(name, shape):
                    return mix.enter_context(nc.sbuf_tensor(name, shape, F32))

                b = Chip()
                b.ln_w, b.ln_b = mb("ln_w", [P, NPAIR]), mb("ln_b", [P, NPAIR])
                b.step = mb("step", [P, NPAIR, NCH])
                b.g2 = mb("g2", [P, W_RW])
                b.bufs = [mb(f"mix{i}", [P, NPAIR, S]) for i in range(3)]
                with (nc.sbuf_tensor("mix3", [P, NPAIR, S], F32) as m3, nc.sbuf_tensor("mix4", [P, NPAIR, S], F32) as m4,
                      nc.sbuf_tensor("w2a2", [P, W_RW], F32) as b.w2a2):
                    b.bufs = [b.bufs[0], b.bufs[1], m3, b.bufs[2], m4]
                    rwkv_prepare(nc, c, a, proj, b)
                c.lower_1, c.upper, c.strict_incl = mb("lower_1", [P, HD]), mb("upper", [P, len(LEVELS), HD]), mb("strict_incl", [P, 2, HD])
                b.ident64 = mb("ident64", [P, HD])
                make_chunk_masks(nc, c, b)
                rwkv_chunks(nc, c, proj, b)
                rwkv_finish(nc, c, proj, b)
            project_out(nc, c, a["ab_w_out"][0], [proj[:, T_R:T_R + 4, :], proj[:, T_GATE:T_GATE + 4, :]])
        moe(nc, c, a, 0)
        with nc.sbuf_tensor("y_T", [P, KT, S], F32) as y_T:
            with nc.sbuf_tensor("h_T_1", [P, KT, S], F32) as h_T:
                norm(nc, c, a["norm_mix"][1], h_T=h_T)
                hgrn(nc, c, a["c_w_in"][0], a["c_lower_bound"], a["c_norm_w"][0], h_T, y_T)
            project_out(nc, c, a["c_w_out"][0], [y_T[:]])
        moe(nc, c, a, 1)
        finish(nc, c, a["norm_final"], out)


_INS = ["x", "norm_mix", "norm_ffn", "norm_final", "ab_w_in", "rw_mu", "rw_w0", "rw_w2", "rw_a0", "rw_a2", "rw_g2",
        "rw_k_k", "rw_k_a", "rw_r_k", "rw_ln_w", "rw_ln_b", "lru_conv_w", "lru_conv_b", "lru_w_a", "lru_b_a",
        "lru_w_x", "lru_b_x", "lru_lambda", "ab_w_out", "c_w_in", "c_lower_bound", "c_norm_w", "c_w_out",
        "moe_w_group", "moe_b_group", "moe_w_expert", "moe_b_expert", "moe_w_gate", "moe_w_up", "moe_w_down"]


def kernel(**inputs):
    import numpy as np
    import concourse.bacc as bacc
    from concourse.bass_utils import run_bass_kernel_spmd

    nc = bacc.Bacc("TRN2", target_bir_lowering=False, num_devices=1)
    arrays, aps = {}, {}
    for name in _INS:
        v = np.ascontiguousarray(inputs[name])
        if name == "x":
            v = v.reshape(S, D)
        arrays["in_" + name] = v
        aps[name] = nc.dram_tensor("in_" + name, v.shape, mybir.dt.from_np(v.dtype), kind="ExternalInput").ap()
    out = nc.dram_tensor("out_y", [S, D], F32, kind="ExternalOutput").ap()
    with nc.allow_non_contiguous_dma(reason="per-channel vectors of a few KB"):
        trunk(nc, aps, out)
    got = run_bass_kernel_spmd(nc, [arrays], core_ids=[0])
    return got.results[0]["out_y"].reshape(1, S, D)
```

```python
from contextlib import ExitStack, contextmanager

import concourse.bass as bass
from concourse import mybir

F32 = mybir.dt.float32
F32R = mybir.dt.float32r
I32 = mybir.dt.int32
U32 = mybir.dt.uint32
ALU = mybir.AluOpType
ACT = mybir.ActivationFunctionType
AX = mybir.AxisListType

P = 128
D = 1024
S = 1024
KT = D // P
TT = S // P
HALF = 512
NH = S // HALF
EPS = 1e-6

W_RW = D // 2
NPAIR = W_RW // P
HD = 64
GN_EPS = 64e-5
AB_COLS = 3 * W_RW + 64 + 64 + 128 + D
AB_TILES = AB_COLS // P
T_R, T_K, T_V, T_WA, T_G, T_GATE, T_XB = 0, 4, 8, 12, 13, 14, 18
NCH = S // HD
LEVELS = (1, 2, 4, 8, 16, 32)

HEADS = 8
HLEVELS = (64, 32, 16, 8, 4, 2, 1)

NG, EPG, NE, FF = 4, 8, 32, 512
NBLK = 2 * S // P + NE
BIG = 1.0e30


def take(eng, sem, n=1):
    eng.wait_ge(sem, n)
    eng.sem_inc(sem, -n)


class Chain:

    def __init__(self, eng, sem):
        self.eng, self.sem, self.n = eng, sem, 0

    def __call__(self, ins):
        self.n += 1
        ins.then_inc(self.sem, 1)
        self.eng.wait_ge(self.sem, self.n)


@contextmanager
def phase(nc, c):
    with ExitStack() as ctx:
        sems, tag = [], nc.next_id()

        def sem(name, by_pool_dma=False):
            if by_pool_dma:
                return c.ctx.enter_context(nc.semaphore(f"{name}_{tag}"))
            s = ctx.enter_context(nc.semaphore(name))
            sems.append(s)
            return s

        def sb(name, shape, dt=F32):
            return ctx.enter_context(nc.sbuf_tensor(f"{name}_{tag}", shape, dt))

        yield sem, sb
        with nc.Block() as block:

            @block.gpsimd
            def _(pool):
                for s in sems:
                    pool.sem_clear(s)


def bcast(ap, axis, n):
    ap = ap.unsqueeze(axis)
    shape = list(ap.shape)
    shape[axis] = n
    return ap.to_broadcast(shape)


def column(vec, lo=0, n=None):
    n = vec.shape[0] if n is None else n
    return vec[lo:lo + n].rearrange("(j p) -> p j", p=P)


def load_x(nc, c, x):
    with phase(nc, c) as (sem, sb):
        x_in, made = sem("x_in"), sem("made")
        with nc.Block() as block:

            @block.sync
            def _(sp):
                for t in range(TT):
                    sp.dma_start(c.res[:, t, :], x[t * P:(t + 1) * P, :]).then_inc(x_in, 16)
                sp.wait_ge(x_in, 16 * TT)

            @block.gpsimd
            def _(pool):
                ch = Chain(pool, made)
                ch(pool.memset(c.ident[:], 1.0))
                ch(pool.affine_select(out=c.ident[:], in_=c.ident[:], pattern=[[-1, P]], compare_op=ALU.is_equal,
                                      fill=0.0, base=0, channel_multiplier=1))
                ch(pool.memset(c.ones[:], 1.0))
                ch(pool.memset(c.head_ones[:], 0.0))
                for p in (0, HD):
                    ch(pool.memset(c.head_ones[p:p + HD, p:p + HD], 1.0))


def norm(nc, c, gain, h_T=None, rows=None):
    with phase(nc, c) as (sem, sb):
        gain_in, squared, var_ready, std_ready, hn_ready = (
            sem(n) for n in ("gain_in", "squared", "var_ready", "std_ready", "hn_ready"))
        turned, copied, stored, order = sem("turned"), sem("copied"), sem("stored"), sem("order")
        hn = sb("hn", [P, TT, D])
        gb = sb("gain_rows", [P, D])
        ss = sb("square_sums", [P, TT])
        var = sb("var", [P, TT])
        std = sb("std", [P, TT])
        rstd = sb("rstd", [P, TT])
        ps = c.ps
        with nc.Block() as block:

            @block.sync
            def _(sp):
                sp.dma_start(gb[:], gain.partition_broadcast(P)).then_inc(gain_in, 16)
                if rows is not None:
                    for t in range(TT):
                        sp.wait_ge(hn_ready, t + 1)
                        sp.dma_start(rows[t * P:(t + 1) * P, :], hn[:, t, :]).then_inc(stored, 16)
                    sp.wait_ge(stored, 16 * TT)

            @block.scalar
            def _(act):
                for t in range(TT):
                    act.activation(hn[:, t, :], c.res[:, t, :], ACT.Square, accum_out=ss[:, t:t + 1]).then_inc(squared, 1)
                act.wait_ge(var_ready, 1)
                act.activation(std[:], var[:], ACT.Sqrt).then_inc(std_ready, 1)
                if h_T is not None:
                    for t in range(TT):
                        for h in range(2):
                            act.wait_ge(turned, 2 * t + h + 1)
                            act.copy(h_T[:, 4 * h:4 * h + 4, t * P:(t + 1) * P],
                                     ps[:, 2 * (t % 2) + h, :].rearrange("p (k n) -> p k n", k=4)).then_inc(copied, 1)

            @block.vector
            def _(dve):
                ch = Chain(dve, order)
                dve.wait_ge(squared, TT)
                dve.tensor_scalar(var[:], ss[:], 1.0 / D, EPS, ALU.mult, ALU.add).then_inc(var_ready, 1)
                dve.wait_ge(std_ready, 1)
                ch(dve.reciprocal(rstd[:], std[:]))
                dve.wait_ge(gain_in, 16)
                for t in range(TT):
                    dve.scalar_tensor_tensor(out=hn[:, t, :], in0=c.res[:, t, :], scalar=rstd[:, t:t + 1], in1=gb[:],
                                             op0=ALU.mult, op1=ALU.mult).then_inc(hn_ready, 1)

            @block.tensor
            def _(pe):
                if h_T is None:
                    return
                for t in range(TT):
                    pe.wait_ge(hn_ready, t + 1)
                    for h in range(2):
                        if t >= 2:
                            pe.wait_ge(copied, 2 * (t - 2) + h + 1)
                        for k in range(4):
                            last = pe.transpose(ps[:, 2 * (t % 2) + h, k * P:(k + 1) * P],
                                                hn[:, t, (4 * h + k) * P:(4 * h + k + 1) * P], c.ident[:])
                        last.then_inc(turned, 1)


def project_ab(nc, c, w, mu, h_T, proj):
    w_t = w.rearrange("(k p) m -> p k m", p=P)
    with phase(nc, c) as (sem, sb):
        w_in = [sem("w_in0"), sem("w_in1")]
        w_free, summed = sem("w_free"), [sem("summed_a"), sem("summed_v")]
        bank_free = [sem("bank_free_a"), sem("bank_free_v")]
        order, order_a, first_copied, mu_in = sem("order"), sem("order_a"), sem("first_copied"), sem("mu_in")
        wt = sb("w_tiles", [P, 2, KT, P])
        mu_t = sb("mu", [P, AB_TILES])
        shift = sb("shift", [P, 1, S])
        ps = c.ps
        cleared, zero_made = sem("cleared", True), sem("zero_made")
        zero = sb("zero_rows", [P, D])
        with nc.Block() as block:

            @block.gpsimd
            def _(pool):
                pool.memset(zero[:], 0.0).then_inc(zero_made, 1)
                pool.wait_ge(zero_made, 1)
                for n in range(NBLK + 1):
                    pool.dma_start(c.ys[n * P:(n + 1) * P, :], zero[:]).then_inc(cleared, 16)
                pool.wait_ge(cleared, 16 * (NBLK + 1))

            @block.sync
            def _(sp):
                sp.dma_start(mu_t[:, 0:T_GATE], column(mu)).then_inc(mu_in, 16)
                with sp.Fori(0, AB_TILES // 2) as i:
                    for q in range(2):
                        take(sp, w_free)
                        sp.dma_start(wt[:, q], w_t[:, :, bass.ds(i * (2 * P) + q * P, P)]).then_inc(w_in[q], 16)

            @block.tensor
            def _(pe):
                pe.sem_inc(w_free, 2)
                with pe.Fori(0, AB_TILES // 2):
                    for q in range(2):
                        take(pe, w_in[q], 16)
                        for h in range(NH):
                            take(pe, bank_free[h])
                            for k in range(KT):
                                last = pe.matmul(ps[:, 2 * q + h, :], wt[:, q, k, :], h_T[:, k, h * HALF:(h + 1) * HALF],
                                                 start=k == 0, stop=k == KT - 1)
                            last.then_inc(summed[h], 1)
                        pe.drain().then_inc(w_free, 1)

            @block.scalar
            def _(act):
                act.sem_inc(bank_free[0], 2)
                with act.Fori(0, AB_TILES // 2) as i:
                    for q in range(2):
                        take(act, summed[0])
                        act.copy(proj[:, bass.ds(2 * i + q, 1), 0:HALF], ps[:, 2 * q:2 * q + 1, :]).then_inc(order_a, 1)
                        take(act, order_a)
                        act.sem_inc(bank_free[0], 1)
                        act.sem_inc(first_copied, 1)

            @block.vector
            def _(dve):
                def link(ins):
                    ins.then_inc(order, 1)
                    take(dve, order)

                link(dve.memset(mu_t[:, T_GATE:AB_TILES], 0.0))
                dve.wait_ge(mu_in, 16)
                dve.sem_inc(bank_free[1], 2)
                with dve.Fori(0, AB_TILES // 2) as i:
                    for q in range(2):
                        take(dve, summed[1])
                        m = bass.ds(2 * i + q, 1)
                        dve.tensor_copy(proj[:, m, HALF:S], ps[:, 2 * q + 1:2 * q + 2, :]).then_inc(order, 1)
                        take(dve, order)
                        dve.sem_inc(bank_free[1], 1)
                        take(dve, first_copied)
                        link(dve.tensor_tensor(shift[:, :, 1:S], proj[:, m, 0:S - 1], proj[:, m, 1:S], ALU.subtract))
                        link(dve.tensor_scalar(shift[:, :, 0:1], proj[:, m, 0:1], -1.0, None, ALU.mult))
                        link(dve.scalar_tensor_tensor(out=proj[:, m, :], in0=shift[:], scalar=mu_t[:, m], in1=proj[:, m, :],
                                                      op0=ALU.mult, op1=ALU.add))


def lru(nc, c, a, proj):
    gate, xb = proj[:, T_GATE:T_GATE + 4, :], proj[:, T_XB:T_XB + 4, :]
    w_a = a["lru_w_a"][0].rearrange("(j p) d e -> (p d) j e", p=2)
    w_x = a["lru_w_x"][0].rearrange("(j p) d e -> (p d) j e", p=2)
    with phase(nc, c) as (sem, sb):
        names = ("par_in", "order", "exp_lam", "lam_ready", "conv_done", "gates_summed", "gates_done", "i_done",
                 "decay_done", "tanh_done", "power_ready", "root_done", "gelu_done", "bank_free")
        s = {n: sem(n) for n in names}
        wa, wx = sb("lru_wa", [P, 4, HD]), sb("lru_wx", [P, 4, HD])
        cw, cb = sb("conv_w", [P, 4, 4]), sb("conv_b", [P, 4])
        ba, bx, lam = sb("b_a", [P, 4]), sb("b_x", [P, 4]), sb("lam", [P, 4])
        neg, y, z, z2, ser, rate, nrate = (sb(n, [P, 4]) for n in ("lam_neg", "lam_y", "lam_z", "lam_z2", "lam_ser", "rate", "nrate"))
        xc, rr, ii, dec = (sb(n, [P, 4, S]) for n in ("conv", "r_gate", "i_gate", "decay"))
        ps = c.ps
        with nc.Block() as block:

            @block.sync
            def _(sp):
                sp.dma_start(wa[:], w_a).then_inc(s["par_in"], 16)
                sp.dma_start(wx[:], w_x).then_inc(s["par_in"], 16)
                for i in range(4):
                    sp.dma_start(cw[:, i, :], column(a["lru_conv_w"][0, i])).then_inc(s["par_in"], 16)
                for t, v in ((cb, "lru_conv_b"), (ba, "lru_b_a"), (bx, "lru_b_x"), (lam, "lru_lambda")):
                    sp.dma_start(t[:], column(a[v][0])).then_inc(s["par_in"], 16)
                sp.wait_ge(s["par_in"], 160)

            @block.vector
            def _(dve):
                ch = Chain(dve, s["order"])
                dve.wait_ge(s["par_in"], 160)
                ch(dve.tensor_scalar(neg[:], lam[:], -1.0, None, ALU.mult))
                dve.tensor_tensor(z[:], lam[:], neg[:], ALU.max).then_inc(s["lam_ready"], 1)
                dve.wait_ge(s["exp_lam"], 1)
                ch(dve.tensor_scalar(z[:], y[:], 2.0, None, ALU.add))
                ch(dve.reciprocal(z2[:], z[:]))
                ch(dve.tensor_tensor(z[:], y[:], z2[:], ALU.mult))
                ch(dve.tensor_tensor(z2[:], z[:], z[:], ALU.mult))
                ch(dve.tensor_scalar(ser[:], z2[:], 1.0 / 17, None, ALU.mult))
                for k in range(7, 0, -1):
                    ch(dve.scalar_tensor_tensor(out=ser[:], in0=ser[:], scalar=1.0 / (2 * k + 1), in1=z2[:],
                                                op0=ALU.add, op1=ALU.mult))
                ch(dve.scalar_tensor_tensor(out=ser[:], in0=ser[:], scalar=1.0, in1=z[:], op0=ALU.add, op1=ALU.mult))
                ch(dve.tensor_scalar(neg[:], neg[:], 0.0, None, ALU.max))
                ch(dve.scalar_tensor_tensor(out=ser[:], in0=ser[:], scalar=2.0, in1=neg[:], op0=ALU.mult, op1=ALU.add))
                ch(dve.tensor_scalar(rate[:], ser[:], -8.0, None, ALU.mult))
                dve.tensor_scalar(nrate[:], ser[:], 8.0, None, ALU.mult).then_inc(s["lam_ready"], 1)
                for j in range(4):
                    ch(dve.tensor_scalar(xc[:, j, :], xb[:, j, :], cw[:, 3, j:j + 1], cb[:, j:j + 1], ALU.mult, ALU.add))
                for d in range(1, 4):
                    for j in range(4):
                        ins = dve.scalar_tensor_tensor(out=xc[:, j, d:S], in0=xb[:, j, 0:S - d], scalar=cw[:, 3 - d, j:j + 1],
                                                       in1=xc[:, j, d:S], op0=ALU.mult, op1=ALU.add)
                        if d < 3:
                            ch(ins)
                        else:
                            ins.then_inc(s["conv_done"], 1)
                for j in range(4):
                    dve.wait_ge(s["tanh_done"], j + 1)
                    ch(dve.tensor_scalar(xb[:, j, :], rr[:, j, :], 1.0, None, ALU.add))
                    ch(dve.reciprocal(xb[:, j, :], xb[:, j, :]))
                    dve.scalar_tensor_tensor(out=rr[:, j, :], in0=rr[:, j, :], scalar=2.0, in1=xb[:, j, :],
                                             op0=ALU.mult, op1=ALU.mult).then_inc(s["power_ready"], 1)
                for j in range(4):
                    dve.wait_ge(s["i_done"], j + 1)
                    ch(dve.tensor_tensor(ii[:, j, :], ii[:, j, :], xc[:, j, :], ALU.mult))
                for j in range(4):
                    dve.wait_ge(s["root_done"], j + 1)
                    ch(dve.tensor_tensor(ii[:, j, :], ii[:, j, :], rr[:, j, :], ALU.mult))
                    ch(dve.tensor_tensor_scan(xc[:, j, :], dec[:, j, :], ii[:, j, :], 0.0, ALU.mult, ALU.add))
                    dve.wait_ge(s["gelu_done"], j + 1)
                    ch(dve.tensor_tensor(gate[:, j, :], gate[:, j, :], xc[:, j, :], ALU.mult))

            @block.tensor
            def _(pe):
                pe.wait_ge(s["par_in"], 160)
                for j in range(4):
                    pe.wait_ge(s["conv_done"], j + 1)
                    if j >= 2:
                        pe.wait_ge(s["gates_done"], j - 1)
                        pe.wait_ge(s["i_done"], j - 1)
                    for g, w in ((0, wa), (1, wx)):
                        for h in range(NH):
                            for p in (0, HD):
                                last = pe.matmul(ps[p:p + HD, 4 * (j % 2) + 2 * g + h, :], w[p:p + HD, j, :],
                                                 xc[p:p + HD, j, h * HALF:(h + 1) * HALF], start=True, stop=True)
                    last.then_inc(s["gates_summed"], 1)

            @block.scalar
            def _(act):
                act.wait_ge(s["lam_ready"], 1)
                act.activation(y[:], z[:], ACT.Exp, scale=-1.0).then_inc(s["exp_lam"], 1)
                for j in range(4):
                    act.wait_ge(s["gates_summed"], j + 1)
                    b = 4 * (j % 2)
                    act.activation(rr[:, j, :], ps[:, b:b + 2, :].rearrange("p h n -> p (h n)"), ACT.Sigmoid,
                                   bias=ba[:, j:j + 1]).then_inc(s["gates_done"], 1)
                    act.activation(ii[:, j, :], ps[:, b + 2:b + 4, :].rearrange("p h n -> p (h n)"), ACT.Sigmoid,
                                   bias=bx[:, j:j + 1]).then_inc(s["i_done"], 1)
                act.wait_ge(s["lam_ready"], 2)
                for j in range(4):
                    act.wait_ge(s["gates_done"], j + 1)
                    act.activation(dec[:, j, :], rr[:, j, :], ACT.Exp, scale=rate[:, j:j + 1]).then_inc(s["decay_done"], 1)
                for j in range(4):
                    act.wait_ge(s["decay_done"], j + 1)
                    act.activation(rr[:, j, :], rr[:, j, :], ACT.Tanh, scale=nrate[:, j:j + 1]).then_inc(s["tanh_done"], 1)
                for j in range(4):
                    act.activation(gate[:, j, :], gate[:, j, :], ACT.Gelu_apprx_tanh).then_inc(s["gelu_done"], 1)
                for j in range(4):
                    act.wait_ge(s["power_ready"], j + 1)
                    act.activation(rr[:, j, :], rr[:, j, :], ACT.Sqrt).then_inc(s["root_done"], 1)


def rwkv_prepare(nc, c, a, proj, b):
    r, k, v = (proj[:, t:t + 4, :] for t in (T_R, T_K, T_V))
    kk = proj[:, T_XB:T_XB + 4, :]
    B0, B1, B2, B3, B4 = b.bufs
    flat = lambda t: t.rearrange("p j s -> p (j s)")
    chunked = lambda t: t.rearrange("p j (n q) -> p (j n) q", q=HD)
    with phase(nc, c) as (sem, sb):
        names = ("par_in", "order", "order_a", "tanh_done", "z_summed", "z_done", "a_summed", "a_done", "cum_ready",
                 "kk_ready", "kk_squared", "kk_summed", "kk_max", "kk_root", "bonus_in", "bonus_summed",
                 "exp_done", "mask_made", "step_ready", "step_done")
        s = {n: sem(n) for n in names}
        w2, a2, g2 = b.w2a2, b.w2a2, b.g2
        th = proj[:, T_WA, :]
        reset = B4[:, 0, :]
        w0, a0, k_k, k_a, r_k, k_a1 = (sb(n, [P, 4]) for n in ("w0", "a0", "k_k", "k_a", "r_k", "one_minus_k_a"))
        mid, end, tmp = (sb(n, [P, 4, NCH]) for n in ("cum_mid", "cum_end", "step_log"))
        ps = c.ps

        with nc.Block() as block:

            @block.sync
            def _(sp):
                sp.dma_start(w2[0:HD, :], a["rw_w2"][0]).then_inc(s["par_in"], 16)
                sp.dma_start(a2[HD:P, :], a["rw_a2"][0]).then_inc(s["par_in"], 16)
                sp.dma_start(g2[:], a["rw_g2"][0]).then_inc(s["par_in"], 16)
                for t, n in ((w0, "rw_w0"), (a0, "rw_a0"), (k_k, "rw_k_k"), (k_a, "rw_k_a"), (b.ln_w, "rw_ln_w"), (b.ln_b, "rw_ln_b")):
                    sp.dma_start(t[:], column(a[n][0])).then_inc(s["par_in"], 16)
                sp.dma_start(r_k[:], a["rw_r_k"][0].rearrange("(j h) n -> (h n) j", h=2)).then_inc(s["par_in"], 16)
                sp.wait_ge(s["par_in"], 160)

            @block.gpsimd
            def _(pool):
                ch = Chain(pool, s["mask_made"])
                ch(pool.memset(reset, 1.0))
                ch(pool.memset(reset.rearrange("p (n q) -> p n q", q=HD)[:, :, 0:1], 0.0))

            @block.scalar
            def _(act):
                ch = Chain(act, s["order_a"])
                act.wait_ge(s["par_in"], 160)
                act.activation(th[0:HD, :], proj[0:HD, T_WA, :], ACT.Tanh).then_inc(s["tanh_done"], 1)
                ch(act.activation(proj[:, T_G, :], proj[:, T_G, :], ACT.Sigmoid))
                for j in range(4):
                    q = j % 2
                    act.wait_ge(s["z_summed"], j + 1)
                    act.activation(B0[:, j, :], ps[:, 2 * q:2 * q + 2, :].rearrange("p h n -> p (h n)"), ACT.Sigmoid,
                                   bias=w0[:, j:j + 1]).then_inc(s["z_done"], 1)
                    act.wait_ge(s["a_summed"], j + 1)
                    act.activation(B1[:, j, :], ps[:, 4 + 2 * q:6 + 2 * q, :].rearrange("p h n -> p (h n)"), ACT.Sigmoid,
                                   bias=a0[:, j:j + 1]).then_inc(s["a_done"], 1)
                act.wait_ge(s["kk_ready"], 1)
                act.activation(flat(B3[:]), flat(kk), ACT.Square).then_inc(s["kk_squared"], 1)
                act.wait_ge(s["kk_max"], 1)
                act.activation(flat(B3[:]), flat(B3[:]), ACT.Sqrt).then_inc(s["kk_root"], 1)
                act.wait_ge(s["step_ready"], 1)
                act.activation(b.step[:].rearrange("p j n -> p (j n)"), tmp[:].rearrange("p j n -> p (j n)"), ACT.Exp).then_inc(s["step_done"], 1)
                act.wait_ge(s["cum_ready"], 2)
                act.activation(flat(B4[:]), flat(B2[:]), ACT.Exp, scale=-1.0).then_inc(s["exp_done"], 1)
                act.activation(flat(B3[:]), flat(B3[:]), ACT.Exp).then_inc(s["exp_done"], 1)
                act.wait_ge(s["exp_done"], 1)
                act.activation(flat(B2[:]), flat(B2[:]), ACT.Exp).then_inc(s["exp_done"], 1)
                act.wait_ge(s["step_done"], 1)

            @block.tensor
            def _(pe):
                pe.wait_ge(s["par_in"], 160)
                pe.wait_ge(s["tanh_done"], 1)
                for j in range(4):
                    q = j % 2
                    if j >= 2:
                        pe.wait_ge(s["z_done"], j - 1)
                        pe.wait_ge(s["a_done"], j - 1)
                    for h in range(NH):
                        last = pe.matmul(ps[:, 2 * q + h, :], w2[0:HD, j * P:(j + 1) * P], th[0:HD, h * HALF:(h + 1) * HALF],
                                         start=True, stop=True)
                    last.then_inc(s["z_summed"], 1)
                    for h in range(NH):
                        last = pe.matmul(ps[:, 4 + 2 * q + h, :], a2[HD:P, j * P:(j + 1) * P],
                                         proj[HD:P, T_WA, h * HALF:(h + 1) * HALF], start=True, stop=True)
                    last.then_inc(s["a_summed"], 1)
                pe.wait_ge(s["kk_squared"], 1)
                pe.wait_ge(s["z_done"], 4)
                pe.wait_ge(s["a_done"], 4)
                for j in range(4):
                    for h in range(NH):
                        last = pe.matmul(ps[:, 2 * j + h, :], c.head_ones[:], B3[:, j, h * HALF:(h + 1) * HALF], start=True, stop=True)
                last.then_inc(s["kk_summed"], 1)
                pe.wait_ge(s["bonus_in"], 1)
                for j in range(4):
                    for h in range(NH):
                        last = pe.matmul(ps[:, 2 * j + h, :], c.head_ones[:], B0[:, j, h * HALF:(h + 1) * HALF], start=True, stop=True)
                last.then_inc(s["bonus_summed"], 1)

            @block.vector
            def _(dve):
                ch = Chain(dve, s["order"])
                dve.wait_ge(s["par_in"], 160)
                ch(dve.tensor_scalar(k_a1[:], k_a[:], -1.0, 1.0, ALU.mult, ALU.add))
                for j in range(4):
                    ch(dve.tensor_scalar(kk[:, j, :], k[:, j, :], k_k[:, j:j + 1], None, ALU.mult))
                dve.sem_inc(s["kk_ready"], 1)
                dve.wait_ge(s["z_done"], 4)
                ch(dve.tensor_scalar(flat(B0[:]), flat(B0[:]), -0.6065306597126334, None, ALU.mult))
                dve.wait_ge(s["mask_made"], 2)
                for j in range(4):
                    ch(dve.tensor_tensor_scan(B2[:, j, :], reset, B0[:, j, :], 0.0, ALU.mult, ALU.add))
                cum = B2[:].rearrange("p j (n q) -> p j n q", q=HD)
                ch(dve.tensor_copy(mid[:], cum[:, :, :, HD // 2 - 1]))
                ch(dve.tensor_copy(end[:], cum[:, :, :, HD - 1]))
                ch(dve.tensor_tensor(tmp[:], end[:], mid[:], ALU.subtract))
                dve.tensor_tensor(tmp[:, :, 0:NCH - 1], tmp[:, :, 0:NCH - 1], mid[:, :, 1:NCH], ALU.add).then_inc(s["step_ready"], 1)
                ch(dve.tensor_tensor(chunked(B2[:]), chunked(B2[:]),
                                     bcast(mid[:].rearrange("p j n -> p (j n)"), 2, HD), ALU.subtract))
                dve.wait_ge(s["kk_summed"], 1)
                dve.tensor_scalar(flat(B3[:]), ps[:].rearrange("p b n -> p (b n)"), 1e-24, None, ALU.max).then_inc(s["kk_max"], 1)
                dve.wait_ge(s["kk_root"], 1)
                ch(dve.reciprocal(flat(B3[:]), flat(B3[:])))
                ch(dve.tensor_tensor(flat(kk), flat(kk), flat(B3[:]), ALU.mult))
                dve.tensor_tensor(flat(B3[:]), flat(B2[:]), flat(B0[:]), ALU.subtract).then_inc(s["cum_ready"], 2)
                dve.wait_ge(s["a_done"], 4)
                dve.wait_ge(s["cum_ready"], 2)
                for j in range(4):
                    ch(dve.tensor_scalar(B0[:, j, :], B1[:, j, :], k_a[:, j:j + 1], k_a1[:, j:j + 1], ALU.mult, ALU.add))
                ch(dve.tensor_tensor(flat(k), flat(k), flat(B0[:]), ALU.mult))
                for j in range(4):
                    ch(dve.scalar_tensor_tensor(out=B0[:, j, :], in0=r[:, j, :], scalar=r_k[:, j:j + 1], in1=k[:, j, :],
                                                op0=ALU.mult, op1=ALU.mult))
                dve.sem_inc(s["bonus_in"], 1)
                ch(dve.tensor_tensor(flat(B1[:]), flat(B1[:]), flat(kk), ALU.mult))
                dve.wait_ge(s["exp_done"], 3)
                ch(dve.tensor_tensor(flat(B1[:]), flat(B1[:]), flat(B4[:]), ALU.mult))
                ch(dve.scalar_tensor_tensor(out=flat(B3[:]), in0=flat(kk), scalar=-1.0, in1=flat(B3[:]), op0=ALU.mult, op1=ALU.mult))
                ch(dve.tensor_tensor(flat(r), flat(r), flat(B2[:]), ALU.mult))
                ch(dve.tensor_tensor(flat(k), flat(k), flat(B4[:]), ALU.mult))
                dve.wait_ge(s["bonus_summed"], 1)
                ch(dve.tensor_tensor(flat(B0[:]), ps[:].rearrange("p b n -> p (b n)"), flat(v), ALU.mult))


def make_chunk_masks(nc, c, b):
    with phase(nc, c) as (sem, sb):
        made = sem("masks_made")
        with nc.Block() as block:

            @block.gpsimd
            def _(pool):
                ch = Chain(pool, made)
                for p in (0, HD):
                    ch(pool.tensor_copy(b.ident64[p:p + HD, :], c.ident[p:p + HD, p:p + HD]))
                ch(pool.memset(c.lower_1[:], 1.0))
                ch(pool.memset(c.upper[:], 1.0))
                ch(pool.memset(c.strict_incl[:], 1.0))
                for p in (0, HD):
                    def keep(view, pattern, base, mult=0):
                        ch(pool.affine_select(out=view, in_=view, pattern=pattern, compare_op=ALU.is_ge, fill=0.0,
                                              base=base, channel_multiplier=mult))
                    low = c.lower_1[p:p + HD, :].rearrange("p (n h) -> p n h", h=2)
                    keep(low, [[-2, 32], [-1000, 2]], -1, 1)
                    keep(low, [[2, 32], [0, 2]], 1, -1)
                    for i, w in enumerate(LEVELS):
                        up = c.upper[p:p + HD, i, :].rearrange("p (n h q) -> p n h q", h=2, q=w)
                        keep(up, [[-2 * w, HD // (2 * w)], [1000, 2], [0, w]], -1000, 1)
                        keep(up, [[2 * w, HD // (2 * w)], [0, 2], [0, w]], w - 1, -1)
                    keep(c.strict_incl[p:p + HD, 0, :], [[1, HD]], -1, -1)
                    keep(c.strict_incl[p:p + HD, 1, :], [[1, HD]], 0, -1)


def rwkv_chunks(nc, c, proj, b):
    r, k, v = (proj[:, t:t + 4, :] for t in (T_R, T_K, T_V))
    ab, bb = b.bufs[3], b.bufs[1]
    y = r
    NI = 2 * NPAIR
    with phase(nc, c) as (sem, sb):
        names = ("staged", "stage_free", "gram_done", "turned_done", "order", "order_a", "masked", "tok_ready", "x_first",
                 "t1_done", "t1_copied", "dx_done", "x_next", "u_done", "u_copied", "sa_done", "sa_copied", "ds_done",
                 "s_ready", "y_done", "y_copied", "turn_end_a", "turn_end_v")
        s = {n: sem(n) for n in names}
        AR = sb("stage_ar", [P, 2, NPAIR, 2, HD])
        BS, KS, VS = (sb(n, [P, 2, NPAIR, HD]) for n in ("stage_b", "stage_k", "stage_v"))
        tok = sb("row_major", [P, 3, NI, HD])
        MK = proj[:, T_XB + 3, :].rearrange("p (m i n) -> p m i n", m=2, i=NI)
        RB = sb("masked_rb", [P, NI, HD])
        LO = proj[:, T_XB:T_XB + 3, :].rearrange("p t s -> p (t s)")[:, 0:5 * NI * HD].rearrange("p (v i n) -> p v i n", v=5, i=NI)
        X, XT, T1 = (sb(n, [P, NI, HD]) for n in ("x_inv", "x_inv_t", "t1"))
        U, SA = (sb(n, [P, 2, NPAIR, HD]) for n in ("u_rows", "sa_rows"))
        SS = sb("state", [P, 2, NPAIR, HD])
        sn = sb("state_sum", [P, NPAIR, HD])
        ps = c.ps
        eye = [c.ident[p:p + HD, p:p + HD] for p in (0, HD)]
        items = [(ci, j) for ci in range(2) for j in range(NPAIR)]
        lt_rb = ps[:, 0:2, :].rearrange("p k (i m n) -> p (k i) m n", m=2, n=HD)
        mt_rk = ps[:, 2:4, :].rearrange("p k (i m n) -> p (k i) m n", m=2, n=HD)
        low = ps[:, 4, :].rearrange("p (i n) -> p i n", n=HD)
        eye_b = [None]

        def halves():
            return ((0, slice(0, HD)), (1, slice(HD, P)))

        with nc.Block() as block:

            @block.scalar
            def _(act):
                def link(ins):
                    ins.then_inc(s["order_a"], 1)
                    take(act, s["order_a"])

                with act.Fori(0, NCH // 2) as i:
                    for src, dst in ((ab, AR[:, :, :, 0, :]), (r, AR[:, :, :, 1, :])):
                        for ci in range(2):
                            link(act.copy(dst[:, ci], src[:, :, bass.ds(i * P + ci * HD, HD)]))
                    for src, dst in ((bb, BS), (k, KS), (v, VS)):
                        for ci in range(2):
                            link(act.copy(dst[:, ci], src[:, :, bass.ds(i * P + ci * HD, HD)]))
                    act.sem_inc(s["staged"], 1)
                    take(act, s["turned_done"])
                    for m in range(3):
                        link(act.copy(tok[:, m].rearrange("p i n -> p (i n)"), ps[:, 5 + m, :]))
                    act.sem_inc(s["tok_ready"], 1)
                    for lv in range(5):
                        take(act, s["t1_done"])
                        act.copy(T1[:].rearrange("p i n -> p (i n)"), ps[:, 0, :]).then_inc(s["t1_copied"], 1)
                    for ci in range(2):
                        take(act, s["u_done"])
                        act.copy(U[:, ci].rearrange("p j n -> p (j n)"), ps[:, 3, 0:NPAIR * HD]).then_inc(s["u_copied"], 1)
                        take(act, s["sa_done"])
                        act.copy(SA[:, ci].rearrange("p j n -> p (j n)"), ps[:, 4, 0:NPAIR * HD]).then_inc(s["sa_copied"], 1)
                        take(act, s["y_done"])
                        link(act.copy(y[:, :, bass.ds(i * P + ci * HD, HD)], ps[:, 6 + ci, 0:NPAIR * HD].rearrange("p (j n) -> p j n", j=NPAIR)))
                    act.sem_inc(s["turn_end_a"], 1)

            @block.tensor
            def _(pe):
                pe.sem_inc(s["turn_end_v"], 1)
                pe.sem_inc(s["turn_end_a"], 1)
                with pe.Fori(0, NCH // 2):
                    take(pe, s["staged"])
                    take(pe, s["turn_end_a"])
                    take(pe, s["turn_end_v"])
                    for m, src in enumerate((VS, BS, KS)):
                        for n, (ci, j) in enumerate(items):
                            for h, q in halves():
                                last = pe.matmul(ps[q, 5 + m, n * HD:(n + 1) * HD], src[q, ci, j, :], eye[h], start=True, stop=True)
                    last.then_inc(s["turned_done"], 1)
                    for n, (ci, j) in enumerate(items):
                        for h, q in halves():
                            pe.matmul(lt_rb[q, n].rearrange("p m n -> p (m n)"), BS[q, ci, j, :],
                                      AR[q, ci, j].rearrange("p m n -> p (m n)"), start=True, stop=True)
                            pe.matmul(mt_rk[q, n].rearrange("p m n -> p (m n)"), KS[q, ci, j, :],
                                      AR[q, ci, j].rearrange("p m n -> p (m n)"), start=True, stop=True)
                            last = pe.matmul(low[q, n], AR[q, ci, j, 0, :], BS[q, ci, j, :], start=True, stop=True)
                    last.then_inc(s["gram_done"], 1)
                    take(pe, s["x_first"])
                    for lv in range(5):
                        if lv:
                            take(pe, s["x_next"])
                        for n in range(NI):
                            for h, q in halves():
                                last = pe.matmul(ps[q, 0, n * HD:(n + 1) * HD], LO[q, lv, n, :], X[q, n, :], start=True, stop=True)
                        last.then_inc(s["t1_done"], 1)
                        take(pe, s["t1_copied"])
                        for n in range(NI):
                            for h, q in halves():
                                if lv < 4:
                                    pe.matmul(ps[q, 1, n * HD:(n + 1) * HD], XT[q, n, :], T1[q, n, :], start=True, stop=True)
                                last = pe.matmul(ps[q, 2, n * HD:(n + 1) * HD], T1[q, n, :], XT[q, n, :], start=True, stop=True)
                        last.then_inc(s["dx_done"], 1)
                    take(pe, s["x_next"])
                    take(pe, s["tok_ready"])
                    for ci in range(2):
                        take(pe, s["s_ready"])
                        for j in range(NPAIR):
                            n = ci * NPAIR + j
                            for h, q in halves():
                                pe.matmul(ps[q, 3, j * HD:(j + 1) * HD], MK[q, 0, n, :], tok[q, 0, n, :], start=True, stop=False)
                                last = pe.matmul(ps[q, 3, j * HD:(j + 1) * HD], AR[q, ci, j, 0, :], SS[q, ci, j, :], start=False, stop=True)
                        last.then_inc(s["u_done"], 1)
                        take(pe, s["u_copied"])
                        for j in range(NPAIR):
                            n = ci * NPAIR + j
                            for h, q in halves():
                                last = pe.matmul(ps[q, 4, j * HD:(j + 1) * HD], XT[q, n, :], U[q, ci, j, :], start=True, stop=True)
                        last.then_inc(s["sa_done"], 1)
                        take(pe, s["sa_copied"])
                        for j in range(NPAIR):
                            n = ci * NPAIR + j
                            for h, q in halves():
                                pe.matmul(ps[q, 5, j * HD:(j + 1) * HD], tok[q, 1, n, :], SA[q, ci, j, :], start=True, stop=False)
                                last = pe.matmul(ps[q, 5, j * HD:(j + 1) * HD], tok[q, 2, n, :], tok[q, 0, n, :], start=False, stop=True)
                        last.then_inc(s["ds_done"], 1)
                        for j in range(NPAIR):
                            n = ci * NPAIR + j
                            for h, q in halves():
                                o = ps[q, 6 + ci, j * HD:(j + 1) * HD]
                                pe.matmul(o, SS[q, ci, j, :], AR[q, ci, j, 1, :], start=True, stop=False)
                                pe.matmul(o, SA[q, ci, j, :], RB[q, n, :], start=False, stop=False)
                                last = pe.matmul(o, tok[q, 0, n, :], MK[q, 1, n, :], start=False, stop=True)
                        last.then_inc(s["y_done"], 1)

            @block.vector
            def _(dve):
                def link(ins):
                    ins.then_inc(s["order"], 1)
                    take(dve, s["order"])

                link(dve.memset(SS[:, 0], 0.0))
                dve.sem_inc(s["s_ready"], 1)
                ident64 = b.ident64
                up = lambda lv: bcast(c.upper[:, lv, :], 1, NI)
                with dve.Fori(0, NCH // 2) as i:
                    take(dve, s["gram_done"])
                    link(dve.tensor_tensor(X[:], low, bcast(c.lower_1[:], 1, NI), ALU.mult))
                    link(dve.tensor_tensor(X[:], X[:], bcast(ident64[:], 1, NI), ALU.add))
                    link(dve.tensor_tensor(XT[:], lt_rb[:, :, 0, :], up(0), ALU.mult))
                    link(dve.tensor_tensor(XT[:], XT[:], bcast(ident64[:], 1, NI), ALU.add))
                    for lv in range(5):
                        link(dve.tensor_tensor(LO[:, lv], lt_rb[:, :, 0, :], up(lv + 1), ALU.mult))
                    link(dve.tensor_tensor(RB[:], lt_rb[:, :, 1, :], bcast(c.strict_incl[:, 1, :], 1, NI), ALU.mult))
                    for m in range(2):
                        link(dve.tensor_tensor(MK[:, m], mt_rk[:, :, m, :], bcast(c.strict_incl[:, m, :], 1, NI), ALU.mult))
                    dve.sem_inc(s["x_first"], 1)
                    for lv in range(5):
                        take(dve, s["dx_done"])
                        fl = lambda t: t[:].rearrange("p i n -> p (i n)")
                        if lv < 4:
                            link(dve.tensor_tensor(fl(X), fl(X), ps[:, 1, :], ALU.add))
                        dve.tensor_tensor(fl(XT), fl(XT), ps[:, 2, :], ALU.add).then_inc(s["x_next"], 1)
                    for ci in range(2):
                        take(dve, s["ds_done"])
                        link(dve.tensor_tensor(sn[:], SS[:, ci], ps[:, 5, 0:NPAIR * HD].rearrange("p (j n) -> p j n", j=NPAIR), ALU.add))
                        stepc = b.step[:, :, bass.ds(2 * i + ci, 1)].to_broadcast([P, NPAIR, HD])
                        dve.tensor_tensor(SS[:, 1 - ci], sn[:], stepc, ALU.mult).then_inc(s["s_ready"], 1)
                    dve.sem_inc(s["turn_end_v"], 1)


def rwkv_finish(nc, c, proj, b):
    B0, y = b.bufs[0], proj[:, T_R:T_R + 4, :]
    yc = y
    flat = lambda t: t.rearrange("p j s -> p (j s)")
    with phase(nc, c) as (sem, sb):
        names = ("order", "mean_summed", "centred", "squared", "var_summed", "var_ready", "root_done", "g_summed", "banks_read")
        s = {n: sem(n) for n in names}
        B4 = sb("squares", [P, NPAIR, S])
        ps = c.ps
        psf = ps[:].rearrange("p b n -> p (b n)")
        with nc.Block() as block:

            @block.tensor
            def _(pe):
                for j in range(4):
                    for h in range(NH):
                        last = pe.matmul(ps[:, 2 * j + h, :], c.head_ones[:], y[:, j, h * HALF:(h + 1) * HALF], start=True, stop=True)
                last.then_inc(s["mean_summed"], 1)
                pe.wait_ge(s["squared"], 1)
                for j in range(4):
                    for h in range(NH):
                        last = pe.matmul(ps[:, 2 * j + h, :], c.head_ones[:], B4[:, j, h * HALF:(h + 1) * HALF], start=True, stop=True)
                last.then_inc(s["var_summed"], 1)
                pe.wait_ge(s["var_ready"], 1)
                for j in range(4):
                    for h in range(NH):
                        last = pe.matmul(ps[:, 2 * j + h, :], b.g2[:, j * P:(j + 1) * P], proj[:, T_G, h * HALF:(h + 1) * HALF],
                                         start=True, stop=True)
                last.then_inc(s["g_summed"], 1)

            @block.scalar
            def _(act):
                act.wait_ge(s["centred"], 1)
                act.activation(flat(B4[:]), flat(yc), ACT.Square).then_inc(s["squared"], 1)
                act.wait_ge(s["var_ready"], 1)
                act.activation(flat(B4[:]), flat(B4[:]), ACT.Sqrt).then_inc(s["root_done"], 1)

            @block.vector
            def _(dve):
                ch = Chain(dve, s["order"])
                dve.wait_ge(s["mean_summed"], 1)
                dve.scalar_tensor_tensor(out=flat(yc), in0=psf, scalar=-1.0 / HD, in1=flat(y), op0=ALU.mult,
                                         op1=ALU.add).then_inc(s["centred"], 1)
                dve.wait_ge(s["var_summed"], 1)
                dve.tensor_scalar(flat(B4[:]), psf, 1.0 / HD, GN_EPS, ALU.mult, ALU.add).then_inc(s["var_ready"], 1)
                dve.wait_ge(s["root_done"], 1)
                ch(dve.reciprocal(flat(B4[:]), flat(B4[:])))
                ch(dve.tensor_tensor(flat(yc), flat(yc), flat(B4[:]), ALU.mult))
                for j in range(4):
                    ch(dve.tensor_scalar(yc[:, j, :], yc[:, j, :], b.ln_w[:, j:j + 1], b.ln_b[:, j:j + 1], ALU.mult, ALU.add))
                ch(dve.tensor_tensor(flat(yc), flat(yc), flat(B0[:]), ALU.add))
                dve.wait_ge(s["g_summed"], 1)
                ch(dve.tensor_tensor(flat(yc), flat(yc), psf, ALU.mult))


def project_out(nc, c, w, parts):
    w_t = w.rearrange("(k p) n -> p k n", p=P)
    with phase(nc, c) as (sem, sb):
        w_in = [sem("w_in0"), sem("w_in1")]
        w_high, w_low, staged, stage_high, stage_free = (
            sem(n) for n in ("w_high", "w_low", "staged", "stage_high", "stage_free"))
        summed, bank_free, order = sem("summed"), sem("bank_free"), sem("order")
        raw = sb("w_raw", [P, 2, HALF])
        wh, wl = sb("w_high", [P, KT, D], F32R), sb("w_low", [P, KT, D], F32R)
        sh, sl = sb("y_high", [P, 2, KT, P], F32R), sb("y_low", [P, 2, KT, P], F32R)
        ps = c.ps
        pieces = [(k, slice(h * HALF, (h + 1) * HALF)) for k in range(KT) for h in range(2)]
        spans, k0 = [], 0
        for part in parts:
            spans.append((part, slice(k0, k0 + part.shape[1])))
            k0 += part.shape[1]
        with nc.Block() as block:

            @block.sync
            def _(sp):
                for n, (k, cols) in enumerate(pieces):
                    if n >= 2:
                        sp.wait_ge(w_low, n - 1)
                    sp.dma_start(raw[:, n % 2, :], w_t[:, k, cols]).then_inc(w_in[n % 2], 16)

            @block.scalar
            def _(act):
                for n, (k, cols) in enumerate(pieces):
                    act.wait_ge(w_in[n % 2], 16 * (n // 2 + 1))
                    act.copy(wh[:, k, cols], raw[:, n % 2, :]).then_inc(w_high, 1)
                with act.Fori(0, TT // 2) as i:
                    for q in range(2):
                        take(act, stage_free)
                        for part, ks in spans:
                            act.copy(sh[:, q, ks, :], part[:, :, bass.ds(i * (2 * P) + q * P, P)]).then_inc(order, 1)
                            take(act, order)
                        act.sem_inc(stage_high, 1)

            @block.vector
            def _(dve):
                for n, (k, cols) in enumerate(pieces):
                    dve.wait_ge(w_high, n + 1)
                    dve.tensor_tensor(wl[:, k, cols], raw[:, n % 2, :], wh[:, k, cols].bitcast(F32), ALU.subtract).then_inc(w_low, 1)
                dve.sem_inc(bank_free, 4)

                def lows(i, q):
                    take(dve, stage_high)
                    for part, ks in spans:
                        dve.tensor_tensor(sl[:, q, ks, :], part[:, :, bass.ds(i * (2 * P) + q * P, P)],
                                          sh[:, q, ks, :].bitcast(F32), ALU.subtract).then_inc(staged, 1)

                def add(i, q):
                    for h in range(2):
                        take(dve, summed)
                        rs = c.res[:, bass.ds(2 * i + q, 1), h * HALF:(h + 1) * HALF]
                        dve.tensor_tensor(rs, rs, ps[:, 2 * q + h:2 * q + h + 1, :], ALU.add).then_inc(bank_free, 1)

                with dve.Fori(0, TT // 2) as i:
                    lows(i, 0)
                    lows(i, 1)
                    add(i, 0)
                    add(i, 1)

            @block.tensor
            def _(pe):
                pe.sem_inc(stage_free, 2)
                pe.wait_ge(w_low, len(pieces))
                with pe.Fori(0, TT // 2):
                    for q in range(2):
                        take(pe, staged, len(spans))
                        for h in range(2):
                            take(pe, bank_free)
                            n = 0
                            for y, wp in ((sh, wh), (sh, wl), (sl, wh)):
                                for k in range(KT):
                                    last = pe.matmul(ps[:, 2 * q + h, :], y[:, q, k, :], wp[:, k, h * HALF:(h + 1) * HALF],
                                                     start=n == 0, stop=n == 3 * KT - 1)
                                    n += 1
                            last.then_inc(summed, 1)
                        pe.drain().then_inc(stage_free, 1)


def route(nc, c, m, h_T, w_group, b_group, w_expert, b_expert):
    NL = NG + NE
    with phase(nc, c) as (sem, sb):
        names = ("par_in", "made", "summed", "order", "group_shift", "group_exp", "pair_shift", "pair_exp", "picked",
                 "ranked")
        s = {n: sem(n) for n in names}
        wr = sb("w_router", [P, KT, NL])
        bias = sb("b_router", [P, NL])
        upper = sb("tokens_before", [P, P])
        it = sb("iota", [P, 64])
        i128 = sb("iota_128", [P, EPG])
        lg = sb("logits", [P, TT, NL])
        col = {n: sb(n, [P, TT]) for n in ("gmax", "gsum", "ggate", "m1", "m2", "rden", "first")}
        gsh, gsel, gtmp = (sb(n, [P, TT, NG]) for n in ("g_shift", "g_sel", "g_tmp"))
        ex, ex2, etmp, oh1, oh2 = (sb(n, [P, TT, EPG]) for n in ("e_logits", "e_rest", "e_tmp", "e_hot1", "e_hot2"))
        prod = sb("e_prod", [P, TT, EPG, NG])
        sel = [sb(f"sel{k}", [P, TT, NE]) for k in range(2)]
        both = sb("sel_both", [P, TT, NE])
        rows = sb("rows_of_expert", [P, TT, NE])
        rtmp = sb("rows_tmp", [P, TT, NE])
        rowf = sb("row_f", [P, 2, TT])
        nblk, pend, pstart = (sb(n, [P, NE]) for n in ("n_blocks", "blocks_end", "blocks_start"))
        cmp8 = sb("cmp_blocks", [P, NE, EPG])
        cmpb = sb("cmp_expert", [P, NBLK, NE])
        blkf = sb("block_expert_f", [P, NBLK])
        turnf, tcmp = sb("turns_f", [P, 1]), sb("turns_cmp", [P, NBLK // 2])
        ps = c.ps
        with nc.Block() as block:

            @block.sync
            def _(sp):
                sp.dma_start(wr[:, :, 0:NG], w_group.rearrange("(k p) g -> p k g", p=P)).then_inc(s["par_in"], 16)
                sp.dma_start(wr[:, :, NG:NL], w_expert.rearrange("(k p) g -> p k g", p=P)).then_inc(s["par_in"], 16)
                sp.dma_start(bias[:, 0:NG], b_group.partition_broadcast(P)).then_inc(s["par_in"], 16)
                sp.dma_start(bias[:, NG:NL], b_expert.partition_broadcast(P)).then_inc(s["par_in"], 16)
                sp.wait_ge(s["par_in"], 64)

            @block.gpsimd
            def _(pool):
                ch = Chain(pool, s["made"])
                ch(pool.iota(it[:], [[1, 64]], base=0, channel_multiplier=0, allow_small_or_imprecise_dtypes=True))
                ch(pool.iota(i128[:], [[P, EPG]], base=0, channel_multiplier=0, allow_small_or_imprecise_dtypes=True))
                ch(pool.memset(upper[:], 1.0))
                ch(pool.affine_select(out=upper[:], in_=upper[:], pattern=[[1, P]], compare_op=ALU.is_gt, fill=0.0,
                                      base=0, channel_multiplier=-1))

            @block.tensor
            def _(pe):
                pe.wait_ge(s["par_in"], 64)
                for t in range(TT):
                    for k in range(KT):
                        last = pe.matmul(ps[:, 0, t * NL:(t + 1) * NL], h_T[:, k, t * P:(t + 1) * P], wr[:, k, :],
                                         start=k == 0, stop=k == KT - 1)
                last.then_inc(s["summed"], 1)
                pe.wait_ge(s["picked"], 1)
                pe.wait_ge(s["made"], 4)
                for t in range(TT):
                    for u in range(t + 1):
                        pe.matmul(ps[:, 1, t * NE:(t + 1) * NE], upper[:] if u == t else c.ones[:], both[:, u, :],
                                  start=u == 0, stop=u == t)
                for u in range(TT):
                    last = pe.matmul(ps[:, 2, 0:NE], c.ones[:], both[:, u, :], start=u == 0, stop=u == TT - 1)
                last.then_inc(s["ranked"], 1)

            @block.scalar
            def _(act):
                act.wait_ge(s["group_shift"], 1)
                act.activation(gtmp[:], gsh[:], ACT.Exp).then_inc(s["group_exp"], 1)
                act.wait_ge(s["pair_shift"], 1)
                act.activation(col["m2"][:], col["m2"][:], ACT.Exp).then_inc(s["pair_exp"], 1)

            @block.vector
            def _(dve):
                ch = Chain(dve, s["order"])

                def first_hot(hot, src, top, n):
                    ch(dve.tensor_reduce(top[:], src, AX.X, ALU.max))
                    ch(dve.tensor_tensor(hot, src, bcast(top[:], 2, n), ALU.is_equal))
                    ch(dve.scalar_tensor_tensor(out=hot, in0=hot, scalar=-64.0, in1=bcast(it[:, 0:n], 1, TT),
                                                op0=ALU.mult, op1=ALU.add))
                    ch(dve.tensor_reduce(col["first"][:], hot, AX.X, ALU.min))
                    ch(dve.tensor_tensor(hot, hot, bcast(col["first"][:], 2, n), ALU.is_equal))

                dve.wait_ge(s["made"], 2)
                dve.wait_ge(s["summed"], 1)
                ch(dve.tensor_tensor(lg[:], ps[:, 0, 0:TT * NL].rearrange("p (t n) -> p t n", t=TT), bcast(bias[:], 1, TT), ALU.add))
                g = lg[:, :, 0:NG]
                first_hot(gsel[:], g, col["gmax"], NG)
                dve.tensor_tensor(gsh[:], g, bcast(col["gmax"][:], 2, NG), ALU.subtract).then_inc(s["group_shift"], 1)
                dve.wait_ge(s["group_exp"], 1)
                ch(dve.tensor_reduce(col["gsum"][:], gtmp[:], AX.X, ALU.add))
                ch(dve.reciprocal(col["ggate"][:], col["gsum"][:]))
                ch(dve.tensor_tensor(prod[:], lg[:, :, NG:NL].rearrange("p t (g e) -> p t e g", g=NG),
                                     bcast(gsel[:], 2, EPG), ALU.mult))
                ch(dve.tensor_reduce(ex[:], prod[:], AX.X, ALU.add))
                first_hot(oh1[:], ex[:], col["m1"], EPG)
                ch(dve.scalar_tensor_tensor(out=ex2[:], in0=oh1[:], scalar=-BIG, in1=ex[:], op0=ALU.mult, op1=ALU.add))
                first_hot(oh2[:], ex2[:], col["m2"], EPG)
                dve.tensor_tensor(col["m2"][:], col["m2"][:], col["m1"][:], ALU.subtract).then_inc(s["pair_shift"], 1)
                for k, oh in enumerate((oh1, oh2)):
                    ch(dve.tensor_tensor(sel[k][:].rearrange("p t (g e) -> p t g e", g=NG), bcast(gsel[:], 3, EPG),
                                         bcast(oh[:], 2, NG), ALU.mult))
                dve.tensor_tensor(both[:], sel[0][:], sel[1][:], ALU.add).then_inc(s["picked"], 1)
                dve.wait_ge(s["pair_exp"], 1)
                ch(dve.tensor_scalar(col["rden"][:], col["m2"][:], 1.0, None, ALU.add))
                ch(dve.reciprocal(col["rden"][:], col["rden"][:]))
                ch(dve.tensor_tensor(m.gate[:, 0, :], col["rden"][:], col["ggate"][:], ALU.mult))
                ch(dve.tensor_tensor(m.gate[:, 1, :], m.gate[:, 0, :], col["m2"][:], ALU.mult))
                dve.wait_ge(s["ranked"], 1)
                ch(dve.tensor_copy(nblk[:], ps[:, 2, 0:NE]))
                ch(dve.tensor_tensor(cmp8[:], bcast(nblk[:], 2, EPG), bcast(i128[:], 1, NE), ALU.is_gt))
                ch(dve.tensor_reduce(nblk[:], cmp8[:], AX.X, ALU.add))
                ch(dve.tensor_tensor_scan(pend[:], c.ones[:, 0:NE], nblk[:], 0.0, ALU.mult, ALU.add))
                ch(dve.tensor_tensor(pstart[:], pend[:], nblk[:], ALU.subtract))
                ch(dve.tensor_scalar(pstart[:], pstart[:], float(P), float(P), ALU.mult, ALU.add))
                ch(dve.tensor_tensor(rows[:], ps[:, 1, 0:TT * NE].rearrange("p (t n) -> p t n", t=TT), bcast(pstart[:], 1, TT), ALU.add))
                for k in range(2):
                    ch(dve.tensor_tensor(rtmp[:], rows[:], sel[k][:], ALU.mult))
                    ch(dve.tensor_reduce(rowf[:, k, :], rtmp[:], AX.X, ALU.add))
                ch(dve.tensor_copy(m.row[:], rowf[:]))
                ch(dve.tensor_tensor(cmpb[:], bcast(pend[:], 1, NBLK), bcast(it[:, 0:NBLK], 2, NE), ALU.is_le))
                ch(dve.tensor_reduce(blkf[:], cmpb[:], AX.X, ALU.add))
                ch(dve.tensor_scalar(blkf[:], blkf[:], float(NE - 1), None, ALU.min))
                ch(dve.tensor_copy(m.block_expert[:], blkf[:]))
                ch(dve.tensor_scalar(tcmp[:], it[:, 0:NBLK // 2], 2.0, None, ALU.mult))
                ch(dve.tensor_tensor(tcmp[:], tcmp[:], pend[:, NE - 1:NE].to_broadcast([P, NBLK // 2]), ALU.is_lt))
                ch(dve.tensor_reduce(turnf[:], tcmp[:], AX.X, ALU.add))
                ch(dve.tensor_copy(m.turns[:], turnf[:]))


def dispatch(nc, c, m, row_tok):
    with phase(nc, c) as (sem, sb):
        made, cleared, placed, back = sem("made"), sem("cleared", True), sem("placed", True), sem("back", True)
        widened, turned = sem("widened"), sem("turned")
        by_block, by_block_f = sb("token_by_block", [NBLK, P], I32), sb("token_by_block_f", [NBLK, P])
        ps = c.ps
        zero = sb("zero_rows", [P, NBLK + 1], I32)
        tok = sb("token_id", [P, TT], I32)
        with nc.Block() as block:

            @block.gpsimd
            def _(pool):
                ch = Chain(pool, made)
                ch(pool.memset(zero[:], 0))
                ch(pool.iota(tok[:], [[P, TT]], base=0, channel_multiplier=1))
                pool.dma_start(row_tok.rearrange("(p n) o -> p (n o)", p=P), zero[:]).then_inc(cleared, 16)
                pool.wait_ge(cleared, 16)
                for k in range(2):
                    for t in range(TT):
                        pool.indirect_dma_start(row_tok, bass.IndirectOffsetOnAxis(ap=m.row[:, k, t:t + 1], axis=0),
                                                tok[:, t:t + 1], None).then_inc(placed, 16)
                pool.wait_ge(placed, 32 * TT)
                pool.dma_start(by_block[:], row_tok[P:, 0].rearrange("(b p) -> b p", p=P)).then_inc(back, 16)

            @block.vector
            def _(dve):
                dve.wait_ge(back, 16)
                dve.tensor_copy(by_block_f[:], by_block[:]).then_inc(widened, 1)
                dve.wait_ge(turned, 1)
                dve.tensor_copy(m.row_token[:], ps[:, 0, 0:NBLK])

            @block.tensor
            def _(pe):
                pe.wait_ge(widened, 1)
                pe.transpose(ps[:, 0, 0:NBLK], by_block_f[:], c.ident[0:NBLK, 0:NBLK]).then_inc(turned, 1)


def experts(nc, c, m, rows, ys, w_gate, w_up, w_down):
    GU, DN = FF * KT // D, FF // P
    NPC = 2 * GU + DN
    KP = KT // GU
    with phase(nc, c) as (sem, sb):
        x_in, x_ready, x_free = sem("x_in", True), sem("x_ready"), sem("x_free")
        raw_in = [sem(f"raw_in{p}") for p in range(NPC)]
        high_made, low_made, w_ready, w_free = sem("high_made"), sem("low_made"), sem("w_ready"), sem("w_free")
        x_turned, xh_made, xh_ready, xl_ready = sem("x_turned"), sem("xh_made"), sem("xh_ready"), sem("xl_ready")
        g_done, u_done, silu_ready, hid_ready = sem("g_done"), sem("u_done"), sem("silu_ready"), sem("hid_ready")
        hid_turned, hh_made, hh_ready, hl_ready = sem("hid_turned"), sem("hh_made"), sem("hh_ready"), sem("hl_ready")
        d_done, y_stored = sem("d_done"), sem("y_stored")
        order_a, order_p = sem("order_a"), sem("order_p")
        raw = sb("w_raw", [P, NPC, D])
        wh, wl = sb("w_high", [P, NPC, D], F32R), sb("w_low", [P, NPC, D], F32R)
        idx = sb("row_index", [P, 1], I32)
        xg = sb("x_rows", [P, D])
        xh, xl = sb("x_high", [P, 2, KT, P], F32R), sb("x_low", [P, 2, KT, P], F32R)
        hid = sb("hidden", [P, FF])
        hh, hl = sb("hidden_high", [P, DN, P], F32R), sb("hidden_low", [P, DN, P], F32R)
        yb = sb("y_rows", [P, D])
        ps = c.ps
        B_X, B_G, B_U, B_H, B_Y = 0, 2, 3, 4, 6
        gate_up, down_p = range(2 * GU), range(2 * GU, NPC)

        def turns(eng):
            return eng.value_load(m.turns[0:1, 0:1], min_val=NBLK // 3 // 2, max_val=NBLK // 2)

        with nc.Block() as block:

            @block.sync
            def _(sp):
                def expert(b):
                    return sp.value_load(m.block_expert[0:1, bass.ds(b, 1)], min_val=0, max_val=NE - 1)

                def split_done():
                    take(sp, low_made)
                    sp.sem_inc(w_ready, 1)

                def load(e, pieces, fresh=False):
                    for p in pieces:
                        if not fresh:
                            split_done()
                        w, k0, kn = (w_down, p - 2 * GU, 1) if p >= 2 * GU else ((w_gate, w_up)[p // GU], p % GU * KP, KP)
                        src = w[bass.ds(e, 1), k0 * P:(k0 + kn) * P].rearrange("e (k p) f -> p (e k) f", p=P)
                        sp.dma_start(raw[:, p, :].rearrange("p (k f) -> p k f", k=kn), src).then_inc(raw_in[p], 16)

                n = turns(sp)
                e0, e1 = expert(0), expert(1)
                load(e0, gate_up, fresh=True)
                load(e1, gate_up)
                load(e0, down_p, fresh=True)
                with sp.Fori(1, n) as i:
                    e = [expert(2 * i - 1 + d) for d in range(3)]
                    for d in range(2):
                        load(e[d + 1], gate_up)
                        load(e[d], down_p)
                for _p in gate_up:
                    split_done()
                load(expert(2 * n - 1), down_p)
                for _p in down_p:
                    split_done()

            @block.gpsimd
            def _(pool):
                n = turns(pool)
                with pool.Fori(0, n) as i:
                    for q in range(2):
                        take(pool, x_free)
                        pool.tensor_copy(idx[:], m.row_token[:, bass.ds(2 * i + q, 1)]).then_inc(order_p, 1)
                        take(pool, order_p)
                        pool.indirect_dma_start(xg[:], None, rows, bass.IndirectOffsetOnAxis(ap=idx[:], axis=0)).then_inc(x_in, 16)
                        pool.wait_ge(x_in, 32 * i + 16 * (q + 1))
                        pool.sem_inc(x_ready, 1)

            @block.scalar
            def _(act):
                def high(pieces, fresh=False):
                    for p in pieces:
                        take(act, raw_in[p], 16)
                        if not fresh:
                            take(act, w_free)
                        act.copy(wh[:, p, :], raw[:, p, :]).then_inc(high_made, 1)

                def x_high(q):
                    take(act, x_turned)
                    act.sem_inc(x_free, 1)
                    act.copy(xh[:, q], ps[:, B_X:B_X + 2, :].rearrange("p b (k n) -> p (b k) n", k=4)).then_inc(order_a, 1)
                    take(act, order_a)
                    act.sem_inc(xh_made, 1)
                    act.sem_inc(xh_ready, 1)

                def silu():
                    take(act, g_done)
                    act.activation(hid[:], ps[:, B_G, :], ACT.Silu).then_inc(silu_ready, 1)

                def hidden_high():
                    take(act, hid_turned)
                    act.copy(hh[:].rearrange("p k n -> p (k n)"), ps[:, B_H, :]).then_inc(order_a, 1)
                    take(act, order_a)
                    act.sem_inc(hh_made, 1)
                    act.sem_inc(hh_ready, 1)

                def y_out(block_row):
                    take(act, d_done)
                    take(act, y_stored, 16)
                    act.copy(yb[:].rearrange("p (b n) -> p b n", b=2), ps[:, B_Y:B_Y + 2, :]).then_inc(order_a, 1)
                    take(act, order_a)
                    act.dma_start(ys[block_row, :], yb[:]).then_inc(y_stored, 16)

                def step(q, y_row, last=False):
                    if not last:
                        high(range(0, 2))
                        x_high(1 - q)
                        high(range(2, GU))
                    silu()
                    if last:
                        take(act, w_free, 2 * GU)
                    else:
                        high(range(GU, 2 * GU))
                    high(down_p, fresh=y_row is None)
                    if y_row is not None:
                        y_out(y_row)
                    hidden_high()

                act.sem_inc(x_free, 1)
                act.sem_inc(y_stored, 16)
                n = turns(act)
                high(gate_up, fresh=True)
                x_high(0)
                step(0, None)
                with act.Fori(1, n) as i:
                    step(1, bass.ds((2 * i - 1) * P, P))
                    step(0, bass.ds(2 * i * P, P))
                step(1, bass.ds((2 * n - 1) * P, P), last=True)
                y_out(bass.ds(2 * n * P, P))
                act.wait_ge(y_stored, 16)

            @block.tensor
            def _(pe):
                def turn_x():
                    take(pe, x_ready)
                    for k in range(KT):
                        last = pe.transpose(ps[:, B_X + k // 4, (k % 4) * P:(k % 4 + 1) * P], xg[:, k * P:(k + 1) * P], c.ident[:])
                    last.then_inc(x_turned, 1)

                def triple(bank, high, low, w_h, w_l, first, final):
                    pe.matmul(ps[:, bank, :], high, w_h, start=first, stop=False)
                    pe.matmul(ps[:, bank, :], high, w_l, start=False, stop=False)
                    return pe.matmul(ps[:, bank, :], low, w_h, start=False, stop=final)

                def gate_or_up(bank, p0, q, done):
                    for p in range(p0, p0 + GU):
                        take(pe, w_ready)
                        for kp in range(KP):
                            k, f = (p - p0) * KP + kp, slice(kp * FF, (kp + 1) * FF)
                            last = triple(bank, xh[:, q, k, :], xl[:, q, k, :], wh[:, p, f], wl[:, p, f], k == 0, k == KT - 1)
                        last.then_inc(w_free, 1)
                    pe.drain().then_inc(done, 1)

                def turn_hidden():
                    take(pe, hid_ready)
                    for k in range(DN):
                        last = pe.transpose(ps[:, B_H, k * P:(k + 1) * P], hid[:, k * P:(k + 1) * P], c.ident[:])
                    last.then_inc(hid_turned, 1)

                def down():
                    take(pe, hh_ready)
                    take(pe, hl_ready)
                    for k in range(DN):
                        take(pe, w_ready)
                        p = 2 * GU + k
                        for h in range(2):
                            f = slice(h * HALF, (h + 1) * HALF)
                            last = triple(B_Y + h, hh[:, k, :], hl[:, k, :], wh[:, p, f], wl[:, p, f], k == 0, k == DN - 1)
                        last.then_inc(w_free, 1)
                    pe.drain().then_inc(d_done, 1)

                def step(q, first=False, last=False):
                    take(pe, xh_ready)
                    take(pe, xl_ready)
                    gate_or_up(B_G, 0, q, g_done)
                    if not last:
                        turn_x()
                    gate_or_up(B_U, GU, q, u_done)
                    if not first:
                        down()
                    turn_hidden()

                n = turns(pe)
                turn_x()
                step(0, first=True)
                with pe.Fori(1, n):
                    step(1)
                    step(0)
                step(1, last=True)
                down()

            @block.vector
            def _(dve):
                def low(pieces):
                    for p in pieces:
                        take(dve, high_made)
                        dve.tensor_tensor(wl[:, p, :], raw[:, p, :], wh[:, p, :].bitcast(F32), ALU.subtract).then_inc(low_made, 1)

                def x_low(q):
                    take(dve, xh_made)
                    dve.tensor_tensor(xl[:, q], ps[:, B_X:B_X + 2, :].rearrange("p b (k n) -> p (b k) n", k=4),
                                      xh[:, q].bitcast(F32), ALU.subtract).then_inc(xl_ready, 1)

                def hidden():
                    take(dve, silu_ready)
                    take(dve, u_done)
                    dve.tensor_tensor(hid[:], hid[:], ps[:, B_U, :], ALU.mult).then_inc(hid_ready, 1)

                def hidden_low():
                    take(dve, hh_made)
                    dve.tensor_tensor(hl[:].rearrange("p k n -> p (k n)"), ps[:, B_H, :],
                                      hh[:].rearrange("p k n -> p (k n)").bitcast(F32), ALU.subtract).then_inc(hl_ready, 1)

                def step(q, last=False):
                    if not last:
                        low(range(0, 2))
                        x_low(1 - q)
                        low(range(2, 2 * GU))
                    hidden()
                    low(down_p)
                    hidden_low()

                n = turns(dve)
                low(gate_up)
                x_low(0)
                step(0)
                with dve.Fori(1, n):
                    step(1)
                    step(0)
                step(1, last=True)


def combine(nc, c, m, ys):
    NB = 4
    with phase(nc, c) as (sem, sb):
        got = [sem(f"got{i}", True) for i in range(NB)]
        used = sem("used")
        yg = sb("y_gathered", [P, NB, D])
        with nc.Block() as block:

            @block.gpsimd
            def _(pool):
                for n in range(2 * TT):
                    t, k = n // 2, n % 2
                    if n >= NB:
                        pool.wait_ge(used, n - NB + 1)
                    pool.indirect_dma_start(yg[:, n % NB, :], None, ys, bass.IndirectOffsetOnAxis(ap=m.row[:, k, t:t + 1], axis=0)).then_inc(got[n % NB], 16)

            @block.vector
            def _(dve):
                for n in range(2 * TT):
                    t, k = n // 2, n % 2
                    dve.wait_ge(got[n % NB], 16 * (n // NB + 1))
                    if n:
                        dve.wait_ge(used, n)
                    dve.scalar_tensor_tensor(out=c.res[:, t, :], in0=yg[:, n % NB, :], scalar=m.gate[:, k, t:t + 1],
                                             in1=c.res[:, t, :], op0=ALU.mult, op1=ALU.add).then_inc(used, 1)


def moe(nc, c, a, layer):
    with ExitStack() as ctx:
        def sb(name, shape, dt=F32):
            return ctx.enter_context(nc.sbuf_tensor(f"{name}_{layer}", shape, dt))

        m = Chip()
        m.row, m.gate = sb("row_of", [P, 2, TT], I32), sb("gate_of", [P, 2, TT])
        m.row_token = sb("token_of_row", [P, NBLK], I32)
        m.block_expert, m.turns = sb("block_expert", [P, NBLK], I32), sb("turns", [P, 1], I32)
        with nc.sbuf_tensor(f"h_T_ffn_{layer}", [P, KT, S], F32) as h_T:
            norm(nc, c, a["norm_ffn"][layer], h_T=h_T, rows=c.rows)
            route(nc, c, m, h_T, a["moe_w_group"][layer], a["moe_b_group"][layer], a["moe_w_expert"][layer], a["moe_b_expert"][layer])
        dispatch(nc, c, m, c.row_tok)
        experts(nc, c, m, c.rows, c.ys, a["moe_w_gate"][layer], a["moe_w_up"][layer], a["moe_w_down"][layer])
        combine(nc, c, m, c.ys)


def hgrn(nc, c, w, lower_bound, norm_w, h_T, y_T):
    w_t = w.rearrange("(k p) m -> p k m", p=P)
    NL = len(HLEVELS)
    with phase(nc, c) as (sem, sb):
        names = ("par_in", "lb_order", "lb_exp", "masks_made", "order", "order_a",
                 "proj_done", "head_ready", "v_ready", "head_done", "fg_ready", "lf_ready", "k_ready",
                 "diff_ready", "exp_ready", "level_ready", "step_ready", "kd_ready", "qe_ready", "bc_ready",
                 "v_turned", "v_rows_ready", "kd_turned", "kd_rows_ready", "ds_done", "s_ready", "score_ready",
                 "o_done", "sq_ready", "sq_summed", "var_ready", "rstd_ready", "tail_free", "o_read")
        s = {n: sem(n) for n in names}
        w_in, w_free = [sem(f"w_in{n}") for n in range(4)], [sem(f"w_free{n}") for n in range(4)]
        bank_free = [sem("bank_free0"), sem("bank_free1")]
        gram_done, gram_free = [sem("gram_done0"), sem("gram_done1")], [sem("gram_free0"), sem("gram_free1")]
        wt = sb("w_tiles", [P, 4, KT, P])
        Q, G, V, F = (sb(n, [P, 2, S]) for n in ("q", "g", "v", "log_f"))
        K, BC = sb("k", [P, S]), sb("cum_log_f", [P, S])
        E = sb("level_ops", [P, 4, S])
        KD, QE = sb("k_to_end", [P, S]), sb("q_from_start", [P, S])
        VR, KR = sb("v_rows", [P, TT, P]), sb("k_rows", [P, TT, P])
        SC = sb("scores_T", [P, TT, P])
        ST = sb("states", [P, TT, P])
        reset = sb("chunk_reset", [P, S])
        mask = sb("level_masks", [P, NL, P])
        step = sb("step", [P, TT])
        lb, lb1, nw = sb("lower_bound", [P, HEADS]), sb("one_minus_lb", [P, HEADS]), sb("norm_w", [P, HEADS])
        l0, l1, lm = (sb(n, [P, HEADS]) for n in ("lb0", "lb1_in", "lb_max"))
        ps = c.ps
        pair = lambda ap: ap.rearrange("p b n -> p (b n)")
        col = lambda t, h: t[:, bass.ds(h, 1)]

        def make_masks(pool):
            ch = Chain(pool, s["masks_made"])
            ch(pool.memset(mask[:], 1.0))
            for i, hw in enumerate(HLEVELS):
                up = mask[:, i, :].rearrange("p (n h q) -> p n h q", h=2, q=hw)
                for pat, base, mult in (([[-2 * hw, P // (2 * hw)], [1000, 2], [0, hw]], -1000, 1),
                                        ([[2 * hw, P // (2 * hw)], [0, 2], [0, hw]], hw - 1, -1)):
                    ch(pool.affine_select(out=up, in_=up, pattern=pat, compare_op=ALU.is_ge, fill=0.0, base=base,
                                          channel_multiplier=mult))
            ch(pool.memset(reset[:], 1.0))
            ch(pool.memset(reset[:].rearrange("p (n q) -> p n q", q=P)[:, :, 0:1], 0.0))
            return ch.n

        n_masks = 1 + 2 * NL + 2

        def level_view(t, lv):
            return t.rearrange("p (n w) -> p n w", w=2 * HLEVELS[lv])

        with nc.Block() as block:

            @block.gpsimd
            def _(pool):
                assert make_masks(pool) == n_masks

            @block.sync
            def _(sp):
                for t, v in ((l0, lower_bound[0]), (l1, lower_bound[1]), (nw, norm_w)):
                    sp.dma_start(t[:], column(v)).then_inc(s["par_in"], 16)

                def load(h):
                    for m in range(4):
                        take(sp, w_free[m])
                        c0 = ORDER[m] * D
                        sp.dma_start(wt[:, m], w_t[:, :, bass.ds(h * P + c0, P)]).then_inc(w_in[m], 16)

                ORDER = (1, 0, 3, 2)
                with sp.Fori(0, HEADS) as h:
                    load(h)
                sp.wait_ge(s["par_in"], 48)

            @block.tensor
            def _(pe):
                def project(m):
                    take(pe, w_in[m], 16)
                    take(pe, bank_free[m % 2])
                    for h in range(NH):
                        for k in range(KT):
                            last = pe.matmul(ps[:, 2 * (m % 2) + h, :], wt[:, m, k, :], h_T[:, k, h * HALF:(h + 1) * HALF],
                                             start=k == 0, stop=k == KT - 1)
                    last.then_inc(s["proj_done"], 1)

                def gram(left, right):
                    for b in range(2):
                        take(pe, gram_free[b])
                        for n in range(4):
                            t = slice((4 * b + n) * P, (4 * b + n + 1) * P)
                            last = pe.matmul(ps[:, 4 + b, n * P:(n + 1) * P], left[:, t], right[:, t], start=True, stop=True)
                        last.then_inc(gram_done[b], 1)

                def turn(src, done):
                    for n in range(TT):
                        last = pe.transpose(ps[:, 6 + n // 4, (n % 4) * P:(n % 4 + 1) * P], src[:, n * P:(n + 1) * P], c.ident[:])
                    last.then_inc(done, 1)

                def half(par, more):
                    take(pe, s["v_ready"])
                    take(pe, s["tail_free"])
                    turn(V[:, par, :], s["v_turned"])
                    take(pe, s["k_ready"])
                    gram(K[:], Q[:, par, :])
                    for m in range(4):
                        if more:
                            project(m)
                        for lv in (2 * m, 2 * m + 1):
                            if lv < NL:
                                take(pe, s["level_ready"])
                                gram(E[:, lv % 4, :], E[:, lv % 4, :])
                    take(pe, s["v_rows_ready"])
                    take(pe, s["kd_ready"])
                    turn(KD[:], s["kd_turned"])
                    take(pe, s["kd_rows_ready"])
                    for n in range(TT):
                        last = pe.matmul(ps[:, 6 + n // 4, (n % 4) * P:(n % 4 + 1) * P], KR[:, n, :], VR[:, n, :], start=True, stop=True)
                    last.then_inc(s["ds_done"], 1)
                    take(pe, s["s_ready"])
                    take(pe, s["qe_ready"])
                    for b in range(2):
                        take(pe, gram_free[b])
                    for n in range(TT):
                        o = ps[:, 4 + n // 4, (n % 4) * P:(n % 4 + 1) * P]
                        pe.matmul(o, VR[:, n, :], SC[:, n, :], start=True, stop=False)
                        last = pe.matmul(o, ST[:, n, :], QE[:, n * P:(n + 1) * P], start=False, stop=True)
                    last.then_inc(s["o_done"], 1)
                    take(pe, s["sq_ready"])
                    for h in range(NH):
                        last = pe.matmul(ps[:, 6 + h, :], c.ones[:], BC[:, h * HALF:(h + 1) * HALF], start=True, stop=True)
                    last.then_inc(s["sq_summed"], 1)

                for m in range(4):
                    project(m)
                with pe.Fori(0, HEADS // 2 - 1):
                    half(0, True)
                    half(1, True)
                half(0, True)
                half(1, False)

            @block.scalar
            def _(act):
                act.wait_ge(s["lb_order"], 2)
                act.activation(l0[:], l0[:], ACT.Exp).then_inc(s["lb_exp"], 1)
                act.activation(l1[:], l1[:], ACT.Exp).then_inc(s["lb_exp"], 1)
                for m in range(4):
                    act.sem_inc(w_free[m], 1)
                for q in range(2):
                    act.sem_inc(bank_free[q], 1)

                def link(ins):
                    ins.then_inc(s["order_a"], 1)
                    take(act, s["order_a"])

                def copy_out(m, par):
                    take(act, s["proj_done"])
                    act.sem_inc(w_free[m], 1)
                    src = pair(ps[:, 2 * (m % 2):2 * (m % 2) + 2, :])
                    if m == 0:
                        link(act.activation(F[:, par, :], src, ACT.Sigmoid))
                    elif m == 3:
                        link(act.copy(V[:, par, :], src))
                    else:
                        link(act.activation((Q, G)[m - 1][:, par, :], src, ACT.Silu))
                    act.sem_inc(bank_free[m % 2], 1)
                    if m == 3:
                        act.sem_inc(s["head_ready"], 1)
                        act.sem_inc(s["v_ready"], 1)

                def level_exp(lv):
                    take(act, s["diff_ready"])
                    v, hw = level_view(E[:, lv % 4, :], lv), HLEVELS[lv]
                    link(act.activation(v[:, :, 0:hw], v[:, :, 0:hw], ACT.Exp, scale=-1.0))
                    act.activation(v[:, :, hw:2 * hw], v[:, :, hw:2 * hw], ACT.Exp).then_inc(s["exp_ready"], 1)

                def half(par, more):
                    take(act, s["fg_ready"])
                    act.activation(F[:, par, :], F[:, par, :], ACT.Ln).then_inc(s["lf_ready"], 1)
                    take(act, s["v_turned"])
                    act.copy(VR[:].rearrange("p t n -> p (t n)"), pair(ps[:, 6:8, :])).then_inc(s["v_rows_ready"], 1)
                    take(act, s["bc_ready"])
                    act.activation(step[:], BC[:].rearrange("p (n q) -> p n q", q=P)[:, :, P - 1], ACT.Exp).then_inc(s["step_ready"], 1)
                    if more:
                        take(act, s["head_done"])
                    for m in range(4):
                        if more:
                            copy_out(m, 1 - par)
                        for lv in (2 * m, 2 * m + 1):
                            if lv < NL:
                                level_exp(lv)
                    take(act, s["diff_ready"])
                    act.activation(KD[:], KD[:], ACT.Exp).then_inc(s["exp_ready"], 1)
                    act.activation(QE[:], BC[:], ACT.Exp).then_inc(s["exp_ready"], 1)
                    take(act, s["kd_turned"])
                    act.copy(KR[:].rearrange("p t n -> p (t n)"), pair(ps[:, 6:8, :])).then_inc(s["kd_rows_ready"], 1)
                    take(act, s["o_done"])
                    act.activation(BC[:], pair(ps[:, 4:6, :]), ACT.Square).then_inc(s["sq_ready"], 1)
                    take(act, s["var_ready"])
                    link(act.activation(F[:, par, :], F[:, par, :], ACT.Ln))
                    act.activation(F[:, par, :], F[:, par, :], ACT.Exp, scale=-0.5).then_inc(s["rstd_ready"], 1)

                for m in range(4):
                    copy_out(m, 0)
                with act.Fori(0, HEADS // 2 - 1):
                    half(0, True)
                    half(1, True)
                half(0, True)
                half(1, False)

            @block.vector
            def _(dve):
                ch = Chain(dve, s["lb_order"])
                dve.wait_ge(s["par_in"], 48)
                ch(dve.tensor_tensor(lm[:], l0[:], l1[:], ALU.max))
                dve.tensor_tensor(l0[:], l0[:], lm[:], ALU.subtract)
                ch(dve.tensor_tensor(l1[:], l1[:], lm[:], ALU.subtract))
                dve.wait_ge(s["lb_exp"], 2)
                ch(dve.tensor_tensor(l0[:], l0[:], l1[:], ALU.add))
                ch(dve.reciprocal(l0[:], l0[:]))
                ch(dve.tensor_tensor(lb[:], l1[:], l0[:], ALU.mult))
                ch(dve.tensor_scalar(lb1[:], lb[:], -1.0, 1.0, ALU.mult, ALU.add))
                dve.wait_ge(s["masks_made"], n_masks)

                def link(ins):
                    ins.then_inc(s["order"], 1)
                    take(dve, s["order"])

                for b in range(2):
                    dve.sem_inc(gram_free[b], 1)
                dve.sem_inc(s["tail_free"], 1)
                dve.sem_inc(s["head_done"], 1)
                link(dve.memset(ST[:, 0, :], 0.0))

                def pick(lv):
                    m = c.ident[:] if lv is None else mask[:, lv, :]
                    for b in range(2):
                        take(dve, gram_done[b])
                        link(dve.copy_predicated(SC[:, 4 * b:4 * b + 4, :], bcast(m.bitcast(U32), 1, 4),
                                                 ps[:, 4 + b, :].rearrange("p (n t) -> p n t", n=4)))
                        dve.sem_inc(gram_free[b], 1)

                def diff(lv):
                    v, hw = level_view(BC[:], lv), HLEVELS[lv]
                    ref = v[:, :, hw - 1:hw].to_broadcast([P, S // (2 * hw), 2 * hw])
                    dve.tensor_tensor(level_view(E[:, lv % 4, :], lv), v, ref, ALU.subtract).then_inc(s["diff_ready"], 1)

                def scale(lv, par):
                    take(dve, s["exp_ready"])
                    v, hw = level_view(E[:, lv % 4, :], lv), HLEVELS[lv]
                    kv, qv = level_view(K[:], lv), level_view(Q[:, par, :], lv)
                    link(dve.tensor_tensor(v[:, :, 0:hw], v[:, :, 0:hw], kv[:, :, 0:hw], ALU.mult))
                    dve.tensor_tensor(v[:, :, hw:2 * hw], v[:, :, hw:2 * hw], qv[:, :, hw:2 * hw], ALU.mult).then_inc(s["level_ready"], 1)

                def half(h, par):
                    take(dve, s["head_ready"])
                    link(dve.tensor_scalar(F[:, par, :], F[:, par, :], col(lb1, h), col(lb, h), ALU.mult, ALU.add))
                    link(dve.tensor_scalar(K[:], F[:, par, :], -1.0, 1.0, ALU.mult, ALU.add))
                    dve.sem_inc(s["fg_ready"], 1)
                    dve.sem_inc(s["k_ready"], 1)
                    link(dve.memset(SC[:], 0.0))
                    take(dve, s["lf_ready"])
                    link(dve.tensor_tensor_scan(BC[:], reset[:], F[:, par, :], 0.0, ALU.mult, ALU.add))
                    dve.sem_inc(s["bc_ready"], 1)
                    diff(0)
                    pick(None)
                    diff(1)
                    scale(0, par)
                    for lv in range(2, NL):
                        diff(lv)
                        scale(lv - 1, par)
                        pick(lv - 2)
                    bc = BC[:].rearrange("p (n q) -> p n q", q=P)
                    dve.tensor_tensor(KD[:].rearrange("p (n q) -> p n q", q=P), bc[:, :, P - 1:P].to_broadcast([P, TT, P]), bc,
                                      ALU.subtract).then_inc(s["diff_ready"], 1)
                    scale(NL - 1, par)
                    pick(NL - 2)
                    pick(NL - 1)
                    take(dve, s["exp_ready"])
                    dve.tensor_tensor(KD[:], KD[:], K[:], ALU.mult).then_inc(s["kd_ready"], 1)
                    take(dve, s["exp_ready"])
                    dve.tensor_tensor(QE[:], QE[:], Q[:, par, :], ALU.mult).then_inc(s["qe_ready"], 1)
                    take(dve, s["ds_done"])
                    take(dve, s["step_ready"])
                    for n in range(TT - 1):
                        link(dve.scalar_tensor_tensor(out=ST[:, n + 1, :], in0=ST[:, n, :], scalar=step[:, n:n + 1],
                                                      in1=ps[:, 6 + n // 4, (n % 4) * P:(n % 4 + 1) * P], op0=ALU.mult, op1=ALU.add))
                    dve.sem_inc(s["s_ready"], 1)
                    take(dve, s["sq_summed"])
                    link(dve.tensor_scalar(F[:, par, :], pair(ps[:, 6:8, :]), 1.0 / P, EPS, ALU.mult, ALU.add))
                    dve.sem_inc(s["var_ready"], 1)
                    dve.sem_inc(s["tail_free"], 1)
                    take(dve, s["rstd_ready"])
                    link(dve.scalar_tensor_tensor(out=F[:, par, :], in0=pair(ps[:, 4:6, :]), scalar=col(nw, h), in1=F[:, par, :],
                                                  op0=ALU.mult, op1=ALU.mult))
                    for b in range(2):
                        dve.sem_inc(gram_free[b], 1)
                    link(dve.tensor_tensor(y_T[:, bass.ds(h, 1), :], F[:, par:par + 1, :], G[:, par:par + 1, :], ALU.mult))
                    dve.sem_inc(s["head_done"], 1)

                with dve.Fori(0, HEADS // 2) as i:
                    half(2 * i, 0)
                    half(2 * i + 1, 1)


def finish(nc, c, gain, out):
    norm(nc, c, gain, rows=out)


class Chip:
    pass


def trunk(nc, a, out):
    c = Chip()
    with ExitStack() as ctx:
        def sb(name, shape, dt=F32):
            return ctx.enter_context(nc.sbuf_tensor(name, shape, dt))

        c.ctx = ctx
        c.res = sb("residual", [P, TT, D])
        c.ident = sb("ident", [P, P])
        c.ones = sb("ones", [P, P])
        c.ps = ctx.enter_context(nc.psum_tensor("ps", [P, 8, HALF], F32))
        c.rows = nc.dram_tensor("h_rows", [S, D], F32).ap()
        c.row_tok = nc.dram_tensor("row_token", [(NBLK + 1) * P, 1], I32).ap()
        c.ys = nc.dram_tensor("expert_rows", [(NBLK + 1) * P, D], F32).ap()
        with nc.sbuf_tensor("head_ones", [P, P], F32) as c.head_ones, nc.sbuf_tensor("proj", [P, AB_TILES, S], F32) as proj:
            load_x(nc, c, a["x"])
            with nc.sbuf_tensor("h_T", [P, KT, S], F32) as h_T:
                norm(nc, c, a["norm_mix"][0], h_T=h_T)
                project_ab(nc, c, a["ab_w_in"][0], a["rw_mu"][0], h_T, proj)
            lru(nc, c, a, proj)
            with ExitStack() as mix:
                def mb(name, shape):
                    return mix.enter_context(nc.sbuf_tensor(name, shape, F32))

                b = Chip()
                b.ln_w, b.ln_b = mb("ln_w", [P, NPAIR]), mb("ln_b", [P, NPAIR])
                b.step = mb("step", [P, NPAIR, NCH])
                b.g2 = mb("g2", [P, W_RW])
                b.bufs = [mb(f"mix{i}", [P, NPAIR, S]) for i in range(3)]
                with (nc.sbuf_tensor("mix3", [P, NPAIR, S], F32) as m3, nc.sbuf_tensor("mix4", [P, NPAIR, S], F32) as m4,
                      nc.sbuf_tensor("w2a2", [P, W_RW], F32) as b.w2a2):
                    b.bufs = [b.bufs[0], b.bufs[1], m3, b.bufs[2], m4]
                    rwkv_prepare(nc, c, a, proj, b)
                c.lower_1, c.upper, c.strict_incl = mb("lower_1", [P, HD]), mb("upper", [P, len(LEVELS), HD]), mb("strict_incl", [P, 2, HD])
                b.ident64 = mb("ident64", [P, HD])
                make_chunk_masks(nc, c, b)
                rwkv_chunks(nc, c, proj, b)
                rwkv_finish(nc, c, proj, b)
            project_out(nc, c, a["ab_w_out"][0], [proj[:, T_R:T_R + 4, :], proj[:, T_GATE:T_GATE + 4, :]])
        moe(nc, c, a, 0)
        with nc.sbuf_tensor("y_T", [P, KT, S], F32) as y_T:
            with nc.sbuf_tensor("h_T_1", [P, KT, S], F32) as h_T:
                norm(nc, c, a["norm_mix"][1], h_T=h_T)
                hgrn(nc, c, a["c_w_in"][0], a["c_lower_bound"], a["c_norm_w"][0], h_T, y_T)
            project_out(nc, c, a["c_w_out"][0], [y_T[:]])
        moe(nc, c, a, 1)
        finish(nc, c, a["norm_final"], out)


_INS = ["x", "norm_mix", "norm_ffn", "norm_final", "ab_w_in", "rw_mu", "rw_w0", "rw_w2", "rw_a0", "rw_a2", "rw_g2",
        "rw_k_k", "rw_k_a", "rw_r_k", "rw_ln_w", "rw_ln_b", "lru_conv_w", "lru_conv_b", "lru_w_a", "lru_b_a",
        "lru_w_x", "lru_b_x", "lru_lambda", "ab_w_out", "c_w_in", "c_lower_bound", "c_norm_w", "c_w_out",
        "moe_w_group", "moe_b_group", "moe_w_expert", "moe_b_expert", "moe_w_gate", "moe_w_up", "moe_w_down"]


def kernel(**inputs):
    import numpy as np
    import concourse.bacc as bacc
    from concourse.bass_utils import run_bass_kernel_spmd

    nc = bacc.Bacc("TRN2", target_bir_lowering=False, num_devices=1)
    arrays, aps = {}, {}
    for name in _INS:
        v = np.ascontiguousarray(inputs[name])
        if name == "x":
            v = v.reshape(S, D)
        arrays["in_" + name] = v
        aps[name] = nc.dram_tensor("in_" + name, v.shape, mybir.dt.from_np(v.dtype), kind="ExternalInput").ap()
    out = nc.dram_tensor("out_y", [S, D], F32, kind="ExternalOutput").ap()
    with nc.allow_non_contiguous_dma(reason="per-channel vectors of a few KB"):
        trunk(nc, aps, out)
    got = run_bass_kernel_spmd(nc, [arrays], core_ids=[0])
    return got.results[0]["out_y"].reshape(1, S, D)
```

```python
from contextlib import ExitStack, contextmanager

import concourse.bass as bass
from concourse import mybir

F32 = mybir.dt.float32
F32R = mybir.dt.float32r
I32 = mybir.dt.int32
U32 = mybir.dt.uint32
ALU = mybir.AluOpType
ACT = mybir.ActivationFunctionType
AX = mybir.AxisListType

P = 128
D = 1024
S = 1024
KT = D // P
TT = S // P
HALF = 512
NH = S // HALF
EPS = 1e-6

W_RW = D // 2
NPAIR = W_RW // P
HD = 64
GN_EPS = 64e-5
AB_COLS = 3 * W_RW + 64 + 64 + 128 + D
AB_TILES = AB_COLS // P
T_R, T_K, T_V, T_WA, T_G, T_GATE, T_XB = 0, 4, 8, 12, 13, 14, 18
NCH = S // HD
LEVELS = (1, 2, 4, 8, 16, 32)

HEADS = 8
HLEVELS = (64, 32, 16, 8, 4, 2, 1)

NG, EPG, NE, FF = 4, 8, 32, 512
NBLK = 2 * S // P + NE
BIG = 1.0e30


def take(eng, sem, n=1):
    eng.wait_ge(sem, n)
    eng.sem_inc(sem, -n)


class Chain:

    def __init__(self, eng, sem):
        self.eng, self.sem, self.n = eng, sem, 0

    def __call__(self, ins):
        self.n += 1
        ins.then_inc(self.sem, 1)
        self.eng.wait_ge(self.sem, self.n)


@contextmanager
def phase(nc, c):
    with ExitStack() as ctx:
        sems, tag = [], nc.next_id()

        def sem(name, by_pool_dma=False):
            if by_pool_dma:
                return c.ctx.enter_context(nc.semaphore(f"{name}_{tag}"))
            s = ctx.enter_context(nc.semaphore(name))
            sems.append(s)
            return s

        def sb(name, shape, dt=F32):
            return ctx.enter_context(nc.sbuf_tensor(f"{name}_{tag}", shape, dt))

        yield sem, sb
        with nc.Block() as block:

            @block.gpsimd
            def _(pool):
                for s in sems:
                    pool.sem_clear(s)


def bcast(ap, axis, n):
    ap = ap.unsqueeze(axis)
    shape = list(ap.shape)
    shape[axis] = n
    return ap.to_broadcast(shape)


def column(vec, lo=0, n=None):
    n = vec.shape[0] if n is None else n
    return vec[lo:lo + n].rearrange("(j p) -> p j", p=P)


def load_x(nc, c, x):
    with phase(nc, c) as (sem, sb):
        x_in, made = sem("x_in"), sem("made")
        with nc.Block() as block:

            @block.sync
            def _(sp):
                for t in range(TT):
                    sp.dma_start(c.res[:, t, :], x[t * P:(t + 1) * P, :]).then_inc(x_in, 16)
                sp.wait_ge(x_in, 16 * TT)

            @block.gpsimd
            def _(pool):
                ch = Chain(pool, made)
                ch(pool.memset(c.ident[:], 1.0))
                ch(pool.affine_select(out=c.ident[:], in_=c.ident[:], pattern=[[-1, P]], compare_op=ALU.is_equal,
                                      fill=0.0, base=0, channel_multiplier=1))
                ch(pool.memset(c.ones[:], 1.0))
                ch(pool.memset(c.head_ones[:], 0.0))
                for p in (0, HD):
                    ch(pool.memset(c.head_ones[p:p + HD, p:p + HD], 1.0))


def norm(nc, c, gain, h_T=None, rows=None, h_low=None, scratch=None):
    with phase(nc, c) as (sem, sb):
        gain_in, squared, var_ready, std_ready, hn_ready = (
            sem(n) for n in ("gain_in", "squared", "var_ready", "std_ready", "hn_ready"))
        turned, copied, stored, order = sem("turned"), sem("copied"), sem("stored"), sem("order")
        low_done = sem("low_done")
        hn = sb("hn", [P, TT, D]) if scratch is None else scratch
        gb = sb("gain_rows", [P, D])
        ss = sb("square_sums", [P, TT])
        var = sb("var", [P, TT])
        std = sb("std", [P, TT])
        rstd = sb("rstd", [P, TT])
        ps = c.ps
        with nc.Block() as block:

            @block.sync
            def _(sp):
                sp.dma_start(gb[:], gain.partition_broadcast(P)).then_inc(gain_in, 16)
                if rows is not None:
                    for t in range(TT):
                        sp.wait_ge(hn_ready, t + 1)
                        sp.dma_start(rows[t * P:(t + 1) * P, :], hn[:, t, :]).then_inc(stored, 16)
                    sp.wait_ge(stored, 16 * TT)

            @block.scalar
            def _(act):
                for t in range(TT):
                    act.activation(hn[:, t, :], c.res[:, t, :], ACT.Square, accum_out=ss[:, t:t + 1]).then_inc(squared, 1)
                act.wait_ge(var_ready, 1)
                act.activation(std[:], var[:], ACT.Sqrt).then_inc(std_ready, 1)
                if h_T is not None:
                    for t in range(TT):
                        for h in range(2):
                            act.wait_ge(turned, 2 * t + h + 1)
                            act.copy(h_T[:, 4 * h:4 * h + 4, t * P:(t + 1) * P],
                                     ps[:, 2 * (t % 2) + h, :].rearrange("p (k n) -> p k n", k=4)).then_inc(copied, 1)

            @block.vector
            def _(dve):
                ch = Chain(dve, order)

                def low_parts(t):
                    for h in range(2):
                        dve.wait_ge(copied, 2 * t + h + 1)
                        tok = slice(t * P, (t + 1) * P)
                        dve.tensor_tensor(h_low[:, 4 * h:4 * h + 4, tok], ps[:, 2 * (t % 2) + h, :].rearrange("p (k n) -> p k n", k=4),
                                          h_T[:, 4 * h:4 * h + 4, tok].bitcast(F32), ALU.subtract).then_inc(low_done, 1)

                dve.wait_ge(squared, TT)
                dve.tensor_scalar(var[:], ss[:], 1.0 / D, EPS, ALU.mult, ALU.add).then_inc(var_ready, 1)
                dve.wait_ge(std_ready, 1)
                ch(dve.reciprocal(rstd[:], std[:]))
                dve.wait_ge(gain_in, 16)
                for t in range(TT):
                    dve.scalar_tensor_tensor(out=hn[:, t, :], in0=c.res[:, t, :], scalar=rstd[:, t:t + 1], in1=gb[:],
                                             op0=ALU.mult, op1=ALU.mult).then_inc(hn_ready, 1)
                    if h_low is not None and t:
                        low_parts(t - 1)
                if h_low is not None:
                    low_parts(TT - 1)

            @block.tensor
            def _(pe):
                if h_T is None:
                    return
                for t in range(TT):
                    pe.wait_ge(hn_ready, t + 1)
                    for h in range(2):
                        if t >= 2:
                            pe.wait_ge(copied if h_low is None else low_done, 2 * (t - 2) + h + 1)
                        for k in range(4):
                            last = pe.transpose(ps[:, 2 * (t % 2) + h, k * P:(k + 1) * P],
                                                hn[:, t, (4 * h + k) * P:(4 * h + k + 1) * P], c.ident[:])
                        last.then_inc(turned, 1)


def project_ab(nc, c, w, mu, h_T, h_low, proj):
    w_t = w.rearrange("(k p) m -> p k m", p=P)
    with phase(nc, c) as (sem, sb):
        w_in, high_made, low_made, w_ready = sem("w_in"), sem("high_made"), sem("low_made"), sem("w_ready")
        w_free, summed = sem("w_free"), [sem("summed_a"), sem("summed_v")]
        bank_free = [sem("bank_free_a"), sem("bank_free_v")]
        order, order_a, first_copied, mu_in = sem("order"), sem("order_a"), sem("first_copied"), sem("mu_in")
        wt = sb("w_tiles", [P, KT, P])
        wh, wl = sb("w_high", [P, 2, KT, P], F32R), sb("w_low", [P, 2, KT, P], F32R)
        mu_t = sb("mu", [P, T_GATE])
        shift = proj[:, AB_TILES - 1:AB_TILES, :]
        ps = c.ps
        cleared, zero_made = sem("cleared", True), sem("zero_made")
        zero = sb("zero_rows", [P, HALF])
        with nc.Block() as block:

            @block.gpsimd
            def _(pool):
                pool.memset(zero[:], 0.0).then_inc(zero_made, 1)
                pool.wait_ge(zero_made, 1)
                for n in range(NBLK + 1):
                    for h in range(2):
                        pool.dma_start(c.ys[n * P:(n + 1) * P, h * HALF:(h + 1) * HALF], zero[:]).then_inc(cleared, 16)
                pool.wait_ge(cleared, 32 * (NBLK + 1))

            @block.sync
            def _(sp):
                sp.dma_start(mu_t[:], column(mu)).then_inc(mu_in, 16)
                with sp.Fori(0, AB_TILES // 2) as i:
                    for q in range(2):
                        sp.dma_start(wt[:], w_t[:, :, bass.ds(i * (2 * P) + q * P, P)]).then_inc(w_in, 16)
                        take(sp, low_made)
                        sp.sem_inc(w_ready, 1)

            @block.tensor
            def _(pe):
                with pe.Fori(0, AB_TILES // 2):
                    for q in range(2):
                        take(pe, w_ready)
                        for h in range(NH):
                            take(pe, bank_free[h])
                            half = slice(h * HALF, (h + 1) * HALF)
                            parts = [(wx, hx, k) for k in range(KT) for wx, hx in ((wh, h_T), (wl, h_T), (wh, h_low))]
                            for n, (wx, hx, k) in enumerate(parts):
                                last = pe.matmul(ps[:, 2 * q + h, :], wx[:, q, k, :], hx[:, k, half],
                                                 start=n == 0, stop=n == len(parts) - 1)
                            last.then_inc(summed[h], 1)
                        pe.drain().then_inc(w_free, 1)

            @block.scalar
            def _(act):
                def high(q):
                    take(act, w_in, 16)
                    take(act, w_free)
                    act.copy(wh[:, q], wt[:]).then_inc(high_made, 1)

                def out(i, q):
                    take(act, summed[0])
                    act.copy(proj[:, bass.ds(2 * i + q, 1), 0:HALF], ps[:, 2 * q:2 * q + 1, :]).then_inc(order_a, 1)
                    take(act, order_a)
                    act.sem_inc(bank_free[0], 1)
                    act.sem_inc(first_copied, 1)

                act.sem_inc(bank_free[0], 2)
                act.sem_inc(w_free, 2)
                high(0)
                high(1)
                with act.Fori(0, AB_TILES // 2 - 1) as i:
                    for q in range(2):
                        out(i, q)
                        high(q)
                for q in range(2):
                    out(AB_TILES // 2 - 1, q)

            @block.vector
            def _(dve):
                def link(ins):
                    ins.then_inc(order, 1)
                    take(dve, order)

                dve.wait_ge(mu_in, 16)
                dve.sem_inc(bank_free[1], 2)

                def low(q):
                    take(dve, high_made)
                    dve.tensor_tensor(wl[:, q], wt[:], wh[:, q].bitcast(F32), ALU.subtract).then_inc(low_made, 1)

                def out(i, q, shifted):
                    take(dve, summed[1])
                    m = bass.ds(2 * i + q, 1)
                    dve.tensor_copy(proj[:, m, HALF:S], ps[:, 2 * q + 1:2 * q + 2, :]).then_inc(order, 1)
                    take(dve, order)
                    dve.sem_inc(bank_free[1], 1)
                    take(dve, first_copied)
                    if shifted:
                        link(dve.tensor_tensor(shift[:, :, 1:S], proj[:, m, 0:S - 1], proj[:, m, 1:S], ALU.subtract))
                        link(dve.tensor_scalar(shift[:, :, 0:1], proj[:, m, 0:1], -1.0, None, ALU.mult))
                        link(dve.scalar_tensor_tensor(out=proj[:, m, :], in0=shift, scalar=mu_t[:, m], in1=proj[:, m, :],
                                                      op0=ALU.mult, op1=ALU.add))

                low(0)
                low(1)
                for shifted, lo, hi in ((True, 0, T_GATE // 2), (False, T_GATE // 2, AB_TILES // 2 - 1)):
                    with dve.Fori(lo, hi) as i:
                        for q in range(2):
                            out(i, q, shifted)
                            low(q)
                for q in range(2):
                    out(AB_TILES // 2 - 1, q, False)


def lru(nc, c, a, proj):
    gate, xb = proj[:, T_GATE:T_GATE + 4, :], proj[:, T_XB:T_XB + 4, :]
    w_a = a["lru_w_a"][0].rearrange("(j p) d e -> (p d) j e", p=2)
    w_x = a["lru_w_x"][0].rearrange("(j p) d e -> (p d) j e", p=2)
    with phase(nc, c) as (sem, sb):
        names = ("par_in", "order", "exp_lam", "lam_ready", "conv_done", "gates_summed", "gates_done", "i_done",
                 "decay_done", "tanh_done", "log_done", "inverse_done", "power_ready", "root_done", "gelu_done", "bank_free")
        s = {n: sem(n) for n in names}
        wa, wx = sb("lru_wa", [P, 4, HD]), sb("lru_wx", [P, 4, HD])
        cw, cb = sb("conv_w", [P, 4, 4]), sb("conv_b", [P, 4])
        ba, bx, lam = sb("b_a", [P, 4]), sb("b_x", [P, 4]), sb("lam", [P, 4])
        neg, y, z, z2, ser, rate, nrate = (sb(n, [P, 4]) for n in ("lam_neg", "lam_y", "lam_z", "lam_z2", "lam_ser", "rate", "nrate"))
        xc, rr, ii, dec = (sb(n, [P, 4, S]) for n in ("conv", "r_gate", "i_gate", "decay"))
        ps = c.ps
        with nc.Block() as block:

            @block.sync
            def _(sp):
                sp.dma_start(wa[:], w_a).then_inc(s["par_in"], 16)
                sp.dma_start(wx[:], w_x).then_inc(s["par_in"], 16)
                for i in range(4):
                    sp.dma_start(cw[:, i, :], column(a["lru_conv_w"][0, i])).then_inc(s["par_in"], 16)
                for t, v in ((cb, "lru_conv_b"), (ba, "lru_b_a"), (bx, "lru_b_x"), (lam, "lru_lambda")):
                    sp.dma_start(t[:], column(a[v][0])).then_inc(s["par_in"], 16)
                sp.wait_ge(s["par_in"], 160)

            @block.vector
            def _(dve):
                ch = Chain(dve, s["order"])
                dve.wait_ge(s["par_in"], 160)
                ch(dve.tensor_scalar(neg[:], lam[:], -1.0, None, ALU.mult))
                dve.tensor_tensor(z[:], lam[:], neg[:], ALU.max).then_inc(s["lam_ready"], 1)
                dve.wait_ge(s["exp_lam"], 1)
                ch(dve.tensor_scalar(z[:], y[:], 2.0, None, ALU.add))
                ch(dve.reciprocal(z2[:], z[:]))
                ch(dve.tensor_tensor(z[:], y[:], z2[:], ALU.mult))
                ch(dve.tensor_tensor(z2[:], z[:], z[:], ALU.mult))
                ch(dve.tensor_scalar(ser[:], z2[:], 1.0 / 17, None, ALU.mult))
                for k in range(7, 0, -1):
                    ch(dve.scalar_tensor_tensor(out=ser[:], in0=ser[:], scalar=1.0 / (2 * k + 1), in1=z2[:],
                                                op0=ALU.add, op1=ALU.mult))
                ch(dve.scalar_tensor_tensor(out=ser[:], in0=ser[:], scalar=1.0, in1=z[:], op0=ALU.add, op1=ALU.mult))
                ch(dve.tensor_scalar(neg[:], neg[:], 0.0, None, ALU.max))
                ch(dve.scalar_tensor_tensor(out=ser[:], in0=ser[:], scalar=2.0, in1=neg[:], op0=ALU.mult, op1=ALU.add))
                ch(dve.tensor_scalar(rate[:], ser[:], -8.0, None, ALU.mult))
                dve.tensor_scalar(nrate[:], ser[:], 8.0, None, ALU.mult).then_inc(s["lam_ready"], 1)
                for j in range(4):
                    ch(dve.tensor_scalar(xc[:, j, :], xb[:, j, :], cw[:, 3, j:j + 1], cb[:, j:j + 1], ALU.mult, ALU.add))
                for d in range(1, 4):
                    for j in range(4):
                        ins = dve.scalar_tensor_tensor(out=xc[:, j, d:S], in0=xb[:, j, 0:S - d], scalar=cw[:, 3 - d, j:j + 1],
                                                       in1=xc[:, j, d:S], op0=ALU.mult, op1=ALU.add)
                        if d < 3:
                            ch(ins)
                        else:
                            ins.then_inc(s["conv_done"], 1)
                for j in range(4):
                    dve.wait_ge(s["inverse_done"], j + 1)
                    dve.scalar_tensor_tensor(out=rr[:, j, :], in0=rr[:, j, :], scalar=2.0, in1=xb[:, j, :],
                                             op0=ALU.mult, op1=ALU.mult).then_inc(s["power_ready"], 1)
                for j in range(4):
                    dve.wait_ge(s["i_done"], j + 1)
                    ch(dve.tensor_tensor(ii[:, j, :], ii[:, j, :], xc[:, j, :], ALU.mult))
                for j in range(4):
                    dve.wait_ge(s["root_done"], j + 1)
                    ch(dve.tensor_tensor(ii[:, j, :], ii[:, j, :], rr[:, j, :], ALU.mult))
                    ch(dve.tensor_tensor_scan(xc[:, j, :], dec[:, j, :], ii[:, j, :], 0.0, ALU.mult, ALU.add))
                    dve.wait_ge(s["gelu_done"], j + 1)
                    ch(dve.tensor_tensor(gate[:, j, :], gate[:, j, :], xc[:, j, :], ALU.mult))

            @block.tensor
            def _(pe):
                pe.wait_ge(s["par_in"], 160)
                for j in range(4):
                    pe.wait_ge(s["conv_done"], j + 1)
                    if j >= 2:
                        pe.wait_ge(s["gates_done"], j - 1)
                        pe.wait_ge(s["i_done"], j - 1)
                    for g, w in ((0, wa), (1, wx)):
                        for h in range(NH):
                            for p in (0, HD):
                                last = pe.matmul(ps[p:p + HD, 4 * (j % 2) + 2 * g + h, :], w[p:p + HD, j, :],
                                                 xc[p:p + HD, j, h * HALF:(h + 1) * HALF], start=True, stop=True)
                    last.then_inc(s["gates_summed"], 1)

            @block.scalar
            def _(act):
                act.wait_ge(s["lam_ready"], 1)
                act.activation(y[:], z[:], ACT.Exp, scale=-1.0).then_inc(s["exp_lam"], 1)
                for j in range(4):
                    act.wait_ge(s["gates_summed"], j + 1)
                    b = 4 * (j % 2)
                    act.activation(rr[:, j, :], ps[:, b:b + 2, :].rearrange("p h n -> p (h n)"), ACT.Sigmoid,
                                   bias=ba[:, j:j + 1]).then_inc(s["gates_done"], 1)
                    act.activation(ii[:, j, :], ps[:, b + 2:b + 4, :].rearrange("p h n -> p (h n)"), ACT.Sigmoid,
                                   bias=bx[:, j:j + 1]).then_inc(s["i_done"], 1)
                act.wait_ge(s["lam_ready"], 2)
                for j in range(4):
                    act.wait_ge(s["gates_done"], j + 1)
                    act.activation(dec[:, j, :], rr[:, j, :], ACT.Exp, scale=rate[:, j:j + 1]).then_inc(s["decay_done"], 1)
                for j in range(4):
                    act.wait_ge(s["decay_done"], j + 1)
                    act.activation(rr[:, j, :], rr[:, j, :], ACT.Tanh, scale=nrate[:, j:j + 1]).then_inc(s["tanh_done"], 1)
                for j in range(4):
                    act.wait_ge(s["tanh_done"], j + 1)
                    act.activation(xb[:, j, :], rr[:, j, :], ACT.Ln, bias=c.ones[:, 0:1]).then_inc(s["log_done"], 1)
                for j in range(4):
                    act.wait_ge(s["log_done"], j + 1)
                    act.activation(xb[:, j, :], xb[:, j, :], ACT.Exp, scale=-1.0).then_inc(s["inverse_done"], 1)
                for j in range(4):
                    act.activation(gate[:, j, :], gate[:, j, :], ACT.Gelu_apprx_tanh).then_inc(s["gelu_done"], 1)
                for j in range(4):
                    act.wait_ge(s["power_ready"], j + 1)
                    act.activation(rr[:, j, :], rr[:, j, :], ACT.Sqrt).then_inc(s["root_done"], 1)


def rwkv_prepare(nc, c, a, proj, b):
    r, k, v = (proj[:, t:t + 4, :] for t in (T_R, T_K, T_V))
    kk = proj[:, T_XB:T_XB + 4, :]
    B0, B1, B2, B3, B4 = b.bufs
    flat = lambda t: t.rearrange("p j s -> p (j s)")
    chunked = lambda t: t.rearrange("p j (n q) -> p (j n) q", q=HD)
    with phase(nc, c) as (sem, sb):
        names = ("par_in", "order", "order_a", "tanh_done", "z_summed", "z_done", "a_summed", "a_done", "cum_ready",
                 "kk_ready", "kk_squared", "kk_summed", "kk_max", "kk_root",
                 "exp_done", "mask_made", "step_ready", "step_done")
        s = {n: sem(n) for n in names}
        w2, a2, g2 = b.w2a2, b.w2a2, b.g2
        th = proj[:, T_WA, :]
        reset = B4[:, 0, :]
        w0, a0, k_k, k_a, k_a1 = (sb(n, [P, 4]) for n in ("w0", "a0", "k_k", "k_a", "one_minus_k_a"))
        mid, end, tmp = (sb(n, [P, 4, NCH]) for n in ("cum_mid", "cum_end", "step_log"))
        ps = c.ps

        with nc.Block() as block:

            @block.sync
            def _(sp):
                sp.dma_start(w2[0:HD, :], a["rw_w2"][0]).then_inc(s["par_in"], 16)
                sp.dma_start(a2[HD:P, :], a["rw_a2"][0]).then_inc(s["par_in"], 16)
                sp.dma_start(g2[:], a["rw_g2"][0]).then_inc(s["par_in"], 16)
                for t, n in ((w0, "rw_w0"), (a0, "rw_a0"), (k_k, "rw_k_k"), (k_a, "rw_k_a"), (b.ln_w, "rw_ln_w"), (b.ln_b, "rw_ln_b")):
                    sp.dma_start(t[:], column(a[n][0])).then_inc(s["par_in"], 16)
                sp.dma_start(b.r_k[:], a["rw_r_k"][0].rearrange("(j h) n -> (h n) j", h=2)).then_inc(s["par_in"], 16)
                sp.wait_ge(s["par_in"], 160)

            @block.gpsimd
            def _(pool):
                ch = Chain(pool, s["mask_made"])
                ch(pool.memset(reset, 1.0))
                ch(pool.memset(reset.rearrange("p (n q) -> p n q", q=HD)[:, :, 0:1], 0.0))

            @block.scalar
            def _(act):
                ch = Chain(act, s["order_a"])
                act.wait_ge(s["par_in"], 160)
                act.activation(th[0:HD, :], proj[0:HD, T_WA, :], ACT.Tanh).then_inc(s["tanh_done"], 1)
                ch(act.activation(proj[:, T_G, :], proj[:, T_G, :], ACT.Sigmoid))
                for j in range(4):
                    q = j % 2
                    act.wait_ge(s["z_summed"], j + 1)
                    act.activation(B0[:, j, :], ps[:, 2 * q:2 * q + 2, :].rearrange("p h n -> p (h n)"), ACT.Sigmoid,
                                   bias=w0[:, j:j + 1]).then_inc(s["z_done"], 1)
                    act.wait_ge(s["a_summed"], j + 1)
                    act.activation(B1[:, j, :], ps[:, 4 + 2 * q:6 + 2 * q, :].rearrange("p h n -> p (h n)"), ACT.Sigmoid,
                                   bias=a0[:, j:j + 1]).then_inc(s["a_done"], 1)
                act.wait_ge(s["kk_ready"], 1)
                act.activation(flat(B3[:]), flat(kk), ACT.Square).then_inc(s["kk_squared"], 1)
                act.wait_ge(s["kk_max"], 1)
                ch(act.activation(flat(B3[:]), flat(B3[:]), ACT.Ln))
                act.activation(flat(B3[:]), flat(B3[:]), ACT.Exp, scale=-0.5).then_inc(s["kk_root"], 1)
                act.wait_ge(s["step_ready"], 1)
                act.activation(b.step[:].rearrange("p j n -> p (j n)"), tmp[:].rearrange("p j n -> p (j n)"), ACT.Exp).then_inc(s["step_done"], 1)
                act.wait_ge(s["cum_ready"], 2)
                act.activation(flat(B4[:]), flat(B2[:]), ACT.Exp, scale=-1.0).then_inc(s["exp_done"], 1)
                act.activation(flat(B3[:]), flat(B3[:]), ACT.Exp).then_inc(s["exp_done"], 1)
                act.wait_ge(s["exp_done"], 1)
                act.activation(flat(B2[:]), flat(B2[:]), ACT.Exp).then_inc(s["exp_done"], 1)
                act.wait_ge(s["step_done"], 1)

            @block.tensor
            def _(pe):
                pe.wait_ge(s["par_in"], 160)
                pe.wait_ge(s["tanh_done"], 1)
                for j in range(4):
                    q = j % 2
                    if j >= 2:
                        pe.wait_ge(s["z_done"], j - 1)
                        pe.wait_ge(s["a_done"], j - 1)
                    for h in range(NH):
                        last = pe.matmul(ps[:, 2 * q + h, :], w2[0:HD, j * P:(j + 1) * P], th[0:HD, h * HALF:(h + 1) * HALF],
                                         start=True, stop=True)
                    last.then_inc(s["z_summed"], 1)
                    for h in range(NH):
                        last = pe.matmul(ps[:, 4 + 2 * q + h, :], a2[HD:P, j * P:(j + 1) * P],
                                         proj[HD:P, T_WA, h * HALF:(h + 1) * HALF], start=True, stop=True)
                    last.then_inc(s["a_summed"], 1)
                pe.wait_ge(s["kk_squared"], 1)
                pe.wait_ge(s["z_done"], 4)
                pe.wait_ge(s["a_done"], 4)
                for j in range(4):
                    for h in range(NH):
                        last = pe.matmul(ps[:, 2 * j + h, :], c.head_ones[:], B3[:, j, h * HALF:(h + 1) * HALF], start=True, stop=True)
                last.then_inc(s["kk_summed"], 1)

            @block.vector
            def _(dve):
                ch = Chain(dve, s["order"])
                dve.wait_ge(s["par_in"], 160)
                ch(dve.tensor_scalar(k_a1[:], k_a[:], -1.0, 1.0, ALU.mult, ALU.add))
                for j in range(4):
                    ch(dve.tensor_scalar(kk[:, j, :], k[:, j, :], k_k[:, j:j + 1], None, ALU.mult))
                dve.sem_inc(s["kk_ready"], 1)
                dve.wait_ge(s["z_done"], 4)
                ch(dve.tensor_scalar(flat(B0[:]), flat(B0[:]), -0.6065306597126334, None, ALU.mult))
                dve.wait_ge(s["mask_made"], 2)
                for j in range(4):
                    ch(dve.tensor_tensor_scan(B2[:, j, :], reset, B0[:, j, :], 0.0, ALU.mult, ALU.add))
                cum = B2[:].rearrange("p j (n q) -> p j n q", q=HD)
                ch(dve.tensor_copy(mid[:], cum[:, :, :, HD // 2 - 1]))
                ch(dve.tensor_copy(end[:], cum[:, :, :, HD - 1]))
                ch(dve.tensor_tensor(tmp[:], end[:], mid[:], ALU.subtract))
                dve.tensor_tensor(tmp[:, :, 0:NCH - 1], tmp[:, :, 0:NCH - 1], mid[:, :, 1:NCH], ALU.add).then_inc(s["step_ready"], 1)
                ch(dve.tensor_tensor(chunked(B2[:]), chunked(B2[:]),
                                     bcast(mid[:].rearrange("p j n -> p (j n)"), 2, HD), ALU.subtract))
                dve.wait_ge(s["kk_summed"], 1)
                dve.tensor_scalar(flat(B3[:]), ps[:].rearrange("p b n -> p (b n)"), 1e-24, None, ALU.max).then_inc(s["kk_max"], 1)
                dve.wait_ge(s["kk_root"], 1)
                ch(dve.tensor_tensor(flat(kk), flat(kk), flat(B3[:]), ALU.mult))
                dve.tensor_tensor(flat(B3[:]), flat(B2[:]), flat(B0[:]), ALU.subtract).then_inc(s["cum_ready"], 2)
                dve.wait_ge(s["a_done"], 4)
                dve.wait_ge(s["cum_ready"], 2)
                for j in range(4):
                    ch(dve.tensor_scalar(B0[:, j, :], B1[:, j, :], k_a[:, j:j + 1], k_a1[:, j:j + 1], ALU.mult, ALU.add))
                ch(dve.tensor_tensor(flat(k), flat(k), flat(B0[:]), ALU.mult))
                ch(dve.tensor_tensor(flat(B1[:]), flat(B1[:]), flat(kk), ALU.mult))
                dve.wait_ge(s["exp_done"], 3)
                ch(dve.tensor_tensor(flat(B1[:]), flat(B1[:]), flat(B4[:]), ALU.mult))
                ch(dve.scalar_tensor_tensor(out=flat(B3[:]), in0=flat(kk), scalar=-1.0, in1=flat(B3[:]), op0=ALU.mult, op1=ALU.mult))
                ch(dve.tensor_tensor(flat(r), flat(r), flat(B2[:]), ALU.mult))
                ch(dve.tensor_tensor(flat(k), flat(k), flat(B4[:]), ALU.mult))


def make_chunk_masks(nc, c, b):
    with phase(nc, c) as (sem, sb):
        made = sem("masks_made")
        with nc.Block() as block:

            @block.gpsimd
            def _(pool):
                ch = Chain(pool, made)
                for p in (0, HD):
                    ch(pool.tensor_copy(b.ident64[p:p + HD, :], c.ident[p:p + HD, p:p + HD]))
                ch(pool.memset(c.lower_1[:], 1.0))
                ch(pool.memset(c.upper[:], 1.0))
                ch(pool.memset(c.strict_incl[:], 1.0))
                for p in (0, HD):
                    def keep(view, pattern, base, mult=0):
                        ch(pool.affine_select(out=view, in_=view, pattern=pattern, compare_op=ALU.is_ge, fill=0.0,
                                              base=base, channel_multiplier=mult))
                    low = c.lower_1[p:p + HD, :].rearrange("p (n h) -> p n h", h=2)
                    keep(low, [[-2, 32], [-1000, 2]], -1, 1)
                    keep(low, [[2, 32], [0, 2]], 1, -1)
                    for i, w in enumerate(LEVELS):
                        up = c.upper[p:p + HD, i, :].rearrange("p (n h q) -> p n h q", h=2, q=w)
                        keep(up, [[-2 * w, HD // (2 * w)], [1000, 2], [0, w]], -1000, 1)
                        keep(up, [[2 * w, HD // (2 * w)], [0, 2], [0, w]], w - 1, -1)
                    keep(c.strict_incl[p:p + HD, 0, :], [[1, HD]], -1, -1)
                    keep(c.strict_incl[p:p + HD, 1, :], [[1, HD]], 0, -1)


def rwkv_chunks(nc, c, proj, b):
    r, k, v = (proj[:, t:t + 4, :] for t in (T_R, T_K, T_V))
    ab, bb = b.bufs[3], b.bufs[1]
    y = ab
    NI = 2 * NPAIR
    NTURN = NCH // 2
    NLV = len(LEVELS) - 1
    W = NPAIR * HD
    with phase(nc, c) as (sem, sb):
        names = ("staged", "turned_done", "tok_ready", "lt_done", "mt_done", "x_first", "t1_done", "t1_copied",
                 "dx_done", "x_next", "s_ready", "u_done", "u_copied", "sa_done", "sa_copied", "ds_done", "y_done",
                 "order", "order_a")
        s = {n: sem(n) for n in names}
        AR = sb("stage_ar", [P, 2, 2, NPAIR, 2, HD])
        tok = sb("row_major", [P, 2, 3, NI, HD])
        XT = sb("x_inv_t", [P, 2, NI, HD])
        spare = proj[:, T_XB:T_XB + 4, :].rearrange("p t s -> p (t s)")
        cut = lambda ap, m: ap.rearrange("p (m i n) -> p m i n", m=m, i=NI)
        LO = cut(spare[:, 0:NLV * NI * HD], NLV)
        RB = [sb("masked_rb", [P, NI, HD])[:], cut(spare[:, NLV * NI * HD:6 * NI * HD], 1)[:, 0]]
        MK = [cut(spare[:, 6 * NI * HD:], 2), cut(proj[:, T_WA, :], 2)]
        BS, KS, VS = (sb(n, [P, 2, NPAIR, HD]) for n in ("stage_b", "stage_k", "stage_v"))
        X, T1 = sb("x_inv", [P, NI, HD]), sb("t1", [P, NI, HD])
        U, SA = (sb(n, [P, 2, NPAIR, HD]) for n in ("u_rows", "sa_rows"))
        SS = sb("state", [P, 2, NPAIR, HD])
        sn = sb("state_sum", [P, NPAIR, HD])
        ps = c.ps
        eye = [c.ident[p:p + HD, p:p + HD] for p in (0, HD)]
        items = [(ci, j) for ci in range(2) for j in range(NPAIR)]
        rows_of = lambda ap: ap.rearrange("p k (i m n) -> p (k i) m n", m=2, n=HD)
        mt_rk, lt_rb = rows_of(ps[:, 0:2, :]), rows_of(ps[:, 3:5, :])
        low = ps[:, 5, :].rearrange("p (i n) -> p i n", n=HD)
        B_TOK, B_T1, B_DX = (0, 1, 2), (2, 5), (3, 4)
        o_y, o_sa, o_ds, o_u = ps[:, 6, 0:W], ps[:, 6, W:2 * W], ps[:, 7, 0:W], ps[:, 7, W:2 * W]
        chunk_items = lambda t, g: t[:, g * NPAIR:(g + 1) * NPAIR, :]

        def halves():
            return ((0, slice(0, HD)), (1, slice(HD, P)))

        def js(j):
            return slice(j * HD, (j + 1) * HD)

        with nc.Block() as block:

            @block.scalar
            def _(act):
                def link(ins):
                    ins.then_inc(s["order_a"], 1)
                    take(act, s["order_a"])

                def stage(turn, f, part):
                    pairs = [(ab, AR[:, f, :, :, 0, :]), (r, AR[:, f, :, :, 1, :]), (bb, BS), (k, KS), (v, VS)]
                    copies = [(src, dst, ci) for src, dst in pairs for ci in range(2)]
                    for src, dst, ci in copies[part::3]:
                        link(act.copy(dst[:, ci], src[:, :, bass.ds(turn * P + ci * HD, HD)]))
                    if part == 2:
                        act.sem_inc(s["staged"], 1)

                def rows_out(f):
                    take(act, s["turned_done"])
                    for m in range(3):
                        link(act.copy(tok[:, f, m].rearrange("p i n -> p (i n)"), ps[:, B_TOK[m], :]))
                    act.sem_inc(s["tok_ready"], 1)

                def t1_out():
                    for g in range(2):
                        take(act, s["t1_done"])
                        act.copy(chunk_items(T1, g).rearrange("p i n -> p (i n)"), ps[:, B_T1[g], 0:W]).then_inc(s["t1_copied"], 1)

                def u_out(ci):
                    take(act, s["u_done"])
                    act.copy(U[:, ci].rearrange("p j n -> p (j n)"), o_u).then_inc(s["u_copied"], 1)

                def sa_out(ci):
                    take(act, s["sa_done"])
                    act.copy(SA[:, ci].rearrange("p j n -> p (j n)"), o_sa).then_inc(s["sa_copied"], 1)

                def y_out(turn, ci):
                    take(act, s["y_done"])
                    link(act.copy(y[:, :, bass.ds(turn * P + ci * HD, HD)], o_y.rearrange("p (j n) -> p j n", j=NPAIR)))

                def step(f, behind=None, ahead=None, front=True):
                    seq = behind is not None
                    if front:
                        rows_out(f)
                    if seq:
                        u_out(0)
                        sa_out(0)
                        y_out(behind, 0)
                    if front:
                        t1_out()
                    if seq:
                        u_out(1)
                        sa_out(1)
                    if front:
                        t1_out()
                    if seq:
                        y_out(behind, 1)
                    if front:
                        for part in range(NLV - 2):
                            t1_out()
                            if ahead is not None:
                                stage(ahead, 1 - f, part)

                for part in range(3):
                    stage(0, 0, part)
                step(0, ahead=1)
                with act.Fori(0, NTURN // 2 - 1) as i:
                    step(1, behind=2 * i, ahead=2 * i + 2)
                    step(0, behind=2 * i + 1, ahead=2 * i + 3)
                step(1, behind=NTURN - 2)
                step(0, behind=NTURN - 1, front=False)

            @block.tensor
            def _(pe):
                def turn_rows():
                    take(pe, s["staged"])
                    for m, src in enumerate((VS, BS, KS)):
                        for n, (ci, j) in enumerate(items):
                            for h, q in halves():
                                last = pe.matmul(ps[q, B_TOK[m], js(n)], src[q, ci, j, :], eye[h], start=True, stop=True)
                    last.then_inc(s["turned_done"], 1)

                def gram_b(f):
                    for n, (ci, j) in enumerate(items):
                        for h, q in halves():
                            pe.matmul(lt_rb[q, n].rearrange("p m n -> p (m n)"), BS[q, ci, j, :],
                                      AR[q, f, ci, j].rearrange("p m n -> p (m n)"), start=True, stop=True)
                            last = pe.matmul(low[q, n], AR[q, f, ci, j, 0, :], BS[q, ci, j, :], start=True, stop=True)
                    last.then_inc(s["lt_done"], 1)

                def gram_k(f):
                    take(pe, s["tok_ready"])
                    for n, (ci, j) in enumerate(items):
                        for h, q in halves():
                            last = pe.matmul(mt_rk[q, n].rearrange("p m n -> p (m n)"), KS[q, ci, j, :],
                                             AR[q, f, ci, j].rearrange("p m n -> p (m n)"), start=True, stop=True)
                    last.then_inc(s["mt_done"], 1)

                def t1(lv):
                    if lv == 0:
                        take(pe, s["x_first"])
                    for g in range(2):
                        if lv:
                            take(pe, s["x_next"])
                        for j in range(NPAIR):
                            for h, q in halves():
                                n = g * NPAIR + j
                                last = pe.matmul(ps[q, B_T1[g], js(j)], LO[q, lv, n, :], X[q, n, :], start=True, stop=True)
                        last.then_inc(s["t1_done"], 1)

                def dx(lv, f):
                    for g in range(2):
                        take(pe, s["t1_copied"])
                        for j in range(NPAIR):
                            for h, q in halves():
                                n = g * NPAIR + j
                                if lv < NLV - 1:
                                    pe.matmul(ps[q, B_DX[g], js(j)], XT[q, f, n, :], T1[q, n, :], start=True, stop=True)
                                last = pe.matmul(ps[q, B_DX[g], js(NPAIR + j)], T1[q, n, :], XT[q, f, n, :], start=True, stop=True)
                        last.then_inc(s["dx_done"], 1)

                def u(f, ci):
                    take(pe, s["s_ready"])
                    for j in range(NPAIR):
                        n = ci * NPAIR + j
                        for h, q in halves():
                            pe.matmul(o_u[q, js(j)], MK[f][q, 0, n, :], tok[q, f, 0, n, :], start=True, stop=False)
                            last = pe.matmul(o_u[q, js(j)], AR[q, f, ci, j, 0, :], SS[q, ci, j, :], start=False, stop=True)
                    last.then_inc(s["u_done"], 1)

                def sa(f, ci):
                    take(pe, s["u_copied"])
                    for j in range(NPAIR):
                        for h, q in halves():
                            last = pe.matmul(o_sa[q, js(j)], XT[q, f, ci * NPAIR + j, :], U[q, ci, j, :], start=True, stop=True)
                    last.then_inc(s["sa_done"], 1)

                def ds_y(f, ci):
                    take(pe, s["sa_copied"])
                    for j in range(NPAIR):
                        n = ci * NPAIR + j
                        for h, q in halves():
                            pe.matmul(o_ds[q, js(j)], tok[q, f, 1, n, :], SA[q, ci, j, :], start=True, stop=False)
                            last = pe.matmul(o_ds[q, js(j)], tok[q, f, 2, n, :], tok[q, f, 0, n, :], start=False, stop=True)
                    last.then_inc(s["ds_done"], 1)
                    for j in range(NPAIR):
                        n = ci * NPAIR + j
                        for h, q in halves():
                            pe.matmul(o_y[q, js(j)], SS[q, ci, j, :], AR[q, f, ci, j, 1, :], start=True, stop=False)
                            pe.matmul(o_y[q, js(j)], SA[q, ci, j, :], RB[f][q, n, :], start=False, stop=False)
                            last = pe.matmul(o_y[q, js(j)], tok[q, f, 0, n, :], MK[f][q, 1, n, :], start=False, stop=True)
                    last.then_inc(s["y_done"], 1)

                def step(f, seq=True, front=True):
                    g = 1 - f
                    if front:
                        turn_rows()
                    if seq:
                        u(g, 0)
                        take(pe, s["x_next"], 2)
                    if front:
                        gram_b(f)
                    if seq:
                        sa(g, 0)
                    if front:
                        gram_k(f)
                    if seq:
                        ds_y(g, 0)
                    if front:
                        t1(0)
                    if seq:
                        u(g, 1)
                    if front:
                        dx(0, f)
                    if seq:
                        sa(g, 1)
                    if front:
                        t1(1)
                    if seq:
                        ds_y(g, 1)
                    if front:
                        dx(1, f)
                        for lv in range(2, NLV):
                            t1(lv)
                            dx(lv, f)

                step(0, seq=False)
                with pe.Fori(0, NTURN // 2 - 1):
                    step(1)
                    step(0)
                step(1)
                step(0, front=False)

            @block.vector
            def _(dve):
                def link(ins):
                    ins.then_inc(s["order"], 1)
                    take(dve, s["order"])

                ident64 = b.ident64
                fl = lambda t: t.rearrange("p i n -> p (i n)")
                up = lambda lv: bcast(c.upper[:, lv, :], 1, NI)

                def masks_b(f):
                    take(dve, s["lt_done"])
                    link(dve.tensor_tensor(X[:], low, bcast(c.lower_1[:], 1, NI), ALU.mult))
                    link(dve.tensor_tensor(X[:], X[:], bcast(ident64[:], 1, NI), ALU.add))
                    link(dve.tensor_tensor(XT[:, f], lt_rb[:, :, 0, :], up(0), ALU.mult))
                    link(dve.tensor_tensor(XT[:, f], XT[:, f], bcast(ident64[:], 1, NI), ALU.add))
                    for lv in range(NLV):
                        dve.tensor_tensor(LO[:, lv], lt_rb[:, :, 0, :], up(lv + 1), ALU.mult)
                    link(dve.tensor_tensor(RB[f], lt_rb[:, :, 1, :], bcast(c.strict_incl[:, 1, :], 1, NI), ALU.mult))
                    dve.sem_inc(s["x_first"], 1)

                def masks_k(f):
                    take(dve, s["mt_done"])
                    for m in range(2):
                        link(dve.tensor_tensor(MK[f][:, m], mt_rk[:, :, m, :], bcast(c.strict_incl[:, m, :], 1, NI), ALU.mult))

                def x_add(lv, f):
                    for g in range(2):
                        take(dve, s["dx_done"])
                        if lv < NLV - 1:
                            x = fl(chunk_items(X, g))
                            link(dve.tensor_tensor(x, x, ps[:, B_DX[g], 0:W], ALU.add))
                        xt = fl(chunk_items(XT[:, f], g))
                        dve.tensor_tensor(xt, xt, ps[:, B_DX[g], W:2 * W], ALU.add).then_inc(s["x_next"], 1)

                def state(turn, ci):
                    take(dve, s["ds_done"])
                    link(dve.tensor_tensor(sn[:], SS[:, ci], o_ds.rearrange("p (j n) -> p j n", j=NPAIR), ALU.add))
                    stepc = b.step[:, :, bass.ds(2 * turn + ci, 1)].to_broadcast([P, NPAIR, HD])
                    dve.tensor_tensor(SS[:, 1 - ci], sn[:], stepc, ALU.mult).then_inc(s["s_ready"], 1)

                def step(f, behind=None, front=True):
                    if front:
                        masks_b(f)
                    if behind is not None:
                        state(behind, 0)
                    if front:
                        masks_k(f)
                        x_add(0, f)
                    if behind is not None:
                        state(behind, 1)
                    if front:
                        for lv in range(1, NLV):
                            x_add(lv, f)

                link(dve.memset(SS[:, 0], 0.0))
                dve.sem_inc(s["s_ready"], 1)
                step(0)
                with dve.Fori(0, NTURN // 2 - 1) as i:
                    step(1, behind=2 * i)
                    step(0, behind=2 * i + 1)
                step(1, behind=NTURN - 2)
                step(0, behind=NTURN - 1, front=False)


def rwkv_finish(nc, c, proj, b):
    r, k, v = (proj[:, t:t + 4, :] for t in (T_R, T_K, T_V))
    y = b.bufs[3]
    flat = lambda t: t.rearrange("p j s -> p (j s)")
    with phase(nc, c) as (sem, sb):
        names = ("order", "mean_summed", "centred", "squared", "bonus_in", "bonus_summed", "bonus_done", "var_summed",
                 "var_ready", "rstd_done", "ln_done", "g_summed")
        s = {n: sem(n) for n in names}
        bonus, sq = sb("bonus", [P, NPAIR, S]), sb("squares", [P, NPAIR, S])
        ps = c.ps
        psf = ps[:].rearrange("p b n -> p (b n)")
        with nc.Block() as block:

            @block.tensor
            def _(pe):
                def head_sums(src, done):
                    for j in range(4):
                        for h in range(NH):
                            last = pe.matmul(ps[:, 2 * j + h, :], c.head_ones[:], src[:, j, h * HALF:(h + 1) * HALF], start=True, stop=True)
                    last.then_inc(s[done], 1)

                head_sums(y, "mean_summed")
                pe.wait_ge(s["bonus_in"], 1)
                pe.wait_ge(s["centred"], 1)
                head_sums(bonus, "bonus_summed")
                pe.wait_ge(s["squared"], 1)
                pe.wait_ge(s["bonus_done"], 1)
                head_sums(sq, "var_summed")
                pe.wait_ge(s["var_ready"], 1)
                for j in range(4):
                    for h in range(NH):
                        last = pe.matmul(ps[:, 2 * j + h, :], b.g2[:, j * P:(j + 1) * P], proj[:, T_G, h * HALF:(h + 1) * HALF],
                                         start=True, stop=True)
                last.then_inc(s["g_summed"], 1)

            @block.scalar
            def _(act):
                act.wait_ge(s["centred"], 1)
                act.activation(flat(sq[:]), flat(y), ACT.Square).then_inc(s["squared"], 1)
                act.wait_ge(s["var_ready"], 1)
                act.activation(flat(sq[:]), flat(sq[:]), ACT.Ln).then_inc(s["ln_done"], 1)
                act.wait_ge(s["ln_done"], 1)
                act.activation(flat(sq[:]), flat(sq[:]), ACT.Exp, scale=-0.5).then_inc(s["rstd_done"], 1)

            @block.vector
            def _(dve):
                ch = Chain(dve, s["order"])
                for j in range(4):
                    ch(dve.scalar_tensor_tensor(out=bonus[:, j, :], in0=r[:, j, :], scalar=b.r_k[:, j:j + 1], in1=k[:, j, :],
                                                op0=ALU.mult, op1=ALU.mult))
                dve.sem_inc(s["bonus_in"], 1)
                dve.wait_ge(s["mean_summed"], 1)
                dve.scalar_tensor_tensor(out=flat(y), in0=psf, scalar=-1.0 / HD, in1=flat(y), op0=ALU.mult,
                                         op1=ALU.add).then_inc(s["centred"], 1)
                dve.wait_ge(s["bonus_summed"], 1)
                dve.tensor_tensor(flat(bonus[:]), psf, flat(v), ALU.mult).then_inc(s["bonus_done"], 1)
                dve.wait_ge(s["var_summed"], 1)
                dve.tensor_scalar(flat(sq[:]), psf, 1.0 / HD, GN_EPS, ALU.mult, ALU.add).then_inc(s["var_ready"], 1)
                dve.wait_ge(s["rstd_done"], 1)
                ch(dve.tensor_tensor(flat(y), flat(y), flat(sq[:]), ALU.mult))
                for j in range(4):
                    dve.tensor_scalar(y[:, j, :], y[:, j, :], b.ln_w[:, j:j + 1], b.ln_b[:, j:j + 1], ALU.mult, ALU.add).then_inc(s["order"], 1)
                ch.n += 4
                dve.wait_ge(s["order"], ch.n)
                ch(dve.tensor_tensor(flat(y), flat(y), flat(bonus[:]), ALU.add))
                dve.wait_ge(s["g_summed"], 1)
                ch(dve.tensor_tensor(flat(r), flat(y), psf, ALU.mult))


def project_out(nc, c, w, parts):
    w_t = w.rearrange("(k p) n -> p k n", p=P)
    with phase(nc, c) as (sem, sb):
        w_in = [sem("w_in0"), sem("w_in1")]
        w_high, w_low, staged, stage_high, stage_free = (
            sem(n) for n in ("w_high", "w_low", "staged", "stage_high", "stage_free"))
        summed, bank_free, order = sem("summed"), sem("bank_free"), sem("order")
        raw = sb("w_raw", [P, 2, HALF])
        wh, wl = sb("w_high", [P, KT, D], F32R), sb("w_low", [P, KT, D], F32R)
        sh, sl = sb("y_high", [P, 2, KT, P], F32R), sb("y_low", [P, 2, KT, P], F32R)
        ps = c.ps
        pieces = [(k, slice(h * HALF, (h + 1) * HALF)) for k in range(KT) for h in range(2)]
        spans, k0 = [], 0
        for part in parts:
            spans.append((part, slice(k0, k0 + part.shape[1])))
            k0 += part.shape[1]
        with nc.Block() as block:

            @block.sync
            def _(sp):
                for n, (k, cols) in enumerate(pieces):
                    if n >= 2:
                        sp.wait_ge(w_low, n - 1)
                    sp.dma_start(raw[:, n % 2, :], w_t[:, k, cols]).then_inc(w_in[n % 2], 16)

            @block.scalar
            def _(act):
                for n, (k, cols) in enumerate(pieces):
                    act.wait_ge(w_in[n % 2], 16 * (n // 2 + 1))
                    act.copy(wh[:, k, cols], raw[:, n % 2, :]).then_inc(w_high, 1)
                with act.Fori(0, TT // 2) as i:
                    for q in range(2):
                        take(act, stage_free)
                        for part, ks in spans:
                            act.copy(sh[:, q, ks, :], part[:, :, bass.ds(i * (2 * P) + q * P, P)]).then_inc(order, 1)
                            take(act, order)
                        act.sem_inc(stage_high, 1)

            @block.vector
            def _(dve):
                for n, (k, cols) in enumerate(pieces):
                    dve.wait_ge(w_high, n + 1)
                    dve.tensor_tensor(wl[:, k, cols], raw[:, n % 2, :], wh[:, k, cols].bitcast(F32), ALU.subtract).then_inc(w_low, 1)
                dve.sem_inc(bank_free, 4)

                def lows(i, q):
                    take(dve, stage_high)
                    for part, ks in spans:
                        dve.tensor_tensor(sl[:, q, ks, :], part[:, :, bass.ds(i * (2 * P) + q * P, P)],
                                          sh[:, q, ks, :].bitcast(F32), ALU.subtract).then_inc(staged, 1)

                def add(i, q):
                    for h in range(2):
                        take(dve, summed)
                        rs = c.res[:, bass.ds(2 * i + q, 1), h * HALF:(h + 1) * HALF]
                        dve.tensor_tensor(rs, rs, ps[:, 2 * q + h:2 * q + h + 1, :], ALU.add).then_inc(bank_free, 1)

                with dve.Fori(0, TT // 2) as i:
                    lows(i, 0)
                    lows(i, 1)
                    add(i, 0)
                    add(i, 1)

            @block.tensor
            def _(pe):
                pe.sem_inc(stage_free, 2)
                pe.wait_ge(w_low, len(pieces))
                with pe.Fori(0, TT // 2):
                    for q in range(2):
                        take(pe, staged, len(spans))
                        for h in range(2):
                            take(pe, bank_free)
                            n = 0
                            for y, wp in ((sh, wh), (sh, wl), (sl, wh)):
                                for k in range(KT):
                                    last = pe.matmul(ps[:, 2 * q + h, :], y[:, q, k, :], wp[:, k, h * HALF:(h + 1) * HALF],
                                                     start=n == 0, stop=n == 3 * KT - 1)
                                    n += 1
                            last.then_inc(summed, 1)
                        pe.drain().then_inc(stage_free, 1)


def route(nc, c, m, h_T, w_group, b_group, w_expert, b_expert):
    NL = NG + NE
    with phase(nc, c) as (sem, sb):
        names = ("par_in", "made", "summed", "order", "group_shift", "group_exp", "pair_shift", "pair_exp", "picked",
                 "ranked")
        s = {n: sem(n) for n in names}
        wr = sb("w_router", [P, KT, NL])
        bias = sb("b_router", [P, NL])
        upper = sb("tokens_before", [P, P])
        it = sb("iota", [P, 64])
        i128 = sb("iota_128", [P, EPG])
        lg = sb("logits", [P, TT, NL])
        col = {n: sb(n, [P, TT]) for n in ("gmax", "gsum", "ggate", "m1", "m2", "rden", "first")}
        gsh, gsel, gtmp = (sb(n, [P, TT, NG]) for n in ("g_shift", "g_sel", "g_tmp"))
        ex, ex2, etmp, oh1, oh2 = (sb(n, [P, TT, EPG]) for n in ("e_logits", "e_rest", "e_tmp", "e_hot1", "e_hot2"))
        prod = sb("e_prod", [P, TT, EPG, NG])
        sel = [sb(f"sel{k}", [P, TT, NE]) for k in range(2)]
        both = sb("sel_both", [P, TT, NE])
        rows = sb("rows_of_expert", [P, TT, NE])
        rtmp = sb("rows_tmp", [P, TT, NE])
        rowf = sb("row_f", [P, 2, TT])
        nblk, pend, pstart = (sb(n, [P, NE]) for n in ("n_blocks", "blocks_end", "blocks_start"))
        cmp8 = sb("cmp_blocks", [P, NE, EPG])
        cmpb = sb("cmp_expert", [P, NBLK, NE])
        blkf = sb("block_expert_f", [P, NBLK])
        turnf, tcmp = sb("turns_f", [P, 1]), sb("turns_cmp", [P, NBLK // 2])
        ps = c.ps
        with nc.Block() as block:

            @block.sync
            def _(sp):
                sp.dma_start(wr[:, :, 0:NG], w_group.rearrange("(k p) g -> p k g", p=P)).then_inc(s["par_in"], 16)
                sp.dma_start(wr[:, :, NG:NL], w_expert.rearrange("(k p) g -> p k g", p=P)).then_inc(s["par_in"], 16)
                sp.dma_start(bias[:, 0:NG], b_group.partition_broadcast(P)).then_inc(s["par_in"], 16)
                sp.dma_start(bias[:, NG:NL], b_expert.partition_broadcast(P)).then_inc(s["par_in"], 16)
                sp.wait_ge(s["par_in"], 64)

            @block.gpsimd
            def _(pool):
                ch = Chain(pool, s["made"])
                ch(pool.iota(it[:], [[1, 64]], base=0, channel_multiplier=0, allow_small_or_imprecise_dtypes=True))
                ch(pool.iota(i128[:], [[P, EPG]], base=0, channel_multiplier=0, allow_small_or_imprecise_dtypes=True))
                ch(pool.memset(upper[:], 1.0))
                ch(pool.affine_select(out=upper[:], in_=upper[:], pattern=[[1, P]], compare_op=ALU.is_gt, fill=0.0,
                                      base=0, channel_multiplier=-1))

            @block.tensor
            def _(pe):
                pe.wait_ge(s["par_in"], 64)
                for t in range(TT):
                    for k in range(KT):
                        last = pe.matmul(ps[:, 0, t * NL:(t + 1) * NL], h_T[:, k, t * P:(t + 1) * P], wr[:, k, :],
                                         start=k == 0, stop=k == KT - 1)
                last.then_inc(s["summed"], 1)
                pe.wait_ge(s["picked"], 1)
                pe.wait_ge(s["made"], 4)
                for t in range(TT):
                    for u in range(t + 1):
                        pe.matmul(ps[:, 1, t * NE:(t + 1) * NE], upper[:] if u == t else c.ones[:], both[:, u, :],
                                  start=u == 0, stop=u == t)
                for u in range(TT):
                    last = pe.matmul(ps[:, 2, 0:NE], c.ones[:], both[:, u, :], start=u == 0, stop=u == TT - 1)
                last.then_inc(s["ranked"], 1)

            @block.scalar
            def _(act):
                act.wait_ge(s["group_shift"], 1)
                act.activation(gtmp[:], gsh[:], ACT.Exp).then_inc(s["group_exp"], 1)
                act.wait_ge(s["pair_shift"], 1)
                act.activation(col["m2"][:], col["m2"][:], ACT.Exp).then_inc(s["pair_exp"], 1)

            @block.vector
            def _(dve):
                ch = Chain(dve, s["order"])

                def first_hot(hot, src, top, n):
                    ch(dve.tensor_reduce(top[:], src, AX.X, ALU.max))
                    ch(dve.tensor_tensor(hot, src, bcast(top[:], 2, n), ALU.is_equal))
                    ch(dve.scalar_tensor_tensor(out=hot, in0=hot, scalar=-64.0, in1=bcast(it[:, 0:n], 1, TT),
                                                op0=ALU.mult, op1=ALU.add))
                    ch(dve.tensor_reduce(col["first"][:], hot, AX.X, ALU.min))
                    ch(dve.tensor_tensor(hot, hot, bcast(col["first"][:], 2, n), ALU.is_equal))

                dve.wait_ge(s["made"], 2)
                dve.wait_ge(s["summed"], 1)
                ch(dve.tensor_tensor(lg[:], ps[:, 0, 0:TT * NL].rearrange("p (t n) -> p t n", t=TT), bcast(bias[:], 1, TT), ALU.add))
                g = lg[:, :, 0:NG]
                first_hot(gsel[:], g, col["gmax"], NG)
                dve.tensor_tensor(gsh[:], g, bcast(col["gmax"][:], 2, NG), ALU.subtract).then_inc(s["group_shift"], 1)
                dve.wait_ge(s["group_exp"], 1)
                ch(dve.tensor_reduce(col["gsum"][:], gtmp[:], AX.X, ALU.add))
                ch(dve.reciprocal(col["ggate"][:], col["gsum"][:]))
                ch(dve.tensor_tensor(prod[:], lg[:, :, NG:NL].rearrange("p t (g e) -> p t e g", g=NG),
                                     bcast(gsel[:], 2, EPG), ALU.mult))
                ch(dve.tensor_reduce(ex[:], prod[:], AX.X, ALU.add))
                first_hot(oh1[:], ex[:], col["m1"], EPG)
                ch(dve.scalar_tensor_tensor(out=ex2[:], in0=oh1[:], scalar=-BIG, in1=ex[:], op0=ALU.mult, op1=ALU.add))
                first_hot(oh2[:], ex2[:], col["m2"], EPG)
                dve.tensor_tensor(col["m2"][:], col["m2"][:], col["m1"][:], ALU.subtract).then_inc(s["pair_shift"], 1)
                for k, oh in enumerate((oh1, oh2)):
                    ch(dve.tensor_tensor(sel[k][:].rearrange("p t (g e) -> p t g e", g=NG), bcast(gsel[:], 3, EPG),
                                         bcast(oh[:], 2, NG), ALU.mult))
                dve.tensor_tensor(both[:], sel[0][:], sel[1][:], ALU.add).then_inc(s["picked"], 1)
                dve.wait_ge(s["pair_exp"], 1)
                ch(dve.tensor_scalar(col["rden"][:], col["m2"][:], 1.0, None, ALU.add))
                ch(dve.reciprocal(col["rden"][:], col["rden"][:]))
                ch(dve.tensor_tensor(m.gate[:, 0, :], col["rden"][:], col["ggate"][:], ALU.mult))
                ch(dve.tensor_tensor(m.gate[:, 1, :], m.gate[:, 0, :], col["m2"][:], ALU.mult))
                dve.wait_ge(s["ranked"], 1)
                ch(dve.tensor_copy(nblk[:], ps[:, 2, 0:NE]))
                ch(dve.tensor_tensor(cmp8[:], bcast(nblk[:], 2, EPG), bcast(i128[:], 1, NE), ALU.is_gt))
                ch(dve.tensor_reduce(nblk[:], cmp8[:], AX.X, ALU.add))
                ch(dve.tensor_tensor_scan(pend[:], c.ones[:, 0:NE], nblk[:], 0.0, ALU.mult, ALU.add))
                ch(dve.tensor_tensor(pstart[:], pend[:], nblk[:], ALU.subtract))
                ch(dve.tensor_scalar(pstart[:], pstart[:], float(P), float(P), ALU.mult, ALU.add))
                ch(dve.tensor_tensor(rows[:], ps[:, 1, 0:TT * NE].rearrange("p (t n) -> p t n", t=TT), bcast(pstart[:], 1, TT), ALU.add))
                for k in range(2):
                    ch(dve.tensor_tensor(rtmp[:], rows[:], sel[k][:], ALU.mult))
                    ch(dve.tensor_reduce(rowf[:, k, :], rtmp[:], AX.X, ALU.add))
                ch(dve.tensor_copy(m.row[:], rowf[:]))
                ch(dve.tensor_tensor(cmpb[:], bcast(pend[:], 1, NBLK), bcast(it[:, 0:NBLK], 2, NE), ALU.is_le))
                ch(dve.tensor_reduce(blkf[:], cmpb[:], AX.X, ALU.add))
                ch(dve.tensor_scalar(blkf[:], blkf[:], float(NE - 1), None, ALU.min))
                ch(dve.tensor_copy(m.block_expert[:], blkf[:]))
                ch(dve.tensor_scalar(tcmp[:], it[:, 0:NBLK // 2], 2.0, None, ALU.mult))
                ch(dve.tensor_tensor(tcmp[:], tcmp[:], pend[:, NE - 1:NE].to_broadcast([P, NBLK // 2]), ALU.is_lt))
                ch(dve.tensor_reduce(turnf[:], tcmp[:], AX.X, ALU.add))
                ch(dve.tensor_copy(m.turns[:], turnf[:]))


def dispatch(nc, c, m, row_tok):
    with phase(nc, c) as (sem, sb):
        made, cleared, placed, back = sem("made"), sem("cleared", True), sem("placed", True), sem("back", True)
        widened, turned = sem("widened"), sem("turned")
        by_block, by_block_f = sb("token_by_block", [NBLK, P], I32), sb("token_by_block_f", [NBLK, P])
        ps = c.ps
        zero = sb("zero_rows", [P, NBLK + 1], I32)
        tok = sb("token_id", [P, TT], I32)
        with nc.Block() as block:

            @block.gpsimd
            def _(pool):
                ch = Chain(pool, made)
                ch(pool.memset(zero[:], 0))
                ch(pool.iota(tok[:], [[P, TT]], base=0, channel_multiplier=1))
                pool.dma_start(row_tok.rearrange("(p n) o -> p (n o)", p=P), zero[:]).then_inc(cleared, 16)
                pool.wait_ge(cleared, 16)
                for k in range(2):
                    for t in range(TT):
                        pool.indirect_dma_start(row_tok, bass.IndirectOffsetOnAxis(ap=m.row[:, k, t:t + 1], axis=0),
                                                tok[:, t:t + 1], None).then_inc(placed, 16)
                pool.wait_ge(placed, 32 * TT)
                pool.dma_start(by_block[:], row_tok[P:, 0].rearrange("(b p) -> b p", p=P)).then_inc(back, 16)

            @block.vector
            def _(dve):
                dve.wait_ge(back, 16)
                dve.tensor_copy(by_block_f[:], by_block[:]).then_inc(widened, 1)
                dve.wait_ge(turned, 1)
                dve.tensor_copy(m.row_token[:], ps[:, 0, 0:NBLK])

            @block.tensor
            def _(pe):
                pe.wait_ge(widened, 1)
                pe.transpose(ps[:, 0, 0:NBLK], by_block_f[:], c.ident[0:NBLK, 0:NBLK]).then_inc(turned, 1)


def experts(nc, c, m, rows, ys, w_gate, w_up, w_down):
    GU, DN = FF * KT // D, FF // P
    NPC = 2 * GU + DN
    KP = KT // GU
    with phase(nc, c) as (sem, sb):
        x_in, x_ready, x_free = sem("x_in", True), sem("x_ready"), sem("x_free")
        raw_in = [sem(f"raw_in{p}") for p in range(NPC)]
        high_made, low_made, w_ready, w_free = sem("high_made"), sem("low_made"), sem("w_ready"), sem("w_free")
        x_turned, xh_made, xh_ready, xl_ready = sem("x_turned"), sem("xh_made"), sem("xh_ready"), sem("xl_ready")
        g_done, u_done, silu_ready, hid_ready = sem("g_done"), sem("u_done"), sem("silu_ready"), sem("hid_ready")
        hid_turned, hh_made, hh_ready, hl_ready = sem("hid_turned"), sem("hh_made"), sem("hh_ready"), sem("hl_ready")
        d_done, y_stored = sem("d_done"), sem("y_stored")
        order_a, order_p = sem("order_a"), sem("order_p")
        raw = sb("w_raw", [P, NPC, D])
        wh, wl = sb("w_high", [P, NPC, D], F32R), sb("w_low", [P, NPC, D], F32R)
        idx = sb("row_index", [P, 1], I32)
        xg = sb("x_rows", [P, D])
        xh, xl = sb("x_high", [P, 2, KT, P], F32R), sb("x_low", [P, 2, KT, P], F32R)
        hid = sb("hidden", [P, FF])
        hh, hl = sb("hidden_high", [P, DN, P], F32R), sb("hidden_low", [P, DN, P], F32R)
        yb = sb("y_rows", [P, D])
        ps = c.ps
        B_X, B_G, B_U, B_H, B_Y = 0, 2, 3, 4, 6
        gate_up, down_p = range(2 * GU), range(2 * GU, NPC)

        def turns(eng):
            return eng.value_load(m.turns[0:1, 0:1], min_val=NBLK // 3 // 2, max_val=NBLK // 2)

        with nc.Block() as block:

            @block.sync
            def _(sp):
                def expert(b):
                    return sp.value_load(m.block_expert[0:1, bass.ds(b, 1)], min_val=0, max_val=NE - 1)

                def split_done():
                    take(sp, low_made)
                    sp.sem_inc(w_ready, 1)

                def load(e, pieces, fresh=False):
                    for p in pieces:
                        if not fresh:
                            split_done()
                        w, k0, kn = (w_down, p - 2 * GU, 1) if p >= 2 * GU else ((w_gate, w_up)[p // GU], p % GU * KP, KP)
                        src = w[bass.ds(e, 1), k0 * P:(k0 + kn) * P].rearrange("e (k p) f -> p (e k) f", p=P)
                        sp.dma_start(raw[:, p, :].rearrange("p (k f) -> p k f", k=kn), src).then_inc(raw_in[p], 16)

                n = turns(sp)
                e0, e1 = expert(0), expert(1)
                load(e0, gate_up, fresh=True)
                load(e1, gate_up)
                load(e0, down_p, fresh=True)
                with sp.Fori(1, n) as i:
                    e = [expert(2 * i - 1 + d) for d in range(3)]
                    for d in range(2):
                        load(e[d + 1], gate_up)
                        load(e[d], down_p)
                for _p in gate_up:
                    split_done()
                load(expert(2 * n - 1), down_p)
                for _p in down_p:
                    split_done()

            @block.gpsimd
            def _(pool):
                n = turns(pool)
                with pool.Fori(0, n) as i:
                    for q in range(2):
                        take(pool, x_free)
                        pool.tensor_copy(idx[:], m.row_token[:, bass.ds(2 * i + q, 1)]).then_inc(order_p, 1)
                        take(pool, order_p)
                        pool.indirect_dma_start(xg[:], None, rows, bass.IndirectOffsetOnAxis(ap=idx[:], axis=0)).then_inc(x_in, 16)
                        pool.wait_ge(x_in, 32 * i + 16 * (q + 1))
                        pool.sem_inc(x_ready, 1)

            @block.scalar
            def _(act):
                def high(pieces, fresh=False):
                    for p in pieces:
                        take(act, raw_in[p], 16)
                        if not fresh:
                            take(act, w_free)
                        act.copy(wh[:, p, :], raw[:, p, :]).then_inc(high_made, 1)

                def x_high(q):
                    take(act, x_turned)
                    act.sem_inc(x_free, 1)
                    act.copy(xh[:, q], ps[:, B_X:B_X + 2, :].rearrange("p b (k n) -> p (b k) n", k=4)).then_inc(order_a, 1)
                    take(act, order_a)
                    act.sem_inc(xh_made, 1)
                    act.sem_inc(xh_ready, 1)

                def silu():
                    take(act, g_done)
                    act.activation(hid[:], ps[:, B_G, :], ACT.Silu).then_inc(silu_ready, 1)

                def hidden_high():
                    take(act, hid_turned)
                    act.copy(hh[:].rearrange("p k n -> p (k n)"), ps[:, B_H, :]).then_inc(order_a, 1)
                    take(act, order_a)
                    act.sem_inc(hh_made, 1)
                    act.sem_inc(hh_ready, 1)

                def y_out(block_row):
                    take(act, d_done)
                    take(act, y_stored, 16)
                    act.copy(yb[:].rearrange("p (b n) -> p b n", b=2), ps[:, B_Y:B_Y + 2, :]).then_inc(order_a, 1)
                    take(act, order_a)
                    act.dma_start(ys[block_row, :], yb[:]).then_inc(y_stored, 16)

                def step(q, y_row, last=False):
                    if not last:
                        high(range(0, 2))
                        x_high(1 - q)
                        high(range(2, GU))
                    silu()
                    if last:
                        take(act, w_free, 2 * GU)
                    else:
                        high(range(GU, 2 * GU))
                    high(down_p, fresh=y_row is None)
                    if y_row is not None:
                        y_out(y_row)
                    hidden_high()

                act.sem_inc(x_free, 1)
                act.sem_inc(y_stored, 16)
                n = turns(act)
                high(gate_up, fresh=True)
                x_high(0)
                step(0, None)
                with act.Fori(1, n) as i:
                    step(1, bass.ds((2 * i - 1) * P, P))
                    step(0, bass.ds(2 * i * P, P))
                step(1, bass.ds((2 * n - 1) * P, P), last=True)
                y_out(bass.ds(2 * n * P, P))
                act.wait_ge(y_stored, 16)

            @block.tensor
            def _(pe):
                def turn_x():
                    take(pe, x_ready)
                    for k in range(KT):
                        last = pe.transpose(ps[:, B_X + k // 4, (k % 4) * P:(k % 4 + 1) * P], xg[:, k * P:(k + 1) * P], c.ident[:])
                    last.then_inc(x_turned, 1)

                def triple(bank, high, low, w_h, w_l, first, final):
                    pe.matmul(ps[:, bank, :], high, w_h, start=first, stop=False)
                    pe.matmul(ps[:, bank, :], high, w_l, start=False, stop=False)
                    return pe.matmul(ps[:, bank, :], low, w_h, start=False, stop=final)

                def gate_or_up(bank, p0, q, done):
                    for p in range(p0, p0 + GU):
                        take(pe, w_ready)
                        for kp in range(KP):
                            k, f = (p - p0) * KP + kp, slice(kp * FF, (kp + 1) * FF)
                            last = triple(bank, xh[:, q, k, :], xl[:, q, k, :], wh[:, p, f], wl[:, p, f], k == 0, k == KT - 1)
                        last.then_inc(w_free, 1)
                    pe.drain().then_inc(done, 1)

                def turn_hidden():
                    take(pe, hid_ready)
                    for k in range(DN):
                        last = pe.transpose(ps[:, B_H, k * P:(k + 1) * P], hid[:, k * P:(k + 1) * P], c.ident[:])
                    last.then_inc(hid_turned, 1)

                def down():
                    take(pe, hh_ready)
                    take(pe, hl_ready)
                    for k in range(DN):
                        take(pe, w_ready)
                        p = 2 * GU + k
                        for h in range(2):
                            f = slice(h * HALF, (h + 1) * HALF)
                            last = triple(B_Y + h, hh[:, k, :], hl[:, k, :], wh[:, p, f], wl[:, p, f], k == 0, k == DN - 1)
                        last.then_inc(w_free, 1)
                    pe.drain().then_inc(d_done, 1)

                def step(q, first=False, last=False):
                    take(pe, xh_ready)
                    take(pe, xl_ready)
                    gate_or_up(B_G, 0, q, g_done)
                    if not last:
                        turn_x()
                    gate_or_up(B_U, GU, q, u_done)
                    if not first:
                        down()
                    turn_hidden()

                n = turns(pe)
                turn_x()
                step(0, first=True)
                with pe.Fori(1, n):
                    step(1)
                    step(0)
                step(1, last=True)
                down()

            @block.vector
            def _(dve):
                def low(pieces):
                    for p in pieces:
                        take(dve, high_made)
                        dve.tensor_tensor(wl[:, p, :], raw[:, p, :], wh[:, p, :].bitcast(F32), ALU.subtract).then_inc(low_made, 1)

                def x_low(q):
                    take(dve, xh_made)
                    dve.tensor_tensor(xl[:, q], ps[:, B_X:B_X + 2, :].rearrange("p b (k n) -> p (b k) n", k=4),
                                      xh[:, q].bitcast(F32), ALU.subtract).then_inc(xl_ready, 1)

                def hidden():
                    take(dve, silu_ready)
                    take(dve, u_done)
                    dve.tensor_tensor(hid[:], hid[:], ps[:, B_U, :], ALU.mult).then_inc(hid_ready, 1)

                def hidden_low():
                    take(dve, hh_made)
                    dve.tensor_tensor(hl[:].rearrange("p k n -> p (k n)"), ps[:, B_H, :],
                                      hh[:].rearrange("p k n -> p (k n)").bitcast(F32), ALU.subtract).then_inc(hl_ready, 1)

                def step(q, last=False):
                    if not last:
                        low(range(0, 2))
                        x_low(1 - q)
                        low(range(2, 2 * GU))
                    hidden()
                    low(down_p)
                    hidden_low()

                n = turns(dve)
                low(gate_up)
                x_low(0)
                step(0)
                with dve.Fori(1, n):
                    step(1)
                    step(0)
                step(1, last=True)


def combine(nc, c, m, ys):
    NB = 4
    with phase(nc, c) as (sem, sb):
        got = [sem(f"got{i}", True) for i in range(NB)]
        used = sem("used")
        yg = sb("y_gathered", [P, NB, D])
        with nc.Block() as block:

            @block.gpsimd
            def _(pool):
                for n in range(2 * TT):
                    t, k = n // 2, n % 2
                    if n >= NB:
                        pool.wait_ge(used, n - NB + 1)
                    pool.indirect_dma_start(yg[:, n % NB, :], None, ys, bass.IndirectOffsetOnAxis(ap=m.row[:, k, t:t + 1], axis=0)).then_inc(got[n % NB], 16)

            @block.vector
            def _(dve):
                for n in range(2 * TT):
                    t, k = n // 2, n % 2
                    dve.wait_ge(got[n % NB], 16 * (n // NB + 1))
                    if n:
                        dve.wait_ge(used, n)
                    dve.scalar_tensor_tensor(out=c.res[:, t, :], in0=yg[:, n % NB, :], scalar=m.gate[:, k, t:t + 1],
                                             in1=c.res[:, t, :], op0=ALU.mult, op1=ALU.add).then_inc(used, 1)


def moe(nc, c, a, layer):
    with ExitStack() as ctx:
        def sb(name, shape, dt=F32):
            return ctx.enter_context(nc.sbuf_tensor(f"{name}_{layer}", shape, dt))

        m = Chip()
        m.row, m.gate = sb("row_of", [P, 2, TT], I32), sb("gate_of", [P, 2, TT])
        m.row_token = sb("token_of_row", [P, NBLK], I32)
        m.block_expert, m.turns = sb("block_expert", [P, NBLK], I32), sb("turns", [P, 1], I32)
        with nc.sbuf_tensor(f"h_T_ffn_{layer}", [P, KT, S], F32) as h_T:
            norm(nc, c, a["norm_ffn"][layer], h_T=h_T, rows=c.rows)
            route(nc, c, m, h_T, a["moe_w_group"][layer], a["moe_b_group"][layer], a["moe_w_expert"][layer], a["moe_b_expert"][layer])
        dispatch(nc, c, m, c.row_tok)
        experts(nc, c, m, c.rows, c.ys, a["moe_w_gate"][layer], a["moe_w_up"][layer], a["moe_w_down"][layer])
        combine(nc, c, m, c.ys)


def hgrn(nc, c, w, lower_bound, norm_w, h_T, y_T):
    w_t = w.rearrange("(k p) m -> p k m", p=P)
    NL = len(HLEVELS)
    with phase(nc, c) as (sem, sb):
        names = ("par_in", "lb_order", "lb_exp", "masks_made", "order", "order_a",
                 "proj_done", "fq_ready", "v_ready", "g_ready", "head_done", "fg_ready", "lf_ready", "k_ready",
                 "diff_ready", "exp_ready", "level_ready", "step_ready", "kd_ready", "qe_ready", "bc_ready",
                 "v_turned", "v_rows_ready", "kd_turned", "kd_rows_ready", "ds_done", "s_ready", "score_ready",
                 "o_done", "sq_ready", "sq_summed", "var_ready", "rstd_ready", "tail_free", "o_read")
        s = {n: sem(n) for n in names}
        w_in, w_free = [sem(f"w_in{n}") for n in range(4)], [sem(f"w_free{n}") for n in range(4)]
        bank_free = [sem("bank_free0"), sem("bank_free1")]
        gram_done, gram_free = [sem("gram_done0"), sem("gram_done1")], [sem("gram_free0"), sem("gram_free1")]
        wt = sb("w_tiles", [P, 4, KT, P])
        Q, G, V, F = (sb(n, [P, 2, S]) for n in ("q", "g", "v", "log_f"))
        K, BC = sb("k", [P, S]), sb("cum_log_f", [P, S])
        E = sb("level_ops", [P, 4, S])
        KD, QE = sb("k_to_end", [P, S]), sb("q_from_start", [P, S])
        VR, KR = sb("v_rows", [P, TT, P]), sb("k_rows", [P, TT, P])
        SC = sb("scores_T", [P, TT, P])
        ST = sb("states", [P, TT, P])
        reset = sb("chunk_reset", [P, S])
        mask = sb("level_masks", [P, NL, P])
        step_decay = sb("step_decay", [P, TT])
        lb, lb1, nw = sb("lower_bound", [P, HEADS]), sb("one_minus_lb", [P, HEADS]), sb("norm_w", [P, HEADS])
        l0, l1, lm = (sb(n, [P, HEADS]) for n in ("lb0", "lb1_in", "lb_max"))
        ps = c.ps
        pair = lambda ap: ap.rearrange("p b n -> p (b n)")
        col = lambda t, h: t[:, bass.ds(h, 1)]

        def make_masks(pool):
            ch = Chain(pool, s["masks_made"])
            ch(pool.memset(mask[:], 1.0))
            for i, hw in enumerate(HLEVELS):
                up = mask[:, i, :].rearrange("p (n h q) -> p n h q", h=2, q=hw)
                for pat, base, mult in (([[-2 * hw, P // (2 * hw)], [1000, 2], [0, hw]], -1000, 1),
                                        ([[2 * hw, P // (2 * hw)], [0, 2], [0, hw]], hw - 1, -1)):
                    ch(pool.affine_select(out=up, in_=up, pattern=pat, compare_op=ALU.is_ge, fill=0.0, base=base,
                                          channel_multiplier=mult))
            ch(pool.memset(reset[:], 1.0))
            ch(pool.memset(reset[:].rearrange("p (n q) -> p n q", q=P)[:, :, 0:1], 0.0))
            return ch.n

        n_masks = 1 + 2 * NL + 2

        def level_view(t, lv):
            return t.rearrange("p (n w) -> p n w", w=2 * HLEVELS[lv])

        with nc.Block() as block:

            @block.gpsimd
            def _(pool):
                assert make_masks(pool) == n_masks

            @block.sync
            def _(sp):
                for t, v in ((l0, lower_bound[0]), (l1, lower_bound[1]), (nw, norm_w)):
                    sp.dma_start(t[:], column(v)).then_inc(s["par_in"], 16)

                def load(h):
                    for m in range(4):
                        take(sp, w_free[m])
                        c0 = ORDER[m] * D
                        sp.dma_start(wt[:, m], w_t[:, :, bass.ds(h * P + c0, P)]).then_inc(w_in[m], 16)

                ORDER = (1, 0, 2, 3)
                with sp.Fori(0, HEADS) as h:
                    load(h)
                sp.wait_ge(s["par_in"], 48)

            @block.tensor
            def _(pe):
                def projection():
                    for m in range(4):
                        take(pe, w_in[m], 16)
                        take(pe, bank_free[m % 2])
                        for h in range(NH):
                            for k in range(KT):
                                last = pe.matmul(ps[:, 2 * (m % 2) + h, :], wt[:, m, k, :], h_T[:, k, h * HALF:(h + 1) * HALF],
                                                 start=k == 0, stop=k == KT - 1)
                                if h == NH - 1 and k == KT - 1:
                                    last.then_inc(s["proj_done"], 1)
                                yield

                def gram(left, right):
                    for b in range(2):
                        take(pe, gram_free[b])
                        for n in range(4):
                            t = slice((4 * b + n) * P, (4 * b + n + 1) * P)
                            last = pe.matmul(ps[:, 4 + b, n * P:(n + 1) * P], left[:, t], right[:, t], start=True, stop=True)
                        last.then_inc(gram_done[b], 1)

                def turn(src, done):
                    for n in range(TT):
                        last = pe.transpose(ps[:, 6 + n // 4, (n % 4) * P:(n % 4 + 1) * P], src[:, n * P:(n + 1) * P], c.ident[:])
                    last.then_inc(done, 1)

                def turn_v(par):
                    take(pe, s["v_ready"])
                    take(pe, s["tail_free"])
                    turn(V[:, par, :], s["v_turned"])

                def step(par, more):
                    ahead = projection() if more else iter(())

                    def project(n):
                        for _ in range(n):
                            next(ahead, None)

                    take(pe, s["k_ready"])
                    gram(K[:], Q[:, par, :])
                    for lv in range(NL):
                        project(4)
                        take(pe, s["level_ready"])
                        gram(E[:, lv % 4, :], E[:, lv % 4, :])
                    project(4)
                    take(pe, s["v_rows_ready"])
                    take(pe, s["kd_ready"])
                    turn(KD[:], s["kd_turned"])
                    project(8)
                    take(pe, s["kd_rows_ready"])
                    for n in range(TT):
                        last = pe.matmul(ps[:, 6 + n // 4, (n % 4) * P:(n % 4 + 1) * P], KR[:, n, :], VR[:, n, :], start=True, stop=True)
                    last.then_inc(s["ds_done"], 1)
                    project(8)
                    take(pe, s["s_ready"])
                    take(pe, s["qe_ready"])
                    for b in range(2):
                        take(pe, gram_free[b])
                    for n in range(TT):
                        o = ps[:, 4 + n // 4, (n % 4) * P:(n % 4 + 1) * P]
                        pe.matmul(o, VR[:, n, :], SC[:, n, :], start=True, stop=False)
                        last = pe.matmul(o, ST[:, n, :], QE[:, n * P:(n + 1) * P], start=False, stop=True)
                    last.then_inc(s["o_done"], 1)
                    project(8)
                    take(pe, s["sq_ready"])
                    for h in range(NH):
                        last = pe.matmul(ps[:, 6 + h, :], c.ones[:], KD[:, h * HALF:(h + 1) * HALF], start=True, stop=True)
                    last.then_inc(s["sq_summed"], 1)
                    project(9)
                    if more:
                        turn_v(1 - par)

                for _ in projection():
                    pass
                turn_v(0)
                with pe.Fori(0, HEADS // 2 - 1):
                    step(0, True)
                    step(1, True)
                step(0, True)
                step(1, False)

            @block.scalar
            def _(act):
                act.wait_ge(s["lb_order"], 2)
                act.activation(l0[:], l0[:], ACT.Exp).then_inc(s["lb_exp"], 1)
                act.activation(l1[:], l1[:], ACT.Exp).then_inc(s["lb_exp"], 1)
                for m in range(4):
                    act.sem_inc(w_free[m], 1)
                for q in range(2):
                    act.sem_inc(bank_free[q], 1)

                def link(ins):
                    ins.then_inc(s["order_a"], 1)
                    take(act, s["order_a"])

                def copy_out(m, par):
                    take(act, s["proj_done"])
                    act.sem_inc(w_free[m], 1)
                    src = pair(ps[:, 2 * (m % 2):2 * (m % 2) + 2, :])
                    if m == 0:
                        link(act.activation(F[:, par, :], src, ACT.Sigmoid))
                    elif m == 2:
                        link(act.copy(V[:, par, :], src))
                    else:
                        link(act.activation((Q if m == 1 else G)[:, par, :], src, ACT.Silu))
                    act.sem_inc(bank_free[m % 2], 1)
                    act.sem_inc(s[("fq_ready", "fq_ready", "v_ready", "g_ready")[m]], 1)

                def level_exp(lv):
                    take(act, s["diff_ready"])
                    v, hw = level_view(E[:, lv % 4, :], lv), HLEVELS[lv]
                    link(act.activation(v[:, :, 0:hw], v[:, :, 0:hw], ACT.Exp, scale=-1.0))
                    act.activation(v[:, :, hw:2 * hw], v[:, :, hw:2 * hw], ACT.Exp).then_inc(s["exp_ready"], 1)

                def log_f(par):
                    take(act, s["fg_ready"])
                    act.activation(F[:, par, :], F[:, par, :], ACT.Ln).then_inc(s["lf_ready"], 1)

                def first_exps():
                    take(act, s["bc_ready"])
                    act.activation(step_decay[:], BC[:].rearrange("p (n q) -> p n q", q=P)[:, :, P - 1], ACT.Exp).then_inc(s["step_ready"], 1)
                    level_exp(0)
                    level_exp(1)

                def v_rows():
                    take(act, s["v_turned"])
                    act.copy(VR[:].rearrange("p t n -> p (t n)"), pair(ps[:, 6:8, :])).then_inc(s["v_rows_ready"], 1)

                def step(par, more):
                    level_exp(2)
                    level_exp(3)
                    if more:
                        take(act, s["head_done"])
                        copy_out(0, 1 - par)
                    for lv in range(4, NL):
                        level_exp(lv)
                    take(act, s["diff_ready"])
                    act.activation(KD[:], KD[:], ACT.Exp).then_inc(s["exp_ready"], 1)
                    act.activation(QE[:], BC[:], ACT.Exp).then_inc(s["exp_ready"], 1)
                    if more:
                        copy_out(1, 1 - par)
                    take(act, s["kd_turned"])
                    act.copy(KR[:].rearrange("p t n -> p (t n)"), pair(ps[:, 6:8, :])).then_inc(s["kd_rows_ready"], 1)
                    if more:
                        copy_out(2, 1 - par)
                        log_f(1 - par)
                    take(act, s["o_done"])
                    act.activation(KD[:], pair(ps[:, 4:6, :]), ACT.Square).then_inc(s["sq_ready"], 1)
                    if more:
                        first_exps()
                    take(act, s["var_ready"])
                    link(act.activation(F[:, par, :], F[:, par, :], ACT.Ln))
                    act.activation(F[:, par, :], F[:, par, :], ACT.Exp, scale=-0.5).then_inc(s["rstd_ready"], 1)
                    if more:
                        copy_out(3, 1 - par)
                        v_rows()

                for m in range(4):
                    copy_out(m, 0)
                log_f(0)
                first_exps()
                v_rows()
                with act.Fori(0, HEADS // 2 - 1):
                    step(0, True)
                    step(1, True)
                step(0, True)
                step(1, False)

            @block.vector
            def _(dve):
                ch = Chain(dve, s["lb_order"])
                dve.wait_ge(s["par_in"], 48)
                ch(dve.tensor_tensor(lm[:], l0[:], l1[:], ALU.max))
                dve.tensor_tensor(l0[:], l0[:], lm[:], ALU.subtract)
                ch(dve.tensor_tensor(l1[:], l1[:], lm[:], ALU.subtract))
                dve.wait_ge(s["lb_exp"], 2)
                ch(dve.tensor_tensor(l0[:], l0[:], l1[:], ALU.add))
                ch(dve.reciprocal(l0[:], l0[:]))
                ch(dve.tensor_tensor(lb[:], l1[:], l0[:], ALU.mult))
                ch(dve.tensor_scalar(lb1[:], lb[:], -1.0, 1.0, ALU.mult, ALU.add))
                dve.wait_ge(s["masks_made"], n_masks)

                def link(ins):
                    ins.then_inc(s["order"], 1)
                    take(dve, s["order"])

                for b in range(2):
                    dve.sem_inc(gram_free[b], 1)
                dve.sem_inc(s["tail_free"], 1)
                dve.sem_inc(s["head_done"], 1)
                link(dve.memset(ST[:, 0, :], 0.0))

                def pick(lv):
                    m = c.ident[:] if lv is None else mask[:, lv, :]
                    for b in range(2):
                        take(dve, gram_done[b])
                        link(dve.copy_predicated(SC[:, 4 * b:4 * b + 4, :], bcast(m.bitcast(U32), 1, 4),
                                                 ps[:, 4 + b, :].rearrange("p (n t) -> p n t", n=4)))
                        dve.sem_inc(gram_free[b], 1)

                def diff(lv):
                    v, hw = level_view(BC[:], lv), HLEVELS[lv]
                    ref = v[:, :, hw - 1:hw].to_broadcast([P, S // (2 * hw), 2 * hw])
                    dve.tensor_tensor(level_view(E[:, lv % 4, :], lv), v, ref, ALU.subtract).then_inc(s["diff_ready"], 1)

                def scale(lv, par):
                    take(dve, s["exp_ready"])
                    v, hw = level_view(E[:, lv % 4, :], lv), HLEVELS[lv]
                    kv, qv = level_view(K[:], lv), level_view(Q[:, par, :], lv)
                    link(dve.tensor_tensor(v[:, :, 0:hw], v[:, :, 0:hw], kv[:, :, 0:hw], ALU.mult))
                    dve.tensor_tensor(v[:, :, hw:2 * hw], v[:, :, hw:2 * hw], qv[:, :, hw:2 * hw], ALU.mult).then_inc(s["level_ready"], 1)

                def front(h, par):
                    take(dve, s["fq_ready"], 2)
                    link(dve.tensor_scalar(F[:, par, :], F[:, par, :], col(lb1, h), col(lb, h), ALU.mult, ALU.add))
                    link(dve.tensor_scalar(K[:], F[:, par, :], -1.0, 1.0, ALU.mult, ALU.add))
                    dve.sem_inc(s["fg_ready"], 1)
                    dve.sem_inc(s["k_ready"], 1)
                    take(dve, s["lf_ready"])
                    link(dve.tensor_tensor_scan(BC[:], reset[:], F[:, par, :], 0.0, ALU.mult, ALU.add))
                    dve.sem_inc(s["bc_ready"], 1)
                    diff(0)
                    diff(1)

                def step(h, par, more):
                    link(dve.memset(SC[:], 0.0))
                    pick(None)
                    diff(2)
                    diff(3)
                    for lv in range(2, NL):
                        pick(lv - 2)
                        scale(lv, par)
                        if lv + 2 < NL:
                            diff(lv + 2)
                        if lv + 2 == NL:
                            bc = BC[:].rearrange("p (n q) -> p n q", q=P)
                            dve.tensor_tensor(KD[:].rearrange("p (n q) -> p n q", q=P), bc[:, :, P - 1:P].to_broadcast([P, TT, P]), bc,
                                              ALU.subtract).then_inc(s["diff_ready"], 1)
                    take(dve, s["exp_ready"])
                    dve.tensor_tensor(KD[:], KD[:], K[:], ALU.mult).then_inc(s["kd_ready"], 1)
                    pick(NL - 2)
                    pick(NL - 1)
                    take(dve, s["exp_ready"])
                    dve.tensor_tensor(QE[:], QE[:], Q[:, par, :], ALU.mult).then_inc(s["qe_ready"], 1)
                    take(dve, s["ds_done"])
                    take(dve, s["step_ready"])
                    for n in range(TT - 1):
                        link(dve.scalar_tensor_tensor(out=ST[:, n + 1, :], in0=ST[:, n, :], scalar=step_decay[:, n:n + 1],
                                                      in1=ps[:, 6 + n // 4, (n % 4) * P:(n % 4 + 1) * P], op0=ALU.mult, op1=ALU.add))
                    dve.sem_inc(s["s_ready"], 1)
                    if more:
                        front(h + 1, 1 - par)
                    take(dve, s["sq_summed"])
                    link(dve.tensor_scalar(F[:, par, :], pair(ps[:, 6:8, :]), 1.0 / P, EPS, ALU.mult, ALU.add))
                    dve.sem_inc(s["var_ready"], 1)
                    dve.sem_inc(s["tail_free"], 1)
                    if more:
                        scale(0, 1 - par)
                        scale(1, 1 - par)
                    take(dve, s["rstd_ready"])
                    link(dve.scalar_tensor_tensor(out=F[:, par, :], in0=pair(ps[:, 4:6, :]), scalar=col(nw, h), in1=F[:, par, :],
                                                  op0=ALU.mult, op1=ALU.mult))
                    for b in range(2):
                        dve.sem_inc(gram_free[b], 1)
                    take(dve, s["g_ready"])
                    link(dve.tensor_tensor(y_T[:, bass.ds(h, 1), :], F[:, par:par + 1, :], G[:, par:par + 1, :], ALU.mult))
                    dve.sem_inc(s["head_done"], 1)

                front(0, 0)
                scale(0, 0)
                scale(1, 0)
                with dve.Fori(0, HEADS // 2 - 1) as i:
                    step(2 * i, 0, True)
                    step(2 * i + 1, 1, True)
                step(HEADS - 2, 0, True)
                step(HEADS - 1, 1, False)


def finish(nc, c, gain, out):
    norm(nc, c, gain, rows=out)


class Chip:
    pass


def trunk(nc, a, out):
    c = Chip()
    with ExitStack() as ctx:
        def sb(name, shape, dt=F32):
            return ctx.enter_context(nc.sbuf_tensor(name, shape, dt))

        c.ctx = ctx
        c.res = sb("residual", [P, TT, D])
        c.ident = sb("ident", [P, P])
        c.ones = sb("ones", [P, P])
        c.ps = ctx.enter_context(nc.psum_tensor("ps", [P, 8, HALF], F32))
        c.rows = nc.dram_tensor("h_rows", [S, D], F32).ap()
        c.row_tok = nc.dram_tensor("row_token", [(NBLK + 1) * P, 1], I32).ap()
        c.ys = nc.dram_tensor("expert_rows", [(NBLK + 1) * P, D], F32).ap()
        with nc.sbuf_tensor("head_ones", [P, P], F32) as c.head_ones, nc.sbuf_tensor("proj", [P, AB_TILES, S], F32) as proj:
            load_x(nc, c, a["x"])
            with nc.sbuf_tensor("h_high", [P, KT, S], F32R) as h_T, nc.sbuf_tensor("h_low", [P, KT, S], F32R) as h_low:
                norm(nc, c, a["norm_mix"][0], h_T=h_T, h_low=h_low, scratch=proj[:, 0:TT, :])
                project_ab(nc, c, a["ab_w_in"][0], a["rw_mu"][0], h_T, h_low, proj)
            lru(nc, c, a, proj)
            with ExitStack() as mix:
                def mb(name, shape):
                    return mix.enter_context(nc.sbuf_tensor(name, shape, F32))

                b = Chip()
                b.ln_w, b.ln_b = mb("ln_w", [P, NPAIR]), mb("ln_b", [P, NPAIR])
                b.step = mb("step", [P, NPAIR, NCH])
                b.g2 = mb("g2", [P, W_RW])
                b.r_k = mb("r_k", [P, NPAIR])
                m1, m3 = mb("mix1", [P, NPAIR, S]), mb("mix3", [P, NPAIR, S])
                with (nc.sbuf_tensor("mix0", [P, NPAIR, S], F32) as m0, nc.sbuf_tensor("mix2", [P, NPAIR, S], F32) as m2,
                      nc.sbuf_tensor("mix4", [P, NPAIR, S], F32) as m4, nc.sbuf_tensor("w2a2", [P, W_RW], F32) as b.w2a2):
                    b.bufs = [m0, m1, m2, m3, m4]
                    rwkv_prepare(nc, c, a, proj, b)
                c.lower_1, c.upper, c.strict_incl = mb("lower_1", [P, HD]), mb("upper", [P, len(LEVELS), HD]), mb("strict_incl", [P, 2, HD])
                b.ident64 = mb("ident64", [P, HD])
                make_chunk_masks(nc, c, b)
                rwkv_chunks(nc, c, proj, b)
                rwkv_finish(nc, c, proj, b)
            project_out(nc, c, a["ab_w_out"][0], [proj[:, T_R:T_R + 4, :], proj[:, T_GATE:T_GATE + 4, :]])
        moe(nc, c, a, 0)
        with nc.sbuf_tensor("y_T", [P, KT, S], F32) as y_T:
            with nc.sbuf_tensor("h_T_1", [P, KT, S], F32) as h_T:
                norm(nc, c, a["norm_mix"][1], h_T=h_T)
                hgrn(nc, c, a["c_w_in"][0], a["c_lower_bound"], a["c_norm_w"][0], h_T, y_T)
            project_out(nc, c, a["c_w_out"][0], [y_T[:]])
        moe(nc, c, a, 1)
        finish(nc, c, a["norm_final"], out)


_INS = ["x", "norm_mix", "norm_ffn", "norm_final", "ab_w_in", "rw_mu", "rw_w0", "rw_w2", "rw_a0", "rw_a2", "rw_g2",
        "rw_k_k", "rw_k_a", "rw_r_k", "rw_ln_w", "rw_ln_b", "lru_conv_w", "lru_conv_b", "lru_w_a", "lru_b_a",
        "lru_w_x", "lru_b_x", "lru_lambda", "ab_w_out", "c_w_in", "c_lower_bound", "c_norm_w", "c_w_out",
        "moe_w_group", "moe_b_group", "moe_w_expert", "moe_b_expert", "moe_w_gate", "moe_w_up", "moe_w_down"]


def kernel(**inputs):
    import numpy as np
    import concourse.bacc as bacc
    from concourse.bass_utils import run_bass_kernel_spmd

    nc = bacc.Bacc("TRN2", target_bir_lowering=False, num_devices=1)
    arrays, aps = {}, {}
    for name in _INS:
        v = np.ascontiguousarray(inputs[name])
        if name == "x":
            v = v.reshape(S, D)
        arrays["in_" + name] = v
        aps[name] = nc.dram_tensor("in_" + name, v.shape, mybir.dt.from_np(v.dtype), kind="ExternalInput").ap()
    out = nc.dram_tensor("out_y", [S, D], F32, kind="ExternalOutput").ap()
    with nc.allow_non_contiguous_dma(reason="per-channel vectors of a few KB"):
        trunk(nc, aps, out)
    got = run_bass_kernel_spmd(nc, [arrays], core_ids=[0])
    return got.results[0]["out_y"].reshape(1, S, D)
```
